# Optimizing a Trainium2 kernel written in Bass

```python
import jax, jax.numpy as jnp
from jax import lax
import numpy as np

D_MODEL = 1024
BATCH = 1
SEQ = 4096
DEPTH = 1

HEAD_DIM = 64
ROT_DIM = HEAD_DIM // 4
ROPE_THETA = 500000.0
BLOCK = 128
N_MEM = 256
D_MIX = D_MODEL
C_HEADS = 4
C_W = C_HEADS * HEAD_DIM
A_Q_HEADS = (D_MIX - C_W) // (2 * HEAD_DIM)
A_KV_HEADS = 2
A_GROUP = A_Q_HEADS // A_KV_HEADS
A_W = A_Q_HEADS * HEAD_DIM
A_KV_W = A_KV_HEADS * HEAD_DIM
A_WINDOW = 128
B_HEADS = A_Q_HEADS
B_W = B_HEADS * HEAD_DIM
B_CONFIGS = ((128, 1), (512, 4), (2048, 16))
RMS_EPS = 1e-6
IN_WIDTHS = (A_W, A_KV_W, A_KV_W, A_W,
             B_W, B_W, B_W, B_W,
             C_W, C_W)
D_IN = sum(IN_WIDTHS)
IN_SPLITS = tuple(int(s) for s in np.cumsum(IN_WIDTHS)[:-1])

kernel_name = "hybrid_swa_sink_dilated_memxattn_layer"

def rms_norm(x, g):
    xf = x.astype(jnp.float32)
    y = xf * lax.rsqrt(jnp.mean(xf * xf, axis=-1, keepdims=True) + RMS_EPS)
    return (y * g.astype(jnp.float32)).astype(x.dtype)

def rope_tables(seq):
    inv_freq = ROPE_THETA ** (-jnp.arange(0, ROT_DIM, 2, dtype=jnp.float32) / ROT_DIM)
    ang = jnp.arange(seq, dtype=jnp.float32)[:, None] * inv_freq[None, :]
    return jnp.cos(ang)[:, None, :], jnp.sin(ang)[:, None, :]

def apply_partial_rope(t, cos, sin):
    tf = t.astype(jnp.float32)
    half = ROT_DIM // 2
    r1, r2, rest = tf[..., :half], tf[..., half:ROT_DIM], tf[..., ROT_DIM:]
    out = jnp.concatenate([r1 * cos - r2 * sin, r2 * cos + r1 * sin, rest], axis=-1)
    return out.astype(t.dtype)

def banded_attention(q, k, v, max_dist, sink):
    N, L, KVH, G, Dh = q.shape
    nb = -(-L // BLOCK)
    Lp = nb * BLOCK
    pad = Lp - L
    n_prev = -(-max_dist // BLOCK)
    W = (n_prev + 1) * BLOCK
    qp = jnp.pad(q, ((0, 0), (0, pad), (0, 0), (0, 0), (0, 0)))
    kp = jnp.pad(k, ((0, 0), (n_prev * BLOCK, pad), (0, 0), (0, 0)))
    vp = jnp.pad(v, ((0, 0), (n_prev * BLOCK, pad), (0, 0), (0, 0)))

    def windows(t):
        return jnp.concatenate(
            [t[:, j * BLOCK:(j + nb) * BLOCK].reshape(N, nb, BLOCK, KVH, Dh)
             for j in range(n_prev + 1)], axis=2)

    kw, vw = windows(kp), windows(vp)
    qb = qp.reshape(N, nb, BLOCK, KVH, G, Dh)
    s = jnp.einsum('nbqhgd,nbkhd->nbhgqk', qb, kw,
                   preferred_element_type=jnp.float32)
    qi = jnp.arange(BLOCK)[:, None]
    kj = jnp.arange(W)[None, :]
    dist = qi + n_prev * BLOCK - kj
    kpos = jnp.arange(nb)[:, None, None] * BLOCK + kj[None] - n_prev * BLOCK
    mask = (dist >= 0)[None] & (dist <= max_dist)[None] & (kpos >= 0)
    s = jnp.where(mask[:, None, None], s, -jnp.inf)
    m = jnp.max(s, axis=-1)
    if sink is not None:
        sink_b = sink.astype(jnp.float32)[None, None, :, :, None]
        m = jnp.maximum(m, sink_b)
    p = jnp.exp(s - m[..., None])
    denom = jnp.sum(p, axis=-1)
    if sink is not None:
        denom = denom + jnp.exp(sink_b - m)
    o = jnp.einsum('nbhgqk,nbkhd->nbqhgd', p, vw.astype(jnp.float32))
    o = o / jnp.moveaxis(denom, -1, 2)[..., None]
    lse = jnp.moveaxis(m + jnp.log(denom), -1, 2)
    o = o.reshape(N, Lp, KVH, G, Dh)[:, :L]
    lse = lse.reshape(N, Lp, KVH, G)[:, :L]
    return o.astype(q.dtype), lse

def to_strided(t, d):
    B, S = t.shape[:2]
    rest = t.shape[2:]
    t = t.reshape((B, S // d, d) + rest)
    t = jnp.moveaxis(t, 2, 1)
    return t.reshape((B * d, S // d) + rest)

def from_strided(t, B, d):
    L = t.shape[1]
    rest = t.shape[2:]
    t = t.reshape((B, d, L) + rest)
    t = jnp.moveaxis(t, 1, 2)
    return t.reshape((B, d * L) + rest)

def setup_inputs(seed: int = 0) -> dict:
    key = jax.random.key(seed)
    ks = jax.random.split(key, 10)
    f32 = jnp.float32
    x = jax.random.normal(ks[0], (BATCH, SEQ, D_MODEL), f32)
    mem = jax.random.normal(ks[1], (BATCH, N_MEM, D_MODEL), f32)
    pre_norm = 1.0 + 0.02 * jax.random.normal(ks[2], (DEPTH, D_MODEL), f32)
    w_in = jax.random.normal(ks[3], (DEPTH, D_MODEL, D_IN), f32) * D_MODEL ** -0.5
    sink_a = 0.5 * jax.random.normal(ks[4], (DEPTH, A_Q_HEADS), f32)
    mem_norm = 1.0 + 0.02 * jax.random.normal(ks[5], (DEPTH, D_MODEL), f32)
    w_mem_kv = jax.random.normal(ks[6], (DEPTH, D_MODEL, 2 * C_W), f32) * D_MODEL ** -0.5
    w_out = jax.random.normal(ks[7], (DEPTH, D_MIX, D_MODEL), f32) * D_MIX ** -0.5
    post_norm = 1.0 + 0.02 * jax.random.normal(ks[8], (DEPTH, D_MODEL), f32)
    return {"x": x, "mem": mem, "pre_norm": pre_norm, "w_in": w_in,
            "sink_a": sink_a, "mem_norm": mem_norm, "w_mem_kv": w_mem_kv,
            "w_out": w_out, "post_norm": post_norm}

def reference(x, mem, pre_norm, w_in, sink_a, mem_norm, w_mem_kv, w_out, post_norm):
    B, S, _ = x.shape
    scale = HEAD_DIM ** -0.5
    cos, sin = rope_tables(S)
    h = x
    for l in range(DEPTH):
        u = rms_norm(h, pre_norm[l])
        proj = jnp.einsum('bsd,de->bse', u, w_in[l])
        qa, ka, va, ga, qb, kb, vb, gb, qc, gc = jnp.split(proj, IN_SPLITS, axis=-1)

        qa = apply_partial_rope(qa.reshape(B, S, A_Q_HEADS, HEAD_DIM), cos, sin)
        qa = qa.reshape(B, S, A_KV_HEADS, A_GROUP, HEAD_DIM)
        ka = apply_partial_rope(ka.reshape(B, S, A_KV_HEADS, HEAD_DIM), cos, sin)
        va = va.reshape(B, S, A_KV_HEADS, HEAD_DIM)
        sink = sink_a[l].reshape(A_KV_HEADS, A_GROUP)
        oa, _ = banded_attention(qa * scale, ka, va, A_WINDOW - 1, sink)
        oa = oa.reshape(B, S, A_W)

        qb = apply_partial_rope(qb.reshape(B, S, B_HEADS, HEAD_DIM), cos, sin)
        kb = apply_partial_rope(kb.reshape(B, S, B_HEADS, HEAD_DIM), cos, sin)
        vb = vb.reshape(B, S, B_HEADS, HEAD_DIM)
        outs, lses = [], []
        for (win, dil) in B_CONFIGS:
            qs = to_strided(qb * scale, dil)[:, :, :, None, :]
            o, lse = banded_attention(qs, to_strided(kb, dil), to_strided(vb, dil),
                                      win // dil, None)
            outs.append(from_strided(o[:, :, :, 0], B, dil).astype(jnp.float32))
            lses.append(from_strided(lse[..., 0], B, dil))
        wts = jax.nn.softmax(jnp.stack(lses, axis=0), axis=0)
        ob = jnp.sum(wts[..., None] * jnp.stack(outs, axis=0), axis=0)
        ob = ob.astype(x.dtype).reshape(B, S, B_W)

        mkv = jnp.einsum('bmd,de->bme', rms_norm(mem, mem_norm[l]), w_mem_kv[l])
        mk, mv = jnp.split(mkv, 2, axis=-1)
        mk = mk.reshape(B, N_MEM, C_HEADS, HEAD_DIM)
        mv = mv.reshape(B, N_MEM, C_HEADS, HEAD_DIM)
        qc = qc.reshape(B, S, C_HEADS, HEAD_DIM)
        sc = jnp.einsum('bshd,bmhd->bhsm', qc * scale, mk,
                        preferred_element_type=jnp.float32)
        pc = jax.nn.softmax(sc, axis=-1)
        oc = jnp.einsum('bhsm,bmhd->bshd', pc, mv.astype(jnp.float32))
        oc = oc.astype(x.dtype).reshape(B, S, C_W)

        y = jnp.concatenate([oa * jax.nn.silu(ga), ob * jax.nn.silu(gb),
                             oc * jax.nn.silu(gc)], axis=-1)
        y = jnp.einsum('bse,ed->bsd', y, w_out[l])
        h = h + rms_norm(y, post_norm[l])
    return h


_drawn_inputs = setup_inputs


def setup_inputs(seed=0):
    import zlib

    import numpy as np

    out = dict(_drawn_inputs(seed))
    spreads = {}
    factors = {'sink_a': 8.0, 'mem_norm': 5.989, 'post_norm': 4.222}
    for name, (base, spread) in spreads.items():
        noise = np.random.default_rng([zlib.crc32(name.encode()), seed]).standard_normal(out[name].shape)
        drawn = base * np.exp(spread * noise) if base else spread * noise
        out[name] = __import__('jax').numpy.asarray(drawn.astype(out[name].dtype))
    for name, factor in factors.items():
        out[name] = (out[name] * factor).astype(out[name].dtype)
    return out
```

```python
from contextlib import ExitStack

import concourse.bass as bass
from concourse import mybir

F32 = mybir.dt.float32
F32R = mybir.dt.float32r
ALU = mybir.AluOpType
ACT = mybir.ActivationFunctionType

P = 128
D = 1024
KD = D // P
SEQ = 4096
NMEM = 256
HD = 64
CHUNK = 512
HALF = SEQ // 2
NCH = HALF // CHUNK
SCALE = HD ** -0.5
NEG = -1e30
EPS = 1e-6
ROPE_TILES = [0, 1, 2, 3, 8, 9, 10, 11, 12, 13]
PLAIN_TILES = [20, 21]
V_TILES = [4, 14, 15, 16]
GATE_TILES = [5, 6, 7, 17, 18, 19, 22, 23]
ORDER = ROPE_TILES + PLAIN_TILES + V_TILES + GATE_TILES
NT = len(ORDER)
NQK = len(ROPE_TILES) + len(PLAIN_TILES)
QA, KA, QB, KB, QC = 0, 384, 512, 896, 1280
SWAP = [8, 9, 10, 11, 12, 13, 14, 15, 0, 1, 2, 3, 4, 5, 6, 7] + list(range(16, 32))


def split_product(nc, out, w_hi, w_lo, m_hi, m_lo, first, last):
    nc.tensor.matmul(out, w_hi, m_hi, start=first, stop=False)
    nc.tensor.matmul(out, w_hi, m_lo, start=False, stop=False)
    return nc.tensor.matmul(out, w_lo, m_hi, start=False, stop=last)


def memory_stage(nc, io, sc):
    with ExitStack() as ctx:
        sb = lambda n, s, d=F32: ctx.enter_context(nc.sbuf_tensor("m_" + n, s, d))
        sem = lambda n: ctx.enter_context(nc.semaphore("m_" + n))
        MT = NMEM // P
        mem = sb("mem", [P, MT, D])
        um = sb("um", [P, MT, D])
        umT = sb("umT", [P, KD, NMEM])
        w = sb("w", [P, KD, 512])
        gain = sb("gain", [P, D])
        ident = sb("ident", [P, P])
        ss = sb("ss", [P, 3 * MT])
        k_hi = sb("k_hi", [P, 2, NMEM], F32R)
        k_lo = sb("k_lo", [P, 2, NMEM], F32R)
        v = sb("v", [P, MT, 256])
        ps_t = ctx.enter_context(nc.psum_tensor("m_ps_t", [P, 4, CHUNK], F32))
        ps = ctx.enter_context(nc.psum_tensor("m_ps", [P, 4, CHUNK], F32))
        loaded, squared, meaned, rooted = sem("loaded"), sem("squared"), sem("meaned"), sem("rooted")
        inverted, scaled, transposed, copied = sem("inverted"), sem("scaled"), sem("transposed"), sem("copied")
        multiplied, hi_ready, lo_ready, v_ready, stored = (sem("multiplied"), sem("hi_ready"), sem("lo_ready"),
                                                           sem("v_ready"), sem("stored"))
        with nc.Block() as block:
            @block.sync
            def _(sp):
                sp.dma_start(mem[:], io["mem"].rearrange("(t p) d -> p t d", p=P)).then_inc(loaded, 16)
                sp.dma_start(gain[:], io["mem_gain"].broadcast_to([P, D])).then_inc(loaded, 16)
                sp.dma_start(ident[:], io["ident"]).then_inc(loaded, 16)
                sp.dma_start(w[:], io["w_mem"].rearrange("(k p) n -> p k n", p=P)).then_inc(loaded, 16)
                sp.wait_ge(lo_ready, 1)
                sp.wait_ge(hi_ready, 1)
                sp.dma_start(sc["mk_hi"].rearrange("(t p) n -> p t n", p=P), k_hi[:].bitcast(F32)).then_inc(stored, 16)
                sp.dma_start(sc["mk_lo"].rearrange("(t p) n -> p t n", p=P), k_lo[:].bitcast(F32)).then_inc(stored, 16)
                sp.wait_ge(v_ready, 1)
                sp.dma_start(sc["mv"].rearrange("(t p) n -> p t n", p=P), v[:]).then_inc(stored, 16)
                sp.wait_ge(stored, 48)

            @block.scalar
            def _(act):
                act.wait_ge(loaded, 64)
                for t in range(MT):
                    nc.scalar.activation(um[:, t, :], mem[:, t, :], ACT.Square,
                                         accum_out=ss[:, t:t + 1]).then_inc(squared, 1)
                act.wait_ge(meaned, 1)
                nc.scalar.activation(ss[:, 4:6], ss[:, 2:4], ACT.Sqrt).then_inc(rooted, 1)
                act.wait_ge(multiplied, 1)
                nc.scalar.activation(k_hi[:], ps[:, 0:2, 0:NMEM], ACT.Copy).then_inc(hi_ready, 1)
                act.wait_ge(multiplied, 2)
                nc.scalar.activation(v[:], ps[:, 2:4, 0:256], ACT.Copy).then_inc(v_ready, 1)

            @block.vector
            def _(dve):
                dve.wait_ge(squared, MT)
                nc.vector.tensor_scalar(ss[:, 2:4], ss[:, 0:2], 1.0 / D, EPS, ALU.mult, ALU.add).then_inc(meaned, 1)
                dve.wait_ge(rooted, 1)
                nc.vector.reciprocal(ss[:, 0:2], ss[:, 4:6]).then_inc(inverted, 1)
                dve.wait_ge(inverted, 1)
                for t in range(MT):
                    nc.vector.scalar_tensor_tensor(out=um[:, t, :], in0=mem[:, t, :], scalar=ss[:, t:t + 1],
                                                   in1=gain[:], op0=ALU.mult, op1=ALU.mult).then_inc(scaled, 1)
                dve.wait_ge(transposed, 1)
                nc.vector.tensor_copy(umT[:].rearrange("p (b k) n -> p b (k n)", b=4), ps_t[:]).then_inc(copied, 1)
                dve.wait_ge(hi_ready, 1)
                nc.vector.tensor_tensor(k_lo[:], ps[:, 0:2, 0:NMEM], k_hi[:].bitcast(F32),
                                        ALU.subtract).then_inc(lo_ready, 1)

            @block.tensor
            def _(pe):
                pe.wait_ge(scaled, MT)
                for k in range(KD):
                    for t in range(MT):
                        at = (k % 2) * NMEM + t * P
                        last = nc.tensor.transpose(ps_t[:, k // 2, at:at + P], um[:, t, k * P:(k + 1) * P], ident[:])
                last.then_inc(transposed, 1)
                pe.wait_ge(copied, 1)
                for c in range(2):
                    for k in range(KD):
                        last = nc.tensor.matmul(ps[:, c, 0:NMEM], w[:, k, c * P:(c + 1) * P], umT[:, k, :],
                                                start=k == 0, stop=k == KD - 1)
                last.then_inc(multiplied, 1)
                for t in range(MT):
                    for k in range(KD):
                        last = nc.tensor.matmul(ps[:, 2 + t, 0:256], umT[:, k, t * P:(t + 1) * P], w[:, k, 256:512],
                                                start=k == 0, stop=k == KD - 1)
                last.then_inc(multiplied, 1)


def project_stage(nc, io, sc):
    with ExitStack() as ctx:
        sb = lambda n, s, d=F32: ctx.enter_context(nc.sbuf_tensor("p_" + n, s, d))
        sem = lambda n: ctx.enter_context(nc.semaphore("p_" + n))
        uT_hi = sb("uT_hi", [P, KD, HALF], F32R)
        uT_lo = sb("uT_lo", [P, KD, HALF], F32R)
        w_hi = sb("w_hi", [P, 2, KD, P], F32R)
        w_lo = sb("w_lo", [P, 2, KD, P], F32R)
        gain = sb("gain", [P, D])
        ident = sb("ident", [P, P])
        ss = sb("ss", [P, 2, 4])
        cos = sb("cos", [P, HALF])
        sin = sb("sin", [P, HALF])
        xb = sb("x", [P, 2, D])
        ub = sb("u", [P, 2, D])
        w_raw = xb
        turned = sb("turned", [P, CHUNK])
        rot = sb("rot", [P, 2, CHUNK])
        o_hi = sb("o_hi", [P, 2, CHUNK], F32R)
        o_lo = sb("o_lo", [P, 2, CHUNK], F32R)
        vT = ub[:, 0, :].rearrange("p (b n) -> p b n", b=2)
        o_v = ub[:, 1, :].rearrange("p (b n) -> p b n", b=2)
        o_g = rot
        ps = ctx.enter_context(nc.psum_tensor("p_ps", [P, 4, CHUNK], F32))
        ps_t = ctx.enter_context(nc.psum_tensor("p_ps_t", [P, 2, 2, CHUNK], F32))
        consts = sem("consts")
        x_loaded = [sem(f"x_loaded{b}") for b in range(2)]
        squared, meaned, rooted, inverted = sem("squared"), sem("meaned"), sem("rooted"), sem("inverted")
        u_ready, u_turned, uT_hi_ready, uT_lo_ready = sem("u_ready"), sem("u_turned"), sem("uT_hi_ready"), sem("uT_lo_ready")
        table = sem("table")
        w_loaded = [sem(f"w_loaded{b}") for b in range(2)]
        w_hi_ready, w_lo_ready = sem("w_hi_ready"), sem("w_lo_ready")
        multiplied = sem("multiplied")
        straight = sem("straight")
        chain = sem("chain")
        rotated, hi_ready = sem("rotated"), sem("hi_ready")
        out_ready = sem("out_ready")
        vT_ready, v_turned = sem("vT_ready"), sem("v_turned")
        qk_stored, v_stored, g_stored = ([sem(f"{n}_stored{b}") for b in range(2)] for n in ("qk", "v", "g"))

        XT = HALF // P
        tiles = lambda half, i: half * NT + i
        NR, NQ, NV, NG = len(ROPE_TILES), NQK, len(V_TILES), len(GATE_TILES)

        for half in range(2):
            with nc.Block() as block:
                C0, R0, H0, V0 = (half * n * NCH for n in (NT, NR, NQ, NV))

                def pairs(eng, lo, hi, body, peel=False):
                    end = hi - 2 if peel else hi
                    if half == 0 and lo in (0, NQ) and end - lo > 2:
                        for b in range(2):
                            body(lo + b, b, False)
                        lo += 2
                    if end - lo > 2:
                        with eng.Fori(lo // 2, end // 2) as two:
                            i = 2 * two
                            for b in range(2):
                                body(i + b, b, False)
                    elif end > lo:
                        for b in range(2):
                            body(lo + b, b, False)
                    if peel:
                        for b in range(2):
                            body(end + b, b, end + b == hi - 1)

                @block.sync
                def _(sp):
                    if half == 0:
                        sp.dma_start(gain[:], io["pre_gain"].broadcast_to([P, D])).then_inc(consts, 16)
                        sp.dma_start(ident[:], io["ident"]).then_inc(consts, 16)
                    for t, d in ((cos, "cos"), (sin, "sin")):
                        sp.dma_start(t[:], io[d][:, half * HALF:(half + 1) * HALF]).then_inc(table, 16)

                    def load_x(i, b):
                        sp.dma_start(xb[:, b, :], io["x"][bass.ts(half * XT + i, P), :]).then_inc(x_loaded[b], 16)
                    for b in range(2):
                        load_x(b, b)
                    with sp.Fori(1, XT // 2) as two:
                        i = 2 * two
                        for b in range(2):
                            sp.wait_ge(u_ready, half * XT + i + b - 1)
                            load_x(i + b, b)

                    def load_w(i, b, n):
                        sp.dma_start(w_raw[:, b, :], io["w_in"][n, :, :]).then_inc(w_loaded[b], 16)
                    sp.wait_ge(u_ready, (half + 1) * XT)
                    load_w(0, 0, 0)
                    load_w(1, 1, 1)

                    def next_w(i, b, last):
                        if not isinstance(i, int) or i + 2 < NT:
                            sp.wait_ge(w_lo_ready, tiles(half, i) + 1)
                            load_w(i + 2, b, i + 2)

                    def store_qk(i, b, last):
                        next_w(i, b, last)
                        for c in range(NCH):
                            sp.wait_ge(out_ready, C0 + i * NCH + c + 1)
                            at = (half * NCH + c) * CHUNK
                            for src, dst in ((o_hi, sc["qk_hi"]), (o_lo, sc["qk_lo"])):
                                sp.dma_start(dst[bass.ts(i, P), at:at + CHUNK], src[:, c % 2, :].bitcast(F32)).then_inc(qk_stored[c % 2], 16)

                    def store_v(i, b, last):
                        next_w(i, b, last)
                        for c in range(NCH):
                            sp.wait_ge(out_ready, C0 + i * NCH + c + 1)
                            at = (half * NCH + c) * CHUNK
                            dst = sc["v"][at:at + CHUNK, bass.ts(i - NQ, P)].rearrange("(t p) n -> p t n", p=P)
                            sp.dma_start(dst, o_v[:, c % 2, :].rearrange("p (t n) -> p t n", n=P)).then_inc(v_stored[c % 2], 16)

                    def store_g(i, b, last):
                        next_w(i, b, last)
                        for c in range(NCH):
                            sp.wait_ge(out_ready, C0 + i * NCH + c + 1)
                            at = (half * NCH + c) * CHUNK
                            sp.dma_start(sc["gate"][bass.ts(i - NQ - NV, P), at:at + CHUNK],
                                         o_g[:, c % 2, :]).then_inc(g_stored[c % 2], 16)

                    pairs(sp, 0, NQ, store_qk)
                    pairs(sp, NQ, NQ + NV, store_v)
                    pairs(sp, NQ + NV, NT, store_g, peel=True)
                    for b in range(2):
                        sp.wait_ge(qk_stored[b], 32 * (NCH // 2) * NQ * (half + 1))
                        sp.wait_ge(v_stored[b], 16 * (NCH // 2) * NV * (half + 1))
                        sp.wait_ge(g_stored[b], 16 * (NCH // 2) * NG * (half + 1))

                def wait_stored(eng, sems, i, c, kind_tiles, per):
                    n = half * kind_tiles * NCH // 2 + i * (NCH // 2) + c // 2
                    if not isinstance(n, int) or n >= 1:
                        eng.wait_ge(sems[c % 2], per * n)

                @block.scalar
                def _(act):
                    XB = half * XT

                    def square(i, b):
                        act.wait_ge(x_loaded[b], 16 * ((half * XT + i - b) // 2 + 1) if isinstance(i, int)
                                    else half * 8 * XT + (i - b) * 8 + 16)
                        if half or not isinstance(i, int) or i >= 2:
                            act.wait_ge(u_turned, XB + i - 1)
                        nc.scalar.activation(ub[:, b, :], xb[:, b, :], ACT.Square,
                                             accum_out=ss[:, b, 0:1]).then_inc(squared, 1)
                        act.wait_ge(meaned, XB + i + 1)
                        nc.scalar.activation(ss[:, b, 2:3], ss[:, b, 1:2], ACT.Sqrt).then_inc(rooted, 1)

                    def part(i, b):
                        act.wait_ge(u_turned, XB + i + 1)
                        nc.scalar.activation(uT_hi[:, :, bass.ts(i, P)],
                                             ps_t[:, b, :, :].rearrange("p a (k n) -> p (a k) n", n=P),
                                             ACT.Copy).then_inc(uT_hi_ready, 1)
                    act.wait_ge(consts, 32)
                    square(0, 0)
                    square(1, 1)
                    part(0, 0)
                    with act.Fori(1, XT // 2) as two:
                        i = 2 * two
                        for b in range(2):
                            square(i + b, b)
                            part(i + b - 1, 1 - b)
                    part(XT - 1, 1)

                    def w_part(i, b):
                        act.wait_ge(w_loaded[b], 16 * half * (NT // 2) + (i - b) * 8 + 16)
                        if half or not isinstance(i, int) or i >= 2:
                            act.wait_ge(multiplied, C0 + (i - 1) * NCH)
                        nc.scalar.activation(w_hi[:, b, :, :].rearrange("p k n -> p (k n)"), w_raw[:, b, :],
                                             ACT.Copy).then_inc(w_hi_ready, 1)
                    w_part(0, 0)

                    def rope(i, b, last):
                        w_part(i + 1, 1 - b)
                        for c in range(NCH):
                            act.wait_ge(rotated, R0 + i * NCH + c + 1)
                            wait_stored(act, qk_stored, i, c, NQ, 32)
                            nc.scalar.activation(o_hi[:, c % 2, :], rot[:, c % 2, :], ACT.Copy).then_inc(hi_ready, 1)

                    def plain(i, b, last):
                        w_part(i + 1, 1 - b)
                        for c in range(NCH):
                            act.wait_ge(multiplied, C0 + i * NCH + c + 1)
                            wait_stored(act, qk_stored, i, c, NQ, 32)
                            nc.scalar.activation(o_hi[:, c % 2, :], ps[:, c, :], ACT.Copy).then_inc(hi_ready, 1)

                    def values(i, b, last):
                        w_part(i + 1, 1 - b)
                        for c in range(NCH + 1):
                            if c < NCH:
                                act.wait_ge(multiplied, C0 + i * NCH + c + 1)
                                n = V0 + (i - NQ) * NCH + c
                                if not isinstance(n, int) or n >= 2:
                                    act.wait_ge(v_turned, n - 1)
                                nc.scalar.activation(vT[:, c % 2, :], ps[:, c, :], ACT.Copy).then_inc(vT_ready, 1)
                            if c > 0:
                                act.wait_ge(v_turned, V0 + (i - NQ) * NCH + c)
                                wait_stored(act, v_stored, i - NQ, c - 1, NV, 16)
                                nc.scalar.activation(o_v[:, (c - 1) % 2, :], ps_t[:, (c - 1) % 2, 0, :],
                                                     ACT.Copy).then_inc(out_ready, 1)

                    def gates(i, b, last):
                        if not last:
                            w_part(i + 1, 1 - b)
                        for c in range(NCH):
                            act.wait_ge(multiplied, C0 + i * NCH + c + 1)
                            wait_stored(act, g_stored, i - NQ - NV, c, NG, 16)
                            nc.scalar.activation(o_g[:, c % 2, :], ps[:, c, :], ACT.Silu).then_inc(out_ready, 1)

                    pairs(act, 0, NR, rope)
                    pairs(act, NR, NQ, plain)
                    act.wait_ge(out_ready, C0 + NQ * NCH)
                    pairs(act, NQ, NQ + NV, values)
                    pairs(act, NQ + NV, NT, gates, peel=True)

                @block.vector
                def _(dve):
                    XB = half * XT

                    def normalise(i, b):
                        dve.wait_ge(squared, XB + i + 1)
                        nc.vector.tensor_scalar(ss[:, b, 1:2], ss[:, b, 0:1], 1.0 / D, EPS,
                                                ALU.mult, ALU.add).then_inc(meaned, 1)
                        dve.wait_ge(rooted, XB + i + 1)
                        nc.vector.reciprocal(ss[:, b, 3:4], ss[:, b, 2:3]).then_inc(inverted, 1)
                        dve.wait_ge(inverted, XB + i + 1)
                        nc.vector.scalar_tensor_tensor(out=ub[:, b, :], in0=xb[:, b, :], scalar=ss[:, b, 3:4],
                                                       in1=gain[:], op0=ALU.mult, op1=ALU.mult).then_inc(u_ready, 1)

                    def part(i, b):
                        dve.wait_ge(uT_hi_ready, XB + i + 1)
                        nc.vector.tensor_tensor(uT_lo[:, :, bass.ts(i, P)],
                                                ps_t[:, b, :, :].rearrange("p a (k n) -> p (a k) n", n=P),
                                                uT_hi[:, :, bass.ts(i, P)].bitcast(F32),
                                                ALU.subtract).then_inc(uT_lo_ready, 1)
                    normalise(0, 0)
                    normalise(1, 1)
                    part(0, 0)
                    with dve.Fori(1, XT // 2) as two:
                        i = 2 * two
                        for b in range(2):
                            normalise(i + b, b)
                            part(i + b - 1, 1 - b)
                    part(XT - 1, 1)

                    def w_part(i, b):
                        dve.wait_ge(w_hi_ready, tiles(half, i) + 1)
                        nc.vector.tensor_tensor(w_lo[:, b, :, :].rearrange("p k n -> p (k n)"), w_raw[:, b, :],
                                                w_hi[:, b, :, :].rearrange("p k n -> p (k n)").bitcast(F32),
                                                ALU.subtract).then_inc(w_lo_ready, 1)
                    w_part(0, 0)
                    dve.wait_ge(table, 32 * (half + 1))

                    def low(i, c, src, kind_n):
                        dve.wait_ge(hi_ready, kind_n)
                        last = nc.vector.tensor_tensor(o_lo[:, c % 2, :], src, o_hi[:, c % 2, :].bitcast(F32), ALU.subtract)
                        last.then_inc(out_ready, 1)

                    def rope(i, b, last):
                        w_part(i + 1, 1 - b)
                        for c in range(NCH):
                            at = c * CHUNK
                            n = R0 + i * NCH + c
                            dve.wait_ge(multiplied, C0 + i * NCH + c + 1)
                            if not isinstance(n, int) or n >= 1:
                                dve.wait_ge(rotated, n)
                            if not isinstance(n, int) or n >= 2:
                                dve.wait_ge(out_ready, C0 + i * NCH + c - 1)
                            dve.nop(nofuse=True)
                            nc.vector.stream_shuffle(turned[:], ps[:, c, :], SWAP).then_inc(chain, 1)
                            nc.vector.tensor_tensor(rot[:, c % 2, :], ps[:, c, :], cos[:, at:at + CHUNK],
                                                    ALU.mult).then_inc(straight, 1)
                            dve.wait_ge(chain, 2 * n + 1)
                            nc.vector.tensor_tensor(turned[:], turned[:], sin[:, at:at + CHUNK],
                                                    ALU.mult).then_inc(chain, 1)
                            dve.wait_ge(chain, 2 * n + 2)
                            dve.wait_ge(straight, n + 1)
                            nc.vector.tensor_tensor(rot[:, c % 2, :], rot[:, c % 2, :], turned[:],
                                                    ALU.add).then_inc(rotated, 1)
                            dve.wait_ge(rotated, n + 1)
                            low(i, c, rot[:, c % 2, :], H0 + i * NCH + c + 1)

                    def plain(i, b, last):
                        w_part(i + 1, 1 - b)
                        for c in range(NCH):
                            dve.wait_ge(multiplied, C0 + i * NCH + c + 1)
                            low(i, c, ps[:, c, :], H0 + i * NCH + c + 1)

                    def others(i, b, last):
                        if not last:
                            w_part(i + 1, 1 - b)

                    pairs(dve, 0, NR, rope)
                    pairs(dve, NR, NQ, plain)
                    pairs(dve, NQ, NT, others, peel=True)

                @block.tensor
                def _(pe):
                    XB = half * XT
                    pe.wait_ge(consts, 32)

                    def turn(i, b):
                        pe.wait_ge(u_ready, XB + i + 1)
                        if half or not isinstance(i, int) or i >= 2:
                            pe.wait_ge(uT_lo_ready, XB + i - 1)
                        for k in range(KD):
                            last = nc.tensor.transpose(ps_t[:, b, k // 4, (k % 4) * P:(k % 4 + 1) * P],
                                                       ub[:, b, k * P:(k + 1) * P], ident[:])
                        last.then_inc(u_turned, 1)
                    turn(0, 0)
                    turn(1, 1)
                    with pe.Fori(1, XT // 2) as two:
                        i = 2 * two
                        for b in range(2):
                            turn(i + b, b)
                    pe.wait_ge(uT_lo_ready, (half + 1) * XT)

                    def product(i, b, c):
                        n = C0 + i * NCH + c
                        if not isinstance(n, int) or n >= NCH:
                            pe.wait_ge(out_ready, n - NCH + 1)
                        for k in range(KD):
                            last = split_product(nc, ps[:, c, :], w_hi[:, b, k, :], w_lo[:, b, k, :],
                                                 uT_hi[:, k, c * CHUNK:(c + 1) * CHUNK],
                                                 uT_lo[:, k, c * CHUNK:(c + 1) * CHUNK], k == 0, k == KD - 1)
                        last.then_inc(multiplied, 1)

                    def tile(i, b, last):
                        pe.wait_ge(w_lo_ready, tiles(half, i) + 1)
                        for c in range(NCH):
                            product(i, b, c)

                    def turn_v(i, c):
                        n = V0 + (i - NQ) * NCH + c
                        pe.wait_ge(vT_ready, n + 1)
                        if not isinstance(n, int) or n >= 2:
                            pe.wait_ge(out_ready, C0 + i * NCH + c - 1)
                        for t in range(CHUNK // P):
                            last = nc.tensor.transpose(ps_t[:, c % 2, 0, t * P:(t + 1) * P],
                                                       vT[:, c % 2, t * P:(t + 1) * P], ident[:])
                        last.then_inc(v_turned, 1)

                    def tile_v(i, b, last):
                        pe.wait_ge(w_lo_ready, tiles(half, i) + 1)
                        for c in range(NCH):
                            product(i, b, c)
                            if c:
                                turn_v(i, c - 1)
                        turn_v(i, NCH - 1)

                    pairs(pe, 0, NQ, tile)
                    pairs(pe, NQ, NQ + NV, tile_v)
                    pairs(pe, NQ + NV, NT, tile, peel=True)


class Unit:

    def __init__(self, q, k, keys, tiles, out, column):
        self.q, self.k, self.keys = q, k, keys
        self.tiles, self.out, self.column = tiles, out, column


def units_of(kind, s):
    groups = []
    if kind == "B":
        for g in range(4):
            groups.append([Unit((r, 16), (r, 16), 256 if s else 128, [("v16", 0, r), ("v16", 1, r)][0 if s else 0:2 if s else 1],
                                ((r % 4) * P, 1), r) for r in range(4 * g, 4 * g + 4)])
    for c in range(NCH):
        group = []
        if kind == "B":
            for r in range(4):
                n = NCH * s + c
                tiles = [("v4", m // NCH, (m % NCH) * 4 + r) for m in (n - 1, n) if m >= 0]
                group.append(Unit((CHUNK * c + r, 4), (CHUNK * max(n - 1, 0) + r, 4), P * len(tiles), tiles,
                                  (r, 4), 16 + 4 * c + r))
        for b in range(4 * c, 4 * c + 4):
            n = 16 * s + b
            if kind == "C":
                tiles, k = [("v1", 0, 0), ("v1", 0, 1)], 0
            else:
                tiles, k = [("v1", m // 16, m % 16) for m in (n - 1, n) if m >= 0], P * max(n - 1, 0)
            group.append(Unit((P * b, 1), (k, 1), P * len(tiles), tiles, ((b % 4) * P, 1),
                              (32 if kind == "B" else 0) + b))
        groups.append(group)
    return groups


def strided(start, n, step):
    return slice(start, start + (n - 1) * step + 1, step)


def attend_stage(nc, io, sc, kind):
    heads = {"A": 6, "B": 6, "C": 4}[kind]
    q_row = {"A": QA, "B": QB, "C": QC}[kind]
    y_row = {"A": 0, "B": 384, "C": 768}[kind]
    PLANS = [units_of(kind, s) for s in range(2)]
    FLAT = [[u for g in plan for u in g] for plan in PLANS]
    NU = len(FLAT[0])
    NP = NU // 2
    NG = len(PLANS[0])
    EARLY = 12 if kind == "B" else 1
    LAG = 4 if kind == "B" else 2
    NKEY = NMEM if kind == "C" else SEQ
    kinds_v = {"A": ["v1"], "B": ["v16", "v4", "v1"], "C": ["v1"]}[kind]
    last_of = {}
    first_of = {}
    bank_of = []
    at = 0
    for g, group in enumerate(PLANS[0]):
        first_of[at] = g
        bank_of += [g] * len(group)
        at += len(group)
        last_of[at // 2 - 1] = g
    MERGED = NG - NCH

    def ge(eng, sem, value):
        if not isinstance(value, int) or value > 0:
            eng.wait_ge(sem, value)

    with ExitStack() as ctx:
        sb = lambda n, shape, d=F32: ctx.enter_context(nc.sbuf_tensor(kind + "_" + n, shape, d))
        sem = lambda n: ctx.enter_context(nc.semaphore(kind + "_" + n))
        q = sb("q", [P, 2, HALF], F32R)
        k_hi = sb("k_hi", [P, NKEY], F32R)
        k_lo = sb("k_lo", [P, NKEY], F32R)
        v = {n: sb(n, [P, 2, 16, HD]) for n in kinds_v}
        gate = sb("gate", [HD, 2, CHUNK])
        probs = sb("probs", [P, 2, NU, 2 * P])
        pT = sb("pT", [P, 2, 2, 2 * P])
        stat = sb("stat", [P, 2, 2, NU])
        coef = sb("coef", [P, 2, NU])
        mask = sb("mask", [P, 2 * P])
        ident = sb("ident", [P, P])
        y = sb("y", [HD, 2, CHUNK])
        work = sb("work", [P, 8, NU])
        if kind == "A":
            sink = sb("sink", [P, 2, heads])
            sink_now = sb("sink_now", [P, 2, 2])
            sink_ready = sem("sink_ready")
        if kind == "B":
            o16 = sb("o16", [HD, 16, P])
            sel = sb("sel", [P, 2 * P + 8 + 32 + 40])
            sel16, sel4 = sel[:, 0:P], sel[:, P:2 * P]
            back16, back4 = sel[:, 256:264], sel[:, 264:296]
            col16, col4 = sel[:, 296:312], sel[:, 312:316]
            bcol16, bcol4 = sel[:, 316:332], sel[:, 332:336]
            moved = sb("moved", [P, 2, 5, P])
            moved_back = moved[:, :, :, :].rearrange("p a b n -> p (a b) n")
        ps_s = ctx.enter_context(nc.psum_tensor(kind + "_ps_s", [P, 2, 2, 2 * P], F32))
        ps_t = ctx.enter_context(nc.psum_tensor(kind + "_ps_t", [P, 2, 2, 2 * P], F32))
        ps_o = ctx.enter_context(nc.psum_tensor(kind + "_ps_o", [P, 2, CHUNK], F32))
        ps_x = ctx.enter_context(nc.psum_tensor(kind + "_ps_x", [P, 2, CHUNK], F32))

        consts = sem("consts")
        q_loaded = [sem(f"q_loaded{s}") for s in range(2)]
        k_loaded = [sem(f"k_loaded{s}") for s in range(2)]
        v_loaded = [sem(f"v_loaded{s}") for s in range(2)]
        gate_loaded = [sem(f"gate_loaded{b}") for b in range(2)]
        y_stored = [sem(f"y_stored{b}") for b in range(2)]
        scores_ready, max_ready, sums_ready = sem("scores_ready"), sem("max_ready"), sem("sums_ready")
        weighted, turned, turned_copied = sem("weighted"), sem("turned"), sem("turned_copied")
        values_done = sem("values_done")
        kept = sem("kept")
        bank_read, y_ready = sem("bank_read"), sem("y_ready")
        coef_ready = sem("coef_ready")
        spread, gathered, shifted, exps_ready = sem("spread"), sem("gathered"), sem("shifted"), sem("exps_ready")
        step, spread_back, gathered_back = sem("step"), sem("spread_back"), sem("gathered_back")
        CONSTS = 32 if kind == "C" else 48
        DVE_STEPS = 5 if kind == "B" else 1

        def rounds(eng, scores, second):
            def round_(a, c):
                for slot in range(NP + LAG):
                    scores(a, slot) if a else None
                    second(c, slot) if c else None
            round_((0, 0), None)
            round_((0, 1), (0, 0))
            with eng.Fori(1, heads) as h:
                round_((h, 0), (h - 1, 1))
                round_((h, 1), (h, 0))
            for slot in range(NP + LAG):
                second((heads - 1, 1), slot)

        def number(phase):
            return phase[0] * 2 + phase[1]

        with nc.Block() as block:
            @block.sync
            def _(sp):
                sp.dma_start(mask[:], io["mask" + kind]).then_inc(consts, 16)
                sp.dma_start(ident[:], io["ident"]).then_inc(consts, 16)
                if kind == "A":
                    sp.dma_start(sink[:, 0, :], io["sink"].broadcast_to([P, heads])).then_inc(consts, 16)
                if kind == "B":
                    sp.dma_start(sel[:], io["sel"]).then_inc(consts, 16)

                def load_q(h, s):
                    rows = bass.ds(q_row + h * HD, HD)
                    cols = slice(s * HALF, (s + 1) * HALF)
                    sp.dma_start(q[0:HD, s, :].bitcast(F32), sc["qk_hi"][rows, cols]).then_inc(q_loaded[s], 16)
                    sp.dma_start(q[HD:P, s, :].bitcast(F32), sc["qk_lo"][rows, cols]).then_inc(q_loaded[s], 16)

                def load_k(h, s):
                    n = NMEM if kind == "C" else HALF
                    hi, lo, row = {"A": (sc["qk_hi"], sc["qk_lo"], KA + (h // 3) * HD),
                                   "B": (sc["qk_hi"], sc["qk_lo"], KB + h * HD),
                                   "C": (sc["mk_hi"], sc["mk_lo"], h * HD)}[kind]
                    for part, place in ((hi, k_hi), (lo, k_lo)):
                        for half in range(2):
                            sp.dma_start(place[half * HD:(half + 1) * HD, s * HALF:s * HALF + n].bitcast(F32),
                                         part[bass.ds(row, HD), s * HALF:s * HALF + n]).then_inc(k_loaded[s], 16)

                def load_v(h, s):
                    sp.nop(nofuse=True)
                    if kind == "C":
                        sp.dma_start(v["v1"][:, 0, 0:2, :], sc["mv"][:, bass.ts(h, HD)].rearrange(
                            "(t p) n -> p t n", p=P)).then_inc(v_loaded[s], 16)
                        return
                    col = (h // 3) * HD if kind == "A" else P + h * HD
                    rows = sc["v"][s * HALF:(s + 1) * HALF, bass.ds(col, HD)]
                    views = {"v16": ("(p r) n -> p r n", dict(r=16)), "v1": ("(b p) n -> p b n", dict(p=P))}
                    for n in kinds_v:
                        if n == "v4":
                            for c in range(NCH):
                                sp.dma_start(v[n][:, s, 4 * c:4 * c + 4, :], rows[c * CHUNK:(c + 1) * CHUNK, :].rearrange(
                                    "(p r) n -> p r n", r=4)).then_inc(v_loaded[s], 16)
                        else:
                            sp.dma_start(v[n][:, s, :, :], rows.rearrange(views[n][0], **views[n][1])).then_inc(
                                v_loaded[s], 16)

                def head(h, first):
                    p0, p1 = (h - 1) * 2, (h - 1) * 2 + 1
                    if not first:
                        sp.wait_ge(scores_ready, p0 * NP + NP)
                    load_q(h, 0)
                    if kind == "C":
                        if not first:
                            sp.wait_ge(scores_ready, p1 * NP + NP)
                        load_k(h, 0)
                        load_q(h, 1)
                        if not first:
                            sp.wait_ge(values_done, p1 * NP + NP)
                        load_v(h, 0)
                        return
                    if not first:
                        sp.wait_ge(scores_ready, p1 * NP + EARLY)
                    load_k(h, 0)
                    if not first:
                        sp.wait_ge(scores_ready, p1 * NP + NP)
                    load_q(h, 1)
                    load_k(h, 1)
                    if not first:
                        sp.wait_ge(values_done, p1 * NP + EARLY)
                    load_v(h, 0)
                    if not first:
                        sp.wait_ge(values_done, p1 * NP + NP)
                    load_v(h, 1)
                head(0, True)
                with sp.Fori(1, heads) as h:
                    head(h, False)

            @block.tensor
            def _(pe):
                pe.wait_ge(consts, CONSTS)

                def scores(phase, slot):
                    h, s = phase
                    n = number(phase) * NP + slot
                    if slot >= NP:
                        if kind == "B":
                            exchange(phase, slot - NP)
                        return
                    if slot == 0:
                        pe.wait_ge(q_loaded[s], 32 * h + 32)
                        if kind != "C" or s == 0:
                            pe.wait_ge(k_loaded[s], 64 * h + 64)
                    ge(pe, max_ready, n - 1)
                    for j in range(2):
                        u = FLAT[s][2 * slot + j]
                        out = ps_s[:, slot % 2, j, 2 * P - u.keys:]
                        w = q[:, s, strided(u.q[0], P, u.q[1])]
                        keys = strided(u.k[0], u.keys, u.k[1])
                        nc.tensor.matmul(out, w, k_hi[:, keys], start=True, stop=False)
                        last = nc.tensor.matmul(out, w, k_lo[:, keys], start=False, stop=True)
                    last.then_inc(scores_ready, 1)

                def exchange(phase, k):
                    p, s = number(phase), phase[1]
                    if k == 1:
                        pe.wait_ge(spread, p + 1)
                        for x in range(2):
                            nc.tensor.matmul(ps_x[:, 0, 16 * x:16 * x + 16], moved[:, x, 0, :], col16,
                                             start=True, stop=True)
                            for c in range(NCH):
                                at = 32 + 16 * x + 4 * c
                                last = nc.tensor.matmul(ps_x[:, 0, at:at + 4], moved[:, x, 1 + c, :], col4,
                                                        start=True, stop=True)
                        last.then_inc(gathered, 1)
                    if k == 3:
                        pe.wait_ge(spread_back, p + 1)
                        nc.tensor.matmul(ps_x[:, 1, 0:16], moved_back[:, 0, :], bcol16, start=True, stop=True)
                        for c in range(NCH):
                            last = nc.tensor.matmul(ps_x[:, 1, 16 + 4 * c:20 + 4 * c], moved_back[:, 1 + c, :], bcol4,
                                                    start=True, stop=True)
                        last.then_inc(gathered_back, 1)

                def times_values(phase, e):
                    h, s = phase
                    p = number(phase)
                    pe.wait_ge(turned_copied, p * NP + e + 1)
                    for j in range(2):
                        n = 2 * e + j
                        u = FLAT[s][n]
                        bank = bank_of[n]
                        if n in first_of:
                            if 2 <= bank < MERGED + 2 and MERGED:
                                pe.wait_ge(kept, p * MERGED + bank - 1)
                            else:
                                before = p * NCH + (bank - MERGED - 2 if bank >= 2 else bank - 2)
                                ge(pe, bank_read, before + 1)
                        for i, (name, half, tile) in enumerate(u.tiles):
                            at = 2 - len(u.tiles) + i
                            last = nc.tensor.matmul(ps_o[0:HD, bank % 2, strided(u.out[0], P, u.out[1])],
                                                    v[name][:, half, tile, :], pT[:, e % 2, j, at * P:(at + 1) * P],
                                                    start=n in first_of and i == 0,
                                                    stop=e in last_of and j == 1 and i == len(u.tiles) - 1,
                                                    skip_group_check=True)
                    last.then_inc(values_done, 1)

                def second(phase, slot):
                    h, s = phase
                    e = slot - LAG
                    p = number(phase)
                    if e < 0:
                        return
                    if e == 0:
                        if kind != "C":
                            pe.wait_ge(v_loaded[s], 16 * (6 if kind == "B" else 1) * (h + 1))
                        elif s == 0:
                            pe.wait_ge(v_loaded[0], 16 * h + 16)
                    pe.wait_ge(weighted, p * NP + e + 1)
                    ge(pe, turned_copied, p * NP + e - 1)
                    for j in range(2):
                        u = FLAT[s][2 * e + j]
                        for at in range(2 - len(u.tiles), 2):
                            last = nc.tensor.transpose(ps_t[:, e % 2, j, at * P:(at + 1) * P],
                                                       probs[:, s, 2 * e + j, at * P:(at + 1) * P], ident[:])
                    last.then_inc(turned, 1)
                    if e > 0:
                        times_values(phase, e - 1)
                    if e == NP - 1:
                        times_values(phase, e)
                rounds(pe, scores, second)

            @block.vector
            def _(dve):
                dve.wait_ge(consts, CONSTS)
                if kind == "A":
                    nc.vector.tensor_scalar(sink[:, 1, :], sink[:, 0, :], -1.0, None, ALU.mult).then_inc(coef_ready, 1)
                    dve.wait_ge(coef_ready, 1)
                C1 = 1 if kind == "A" else 0

                def scores(phase, slot):
                    h, s = phase
                    p = number(phase)
                    if slot >= NP:
                        (exchange if kind == "B" else inverse)(phase, slot - NP)
                        return
                    n = p * NP + slot
                    dve.wait_ge(scores_ready, n + 1)
                    ge(dve, turned, n + 1 - 2 * NP)
                    if kind == "A" and slot == 0:
                        dve.nop(nofuse=True)
                        nc.vector.tensor_copy(sink_now[:, s, :], sink[:, :, bass.ds(h, 1)].rearrange(
                            "p a o -> p (a o)")).then_inc(sink_ready, 1)
                        dve.wait_ge(sink_ready, p + 1)
                    dve.nop(nofuse=True)
                    for j in range(2):
                        u = FLAT[s][2 * slot + j]
                        a = 2 * P - u.keys
                        start = sink_now[:, s, 1:2] if kind == "A" else 3e38
                        last = nc.vector.tensor_tensor_reduce(
                            out=probs[:, s, 2 * slot + j, a:], in0=ps_s[:, slot % 2, j, a:], in1=mask[:, a:],
                            scale=-SCALE, scalar=start, op0=ALU.add, op1=ALU.min,
                            accum_out=stat[:, s, 0, u.column:u.column + 1])
                    last.then_inc(max_ready, 1)

                def inverse(phase, k):
                    p, s = number(phase), phase[1]
                    if k == 1:
                        dve.wait_ge(sums_ready, p * NP + NP)
                        if kind == "A":
                            dve.wait_ge(exps_ready, p + 1)
                            nc.vector.tensor_tensor(work[:, 1, :], work[:, 0, :], stat[:, s, 1, :],
                                                    ALU.add).then_inc(step, 1)
                            dve.wait_ge(step, p + 1)
                            nc.vector.reciprocal(coef[:, s, :], work[:, 1, :]).then_inc(coef_ready, 1)
                        else:
                            nc.vector.reciprocal(coef[:, s, :], stat[:, s, 1, :]).then_inc(coef_ready, 1)

                def exchange(phase, k):
                    p, s = number(phase), phase[1]
                    n = [p * DVE_STEPS + (2 if k == 2 else 0)]

                    def own(ins):
                        n[0] = n[0] + 1
                        ins.then_inc(step, 1)
                        dve.wait_ge(step, n[0])
                    m1 = stat[:, s, 0, 32:48]
                    x = ps_x[:, 0, 0:64].rearrange("p (a x n) -> p a x n", a=2, x=2)
                    if k == 0:
                        dve.wait_ge(sums_ready, p * NP + NP)
                        for a in range(2):
                            nc.vector.tensor_tensor(moved[:, a, 0, :].rearrange("p (a r) -> p a r", r=16),
                                                    stat[:, s, a, 0:16].unsqueeze(1).broadcast_to([P, 8, 16]),
                                                    sel16.rearrange("p (a r) -> p a r", r=16), ALU.mult)
                            last = nc.vector.tensor_tensor(
                                moved[:, a, 1:5, :].rearrange("p c (a r) -> p c a r", r=4),
                                stat[:, s, a, 16:32].rearrange("p (c r) -> p c r", r=4).unsqueeze(2).broadcast_to([P, 4, 32, 4]),
                                sel4.rearrange("p (a r) -> p a r", r=4).unsqueeze(1).broadcast_to([P, 4, 32, 4]), ALU.mult)
                        last.then_inc(spread, 1)
                    if k == 1:
                        dve.wait_ge(gathered, p + 1)
                        own(nc.vector.tensor_tensor(work[:, 0, 0:16], x[:, 0, 0, :], m1, ALU.min))
                        own(nc.vector.tensor_tensor(work[:, 1, 0:16], x[:, 1, 0, :], work[:, 0, 0:16], ALU.min))
                        low = work[:, 1, 0:16]
                        nc.vector.tensor_tensor(work[:, 2, 0:32].rearrange("p (a n) -> p a n", a=2),
                                                low.unsqueeze(1).broadcast_to([P, 2, 16]), x[:, :, 0, :], ALU.subtract)
                        nc.vector.tensor_tensor(work[:, 2, 32:48], low, m1, ALU.subtract).then_inc(shifted, 1)
                    if k == 2:
                        dve.wait_ge(exps_ready, p + 1)
                        ex = work[:, 3, :]
                        nc.vector.tensor_tensor(work[:, 4, 0:32].rearrange("p (a n) -> p a n", a=2),
                                                ex[:, 0:32].rearrange("p (a n) -> p a n", a=2), x[:, :, 1, :], ALU.mult)
                        own(nc.vector.tensor_tensor(work[:, 4, 32:48], ex[:, 32:48], stat[:, s, 1, 32:48], ALU.mult))
                        own(nc.vector.reduce_sum(work[:, 5, 0:16], work[:, 4, :].rearrange("p (a n) -> p n a", a=3),
                                                 mybir.AxisListType.X))
                        own(nc.vector.reciprocal(work[:, 6, 0:16], work[:, 5, 0:16]))
                        inv = work[:, 6, 0:16]
                        nc.vector.tensor_tensor(coef[:, s, 32:48], ex[:, 32:48], inv, ALU.mult)
                        nc.vector.tensor_tensor(work[:, 7, 0:32].rearrange("p (a n) -> p a n", a=2),
                                                ex[:, 0:32].rearrange("p (a n) -> p a n", a=2),
                                                inv.unsqueeze(1).broadcast_to([P, 2, 16]), ALU.mult).then_inc(shifted, 1)
                        dve.wait_ge(shifted, 2 * p + 2)
                        nc.vector.tensor_tensor(moved_back[:, 0, :].rearrange("p (n a) -> p n a", a=8),
                                                work[:, 7, 0:16].unsqueeze(2).broadcast_to([P, 16, 8]),
                                                back16.unsqueeze(1).broadcast_to([P, 16, 8]), ALU.mult)
                        nc.vector.tensor_tensor(moved_back[:, 1:5, :].rearrange("p c (b a) -> p (c b) a", a=32),
                                                work[:, 7, 16:32].unsqueeze(2).broadcast_to([P, 16, 32]),
                                                back4.unsqueeze(1).broadcast_to([P, 16, 32]), ALU.mult).then_inc(spread_back, 1)
                    if k == 3:
                        dve.wait_ge(gathered_back, p + 1)
                        nc.vector.tensor_copy(coef[:, s, 0:32], ps_x[:, 1, 0:32]).then_inc(coef_ready, 1)

                def second(phase, slot):
                    h, s = phase
                    p = number(phase)
                    e = slot - LAG + 1
                    if 0 <= e < NP:
                        if e == 0:
                            dve.wait_ge(coef_ready, p + 1 + C1)
                        for j in range(2):
                            u = FLAT[s][2 * e + j]
                            place = probs[:, s, 2 * e + j, 2 * P - u.keys:]
                            last = nc.vector.tensor_scalar(place, place, coef[:, s, u.column:u.column + 1], None, ALU.mult)
                        last.then_inc(weighted, 1)
                    done = slot - LAG - 2
                    for d in ([done] if slot < NP + LAG - 1 else [NP - 3, NP - 2, NP - 1]):
                        if d in last_of and last_of[d] >= MERGED:
                            finish_bank(phase, d, last_of[d] - MERGED)

                def finish_bank(phase, d, c):
                    p = number(phase)
                    n = p * NCH + c
                    dve.wait_ge(values_done, p * NP + d + 1)
                    if not isinstance(n, int) or n >= 2:
                        dve.wait_ge(y_stored[c % 2], 16 * (p * 2 + c // 2))
                    dve.wait_ge(gate_loaded[c % 2], 16 * (p * 2 + c // 2) + 16)
                    out = ps_o[0:HD, (MERGED + c) % 2, :]
                    if kind == "B":
                        dve.wait_ge(kept, p * MERGED + MERGED)
                        nc.vector.tensor_tensor(y[:, c % 2, :].rearrange("p (j r) -> p j r", r=16),
                                                out.rearrange("p (j r) -> p j r", r=16),
                                                o16[:, :, 32 * c:32 * c + 32].rearrange("p r j -> p j r"),
                                                ALU.add).then_inc(bank_read, 1)
                        dve.wait_ge(bank_read, n + 1)
                        nc.vector.tensor_tensor(y[:, c % 2, :], y[:, c % 2, :], gate[:, c % 2, :],
                                                ALU.mult).then_inc(y_ready, 1)
                    else:
                        nc.vector.tensor_tensor(y[:, c % 2, :], out, gate[:, c % 2, :], ALU.mult).then_inc(bank_read, 1)
                rounds(dve, scores, second)

            @block.scalar
            def _(act):
                done_sem = y_ready if kind == "B" else bank_read
                act.wait_ge(consts, CONSTS)

                def load_gate(phase, c, first=False):
                    h, s = phase
                    n = number(phase) * NCH + c
                    ge(act, done_sem, n - 1)
                    act.dma_start(gate[:, c % 2, :], sc["gate"][bass.ds(y_row + h * HD, HD),
                                  s * HALF + c * CHUNK:s * HALF + (c + 1) * CHUNK]).then_inc(gate_loaded[c % 2], 16)

                def store(phase, c):
                    h, s = phase
                    act.wait_ge(done_sem, number(phase) * NCH + c + 1)
                    act.dma_start(sc["y"][bass.ds(y_row + h * HD, HD), s * HALF + c * CHUNK:s * HALF + (c + 1) * CHUNK],
                                  y[:, c % 2, :]).then_inc(y_stored[c % 2], 16)

                def scores(phase, slot):
                    h, s = phase
                    p = number(phase)
                    if slot >= NP:
                        if kind == "A" and slot == NP:
                            act.wait_ge(max_ready, p * NP + NP)
                            nc.scalar.activation(work[:, 0, :], stat[:, s, 0, :], ACT.Exp,
                                                 bias=sink_now[:, s, 0:1]).then_inc(exps_ready, 1)
                        if kind == "B" and slot == NP + 1:
                            act.wait_ge(shifted, 2 * p + 1)
                            nc.scalar.activation(work[:, 3, :], work[:, 2, :], ACT.Exp).then_inc(exps_ready, 1)
                        return
                    act.wait_ge(max_ready, p * NP + slot + 1)
                    for j in range(2):
                        u = FLAT[s][2 * slot + j]
                        place = probs[:, s, 2 * slot + j, 2 * P - u.keys:]
                        last = nc.scalar.activation(place, place, ACT.Exp, scale=-1.0,
                                                    bias=stat[:, s, 0, u.column:u.column + 1],
                                                    accum_out=stat[:, s, 1, u.column:u.column + 1])
                    last.then_inc(sums_ready, 1)

                def second(phase, slot):
                    h, s = phase
                    p = number(phase)
                    e = slot - LAG
                    if e == -1:
                        for c in range(2):
                            load_gate(phase, c)
                    if e < 0:
                        return
                    act.wait_ge(turned, p * NP + e + 1)
                    ge(act, values_done, p * NP + e - 1)
                    a = [2 * P - FLAT[s][2 * e + j].keys for j in range(2)]
                    if a[0] == a[1]:
                        nc.scalar.activation(pT[:, e % 2, :, a[0]:], ps_t[:, e % 2, :, a[0]:],
                                             ACT.Copy).then_inc(turned_copied, 1)
                    else:
                        nc.scalar.activation(pT[:, e % 2, 0, a[0]:], ps_t[:, e % 2, 0, a[0]:], ACT.Copy)
                        nc.scalar.activation(pT[:, e % 2, 1, a[1]:], ps_t[:, e % 2, 1, a[1]:],
                                             ACT.Copy).then_inc(turned_copied, 1)
                    for d in ([e - 2] if e < NP - 1 else [NP - 3, NP - 2, NP - 1]):
                        if d in last_of and last_of[d] < MERGED:
                            keep(phase, d, last_of[d])
                    for d in ([e - 3] if e < NP - 1 else [NP - 4, NP - 3, NP - 2, NP - 1]):
                        if d in last_of and last_of[d] >= MERGED:
                            c = last_of[d] - MERGED
                            if c + 2 < NCH:
                                load_gate(phase, c + 2)
                            store(phase, c)

                def keep(phase, d, g):
                    p = number(phase)
                    act.wait_ge(values_done, p * NP + d + 1)
                    ge(act, y_ready, p * NCH)
                    nc.scalar.activation(o16[:, 4 * g:4 * g + 4, :].rearrange("p r j -> p (r j)"),
                                         ps_o[0:HD, g % 2, :], ACT.Copy).then_inc(kept, 1)
                rounds(act, scores, second)
                for b in range(2):
                    act.wait_ge(y_stored[b], 16 * 2 * 2 * heads)


def finish_stage(nc, io, sc, out):
    with ExitStack() as ctx:
        sb = lambda n, s, d=F32: ctx.enter_context(nc.sbuf_tensor("f_" + n, s, d))
        sem = lambda n: ctx.enter_context(nc.semaphore("f_" + n))
        TW = 256
        NB = SEQ // TW
        w_raw = sb("w_raw", [P, 2, D])
        w_hi = sb("w_hi", [P, KD, D], F32R)
        w_lo = sb("w_lo", [P, KD, D], F32R)
        gain = sb("gain", [P, D])
        yT = sb("yT", [P, 2, KD, TW])
        y_hi = sb("y_hi", [P, 2, KD, TW], F32R)
        y_lo = sb("y_lo", [P, 2, KD, TW], F32R)
        xb = sb("xb", [P, 2, D])
        o = sb("o", [P, 2, D])
        junk = sb("junk", [P, D])
        ss = sb("ss", [P, 2, 4])
        ps = ctx.enter_context(nc.psum_tensor("f_ps", [P, 4, 2, CHUNK], F32))
        gain_loaded = sem("gain_loaded")
        w_loaded = [sem(f"w_loaded{b}") for b in range(2)]
        y_loaded = [sem(f"y_loaded{b}") for b in range(2)]
        x_loaded = [sem(f"x_loaded{b}") for b in range(2)]
        stored = [sem(f"stored{b}") for b in range(2)]
        w_hi_ready, w_lo_ready, y_hi_ready, y_lo_ready = sem("w_hi_ready"), sem("w_lo_ready"), sem("y_hi_ready"), sem("y_lo_ready")
        multiplied, squared, meaned, rooted = sem("multiplied"), sem("squared"), sem("meaned"), sem("rooted")
        inverted, normed, added = sem("inverted"), sem("normed"), sem("added")
        with nc.Block() as block:
            @block.sync
            def _(sp):
                def load_y(i, b):
                    for k in range(0, KD, 4):
                        sp.dma_start(yT[:, b, k:k + 4, :], sc["y"][k * P:(k + 4) * P, bass.ts(i, TW)].rearrange(
                            "(k p) n -> p k n", p=P)).then_inc(y_loaded[b], 16)

                def load_x(i, b):
                    sp.dma_start(xb[:, b, :], io["x"][bass.ts(i, P), :]).then_inc(x_loaded[b], 16)

                def store(i, b):
                    sp.wait_ge(added, i + 1)
                    sp.dma_start(out[bass.ts(i, P), :], o[:, b, :]).then_inc(stored[b], 16)
                sp.dma_start(gain[:], io["post_gain"].broadcast_to([P, D])).then_inc(gain_loaded, 16)
                load_y(0, 0)
                for k in range(KD):
                    if k >= 2:
                        sp.wait_ge(w_lo_ready, k - 1)
                    sp.dma_start(w_raw[:, k % 2, :], io["w_out"][k * P:(k + 1) * P, :]).then_inc(w_loaded[k % 2], 16)
                load_y(1, 1)
                load_x(0, 0)
                load_x(1, 1)
                with sp.Fori(0, NB // 2 - 1) as two:
                    i = 2 * two
                    for b in range(2):
                        for t in range(2):
                            store(2 * (i + b) + t, t)
                            load_x(2 * (i + b) + t + 2, t)
                        sp.wait_ge(y_lo_ready, i + b + 1)
                        load_y(i + b + 2, b)
                for t in range(4):
                    store(2 * NB - 4 + t, t % 2)
                    if t < 2:
                        load_x(2 * NB - 2 + t, t)
                for b in range(2):
                    sp.wait_ge(stored[b], 16 * NB)

            @block.scalar
            def _(act):
                def part(i, b):
                    act.wait_ge(y_loaded[b], 32 * ((i - b) // 2) + 32 if isinstance(i, int) else 16 * (i - b) + 32)
                    if not isinstance(i, int) or i >= 2:
                        act.wait_ge(multiplied, 2 * i - 2)
                    nc.scalar.activation(y_hi[:, b, :, :], yT[:, b, :, :], ACT.Copy).then_inc(y_hi_ready, 1)

                def square(i, b):
                    act.wait_ge(multiplied, i + 1)
                    nc.scalar.activation(junk[:], ps[:, b, :, :].rearrange("p a n -> p (a n)"), ACT.Square,
                                         accum_out=ss[:, b % 2, 0:1]).then_inc(squared, 1)
                    act.wait_ge(meaned, i + 1)
                    nc.scalar.activation(ss[:, b % 2, 2:3], ss[:, b % 2, 1:2], ACT.Sqrt).then_inc(rooted, 1)
                part(0, 0)
                for k in range(KD):
                    act.wait_ge(w_loaded[k % 2], 16 * (k // 2) + 16)
                    nc.scalar.activation(w_hi[:, k, :], w_raw[:, k % 2, :], ACT.Copy).then_inc(w_hi_ready, 1)
                part(1, 1)
                with act.Fori(0, NB // 2 - 1) as two:
                    i = 2 * two
                    for b in range(2):
                        for t in range(2):
                            square(2 * (i + b) + t, 2 * b + t)
                        part(i + b + 2, b)
                for t in range(4):
                    square(2 * NB - 4 + t, t)

            @block.vector
            def _(dve):
                dve.wait_ge(gain_loaded, 16)

                def part(i, b):
                    dve.wait_ge(y_hi_ready, i + 1)
                    nc.vector.tensor_tensor(y_lo[:, b, :, :], yT[:, b, :, :], y_hi[:, b, :, :].bitcast(F32),
                                            ALU.subtract).then_inc(y_lo_ready, 1)

                def norm(i, b):
                    dve.wait_ge(squared, i + 1)
                    nc.vector.tensor_scalar(ss[:, b % 2, 1:2], ss[:, b % 2, 0:1], 1.0 / D, EPS,
                                            ALU.mult, ALU.add).then_inc(meaned, 1)
                    dve.wait_ge(rooted, i + 1)
                    nc.vector.reciprocal(ss[:, b % 2, 3:4], ss[:, b % 2, 2:3]).then_inc(inverted, 1)
                    dve.wait_ge(inverted, i + 1)
                    if not isinstance(i, int) or i >= 2:
                        dve.wait_ge(stored[b % 2], 16 * ((i - b % 2) // 2) if isinstance(i, int) else 8 * (i - b % 2))
                    nc.vector.scalar_tensor_tensor(out=o[:, b % 2, :], in0=ps[:, b, :, :].rearrange("p a n -> p (a n)"),
                                                   scalar=ss[:, b % 2, 3:4], in1=gain[:],
                                                   op0=ALU.mult, op1=ALU.mult).then_inc(normed, 1)
                    dve.wait_ge(normed, i + 1)
                    dve.wait_ge(x_loaded[b % 2], 16 * ((i - b % 2) // 2) + 16 if isinstance(i, int)
                                else 8 * (i - b % 2) + 16)
                    nc.vector.tensor_tensor(o[:, b % 2, :], o[:, b % 2, :], xb[:, b % 2, :], ALU.add).then_inc(added, 1)
                part(0, 0)
                for k in range(KD):
                    dve.wait_ge(w_hi_ready, k + 1)
                    nc.vector.tensor_tensor(w_lo[:, k, :], w_raw[:, k % 2, :], w_hi[:, k, :].bitcast(F32),
                                            ALU.subtract).then_inc(w_lo_ready, 1)
                part(1, 1)
                for t in range(2):
                    norm(t, t)
                part(2, 0)
                for t in range(2):
                    norm(2 + t, 2 + t)
                part(3, 1)
                with dve.Fori(1, NB // 2 - 1) as two:
                    i = 2 * two
                    for b in range(2):
                        for t in range(2):
                            norm(2 * (i + b) + t, 2 * b + t)
                        part(i + b + 2, b)
                for t in range(4):
                    norm(2 * NB - 4 + t, t)

            @block.tensor
            def _(pe):
                def product(i, b):
                    pe.wait_ge(y_lo_ready, i + 1)
                    for t in range(2):
                        if not isinstance(i, int) or i >= 2:
                            pe.wait_ge(normed, 2 * i + t - 3)
                        for c in range(2):
                            for k in range(KD):
                                if isinstance(i, int) and i == 0 and t == 0 and c == 0:
                                    pe.wait_ge(w_lo_ready, k + 1)
                                y, cols = slice(t * P, (t + 1) * P), slice(c * CHUNK, (c + 1) * CHUNK)
                                last = split_product(nc, ps[:, 2 * b + t, c, :], y_hi[:, b, k, y], y_lo[:, b, k, y],
                                                     w_hi[:, k, cols], w_lo[:, k, cols], k == 0, k == KD - 1)
                        last.then_inc(multiplied, 1)
                product(0, 0)
                product(1, 1)
                with pe.Fori(1, NB // 2) as two:
                    i = 2 * two
                    for b in range(2):
                        product(i + b, b)


def build(nc, io, out):
    scratch = lambda n, s, d=F32: nc.dram_tensor("scratch_" + n, s, d, kind="Internal").ap()
    sc = {
        "qk_hi": scratch("qk_hi", [NQK * P, SEQ]), "qk_lo": scratch("qk_lo", [NQK * P, SEQ]),
        "v": scratch("v", [SEQ, len(V_TILES) * P]), "gate": scratch("gate", [D, SEQ]), "y": scratch("y", [D, SEQ]),
        "mk_hi": scratch("mk_hi", [256, NMEM]), "mk_lo": scratch("mk_lo", [256, NMEM]),
        "mv": scratch("mv", [NMEM, 256]),
    }
    memory_stage(nc, io, sc)
    project_stage(nc, io, sc)
    for kind in "BAC":
        attend_stage(nc, io, sc, kind)
    finish_stage(nc, io, sc, out)


def constants():
    import numpy as np
    rot = HD // 4
    inv = (np.float32(500000.0) ** (-np.arange(0, rot, 2, dtype=np.float32) / np.float32(rot))).astype(np.float32)
    ang = (np.arange(SEQ, dtype=np.float32)[None, :] * inv[:, None]).astype(np.float32)
    c, s = np.cos(ang).astype(np.float32), np.sin(ang).astype(np.float32)
    cos, sin = np.ones((P, SEQ), np.float32), np.zeros((P, SEQ), np.float32)
    for h in (0, HD):
        cos[h:h + 8], cos[h + 8:h + 16] = c, c
        sin[h:h + 8], sin[h + 8:h + 16] = -s, s
    q, k = np.arange(P)[:, None], np.arange(P)[None, :]
    diag = np.where(k <= q, 0.0, NEG)
    mask_a = np.concatenate([np.where(k > q, 0.0, NEG), diag], 1).astype(np.float32)
    mask_b = np.concatenate([np.where(k >= q, 0.0, NEG), diag], 1).astype(np.float32)
    j = np.arange(P)[:, None]
    n = lambda m: np.arange(m)[None, :]
    sel = np.concatenate([
        j % 8 == n(P) // 16,
        j % 32 == n(P) // 4,
        j // 16 == n(8), j // 4 == n(32),
        j // 8 == n(16), j // 32 == n(4), j % 16 == n(16), j % 4 == n(4),
    ], 1).astype(np.float32)
    return {"cos": cos, "sin": sin, "maskA": mask_a, "maskB": mask_b, "maskC": np.zeros((P, 2 * P), np.float32),
            "sel": sel, "ident": np.eye(P, dtype=np.float32)}


def kernel(x, mem, pre_norm, w_in, sink_a, mem_norm, w_mem_kv, w_out, post_norm):
    import numpy as np
    import concourse.bacc as bacc
    from concourse.bass_utils import run_bass_kernel_spmd

    nc = bacc.Bacc("TRN2", target_bir_lowering=False, num_devices=1)
    w = np.asarray(w_in)[0].reshape(KD, P, NT, P).transpose(2, 1, 0, 3)[np.array(ORDER)]
    given = {
        "x": np.asarray(x)[0], "mem": np.asarray(mem)[0], "pre_gain": np.asarray(pre_norm), "w_in": w.reshape(NT, P, D),
        "sink": np.asarray(sink_a), "mem_gain": np.asarray(mem_norm), "w_mem": np.asarray(w_mem_kv)[0],
        "w_out": np.asarray(w_out)[0], "post_gain": np.asarray(post_norm), **constants(),
    }
    arrays = {f"in_{n}": np.ascontiguousarray(a) for n, a in given.items()}
    io = {n: nc.dram_tensor(f"in_{n}", a.shape, F32, kind="ExternalInput").ap() for n, a in given.items()}
    out = nc.dram_tensor("out_0", [SEQ, D], F32, kind="ExternalOutput").ap()
    build(nc, io, out)
    r = run_bass_kernel_spmd(nc, [arrays], core_ids=[0])
    return r.results[0]["out_0"].reshape(1, SEQ, D)
```

```python
from contextlib import ExitStack

import concourse.bass as bass
from concourse import mybir

F32 = mybir.dt.float32
F32R = mybir.dt.float32r
ALU = mybir.AluOpType
ACT = mybir.ActivationFunctionType

P = 128
D = 1024
KD = D // P
SEQ = 4096
NMEM = 256
HD = 64
CHUNK = 512
HALF = SEQ // 2
NCH = HALF // CHUNK
SCALE = HD ** -0.5
NEG = -1e30
EPS = 1e-6
ROPE_TILES = [0, 1, 2, 3, 8, 9, 10, 11, 12, 13]
PLAIN_TILES = [20, 21]
V_TILES = [4, 14, 15, 16]
GATE_TILES = [5, 6, 7, 17, 18, 19, 22, 23]
ORDER = ROPE_TILES + PLAIN_TILES + V_TILES + GATE_TILES
NT = len(ORDER)
NQK = len(ROPE_TILES) + len(PLAIN_TILES)
QA, KA, QB, KB, QC = 0, 384, 512, 896, 1280
SWAP = [8, 9, 10, 11, 12, 13, 14, 15, 0, 1, 2, 3, 4, 5, 6, 7] + list(range(16, 32))


def split_product(nc, out, w_hi, w_lo, m_hi, m_lo, first, last):
    nc.tensor.matmul(out, w_hi, m_hi, start=first, stop=False)
    nc.tensor.matmul(out, w_hi, m_lo, start=False, stop=False)
    return nc.tensor.matmul(out, w_lo, m_hi, start=False, stop=last)


def project_stage(nc, io, sc):
    with ExitStack() as ctx:
        sb = lambda n, s, d=F32: ctx.enter_context(nc.sbuf_tensor("p_" + n, s, d))
        sem = lambda n: ctx.enter_context(nc.semaphore("p_" + n))
        QT = SEQ // 4
        NCH = QT // CHUNK
        XT = QT // P
        MT = NMEM // P
        with ExitStack() as early:
            tmp = lambda n, s, d=F32: early.enter_context(nc.sbuf_tensor("m_" + n, s, d))
            mem = tmp("mem", [P, MT, D])
            um = tmp("um", [P, MT, D])
            umT = tmp("umT", [P, KD, NMEM])
            mem_gain = tmp("gain", [P, D])
            w_mem = tmp("w", [P, KD, 512])
            mk_hi = tmp("k_hi", [P, 2, NMEM], F32R)
            mk_lo = tmp("k_lo", [P, 2, NMEM], F32R)
            mem_v = tmp("v", [P, MT, 256])
        uT_hi, uT_lo = {}, {}
        for half in (1, 0):
            uT_hi[half] = sb(f"uT_hi{half}", [P, KD, QT], F32R)
            uT_lo[half] = sb(f"uT_lo{half}", [P, KD, QT], F32R)
        w_hi = sb("w_hi", [P, 2, KD, P], F32R)
        w_lo = sb("w_lo", [P, 2, KD, P], F32R)
        w_raw = sb("w_raw", [P, 2, D])
        xb = sb("x", [P, 2, D])
        ub = sb("u", [P, 2, D])
        gain = sb("gain", [P, D])
        ident = sb("ident", [P, P])
        ss = sb("ss", [P, 2, 4])
        cos = sb("cos", [P, QT])
        sin = sb("sin", [P, QT])
        turned = sb("turned", [P, CHUNK])
        rot = sb("rot", [P, 2, CHUNK])
        o_hi = sb("o_hi", [P, 2, CHUNK], F32R)
        o_lo = sb("o_lo", [P, 2, CHUNK], F32R)
        vT = sb("vT", [P, 2, CHUNK])
        o_v = sb("o_v", [P, 2, CHUNK])
        o_g = rot
        ps = ctx.enter_context(nc.psum_tensor("p_ps", [P, 4, CHUNK], F32))
        ps_t = ctx.enter_context(nc.psum_tensor("p_ps_t", [P, 2, 2, CHUNK], F32))
        m_ss = sb("m_ss", [P, 3 * MT])
        m_loaded, m_weights, m_squared, m_meaned = sem("m_loaded"), sem("m_weights"), sem("m_squared"), sem("m_meaned")
        m_rooted, m_inverted, m_scaled, m_turned = sem("m_rooted"), sem("m_inverted"), sem("m_scaled"), sem("m_turned")
        m_copied, m_multiplied, m_hi_ready, m_lo_ready = (sem("m_copied"), sem("m_multiplied"), sem("m_hi_ready"),
                                                          sem("m_lo_ready"))
        m_v_ready, m_stored = sem("m_v_ready"), sem("m_stored")
        consts, table = sem("consts"), sem("table")
        x_loaded = [sem(f"x_loaded{b}") for b in range(2)]
        squared, meaned, rooted, inverted = sem("squared"), sem("meaned"), sem("rooted"), sem("inverted")
        u_ready, u_turned, uT_hi_ready, uT_lo_ready = sem("u_ready"), sem("u_turned"), sem("uT_hi_ready"), sem("uT_lo_ready")
        w_loaded = [sem(f"w_loaded{b}") for b in range(2)]
        w_hi_ready, w_lo_ready = sem("w_hi_ready"), sem("w_lo_ready")
        multiplied = sem("multiplied")
        chain, straight = sem("chain"), sem("straight")
        rotated, hi_ready = sem("rotated"), sem("hi_ready")
        out_ready = sem("out_ready")
        vT_ready, v_turned = sem("vT_ready"), sem("v_turned")
        qk_stored, v_stored, g_stored = ([sem(f"{n}_stored{b}") for b in range(2)] for n in ("qk", "v", "g"))

        NR, NQ, NV, NG = len(ROPE_TILES), NQK, len(V_TILES), len(GATE_TILES)
        GATES = NQ + NV
        assert NG == XT and QT % (2 * P) == 0

        def pairs(eng, quarter, lo, hi, body, peel=False):
            end = hi - 2 if peel else hi
            if quarter == 0 and lo in (0, NQ) and end - lo > 2:
                for b in range(2):
                    body(lo + b, b, False)
                lo += 2
            if end - lo > 2:
                with eng.Fori(lo // 2, end // 2) as two:
                    i = 2 * two
                    for b in range(2):
                        body(i + b, b, False)
            elif end > lo:
                for b in range(2):
                    body(lo + b, b, False)
            if peel:
                for b in range(2):
                    body(end + b, b, end + b == hi - 1)

        def wait_stored(eng, sems, n, c):
            if not isinstance(n, int) or n >= 1:
                eng.wait_ge(sems[c], (32 if sems is qk_stored else 16) * n)

        with nc.Block() as block:
            @block.sync
            def _(sp):
                def load_x(quarter, t, b):
                    n = quarter * XT + t
                    if not isinstance(n, int) or n >= 2:
                        sp.wait_ge(u_ready, n - 1)
                    sp.dma_start(xb[:, b, :], io["x"][bass.ts(n, P), :]).then_inc(x_loaded[b], 16)

                def load_w(i, b):
                    sp.dma_start(w_raw[:, b, :], io["w_in"][i, :, :]).then_inc(w_loaded[b], 16)

                def load_tables(quarter):
                    for t, d in ((cos, "cos"), (sin, "sin")):
                        sp.dma_start(t[:], io[d][:, quarter * QT:(quarter + 1) * QT]).then_inc(table, 16)

                load_x(0, 0, 0)
                sp.dma_start(gain[:], io["pre_gain"].broadcast_to([P, D])).then_inc(consts, 16)
                sp.dma_start(ident[:], io["ident"]).then_inc(consts, 16)
                load_x(0, 1, 1)
                load_w(0, 0)
                sp.dma_start(mem[:], io["mem"].rearrange("(t p) d -> p t d", p=P)).then_inc(m_loaded, 16)
                sp.dma_start(mem_gain[:], io["mem_gain"].broadcast_to([P, D])).then_inc(m_loaded, 16)
                for t in range(2, XT):
                    load_x(0, t, t % 2)
                    if t == 3:
                        sp.dma_start(w_mem[:], io["w_mem"].rearrange("(k p) n -> p k n", p=P)).then_inc(m_weights, 16)
                load_w(1, 1)
                load_tables(0)
                sp.wait_ge(m_hi_ready, 1)
                sp.wait_ge(m_lo_ready, 1)
                sp.dma_start(sc["mk_hi"].rearrange("(t p) n -> p t n", p=P), mk_hi[:].bitcast(F32)).then_inc(m_stored, 16)
                sp.dma_start(sc["mk_lo"].rearrange("(t p) n -> p t n", p=P), mk_lo[:].bitcast(F32)).then_inc(m_stored, 16)
                sp.wait_ge(m_v_ready, 1)
                sp.dma_start(sc["mv"].rearrange("(t p) n -> p t n", p=P), mem_v[:]).then_inc(m_stored, 16)

                for quarter in range(4):
                    C0 = quarter * NT * NCH

                    def next_w(i, b):
                        if isinstance(i, int) and i + 2 >= NT and quarter == 3:
                            return
                        sp.wait_ge(w_lo_ready, quarter * NT + i + 1)
                        load_w(i + 2 - NT if isinstance(i, int) and i + 2 >= NT else i + 2, b)

                    def store_qk(i, b, last):
                        next_w(i, b)
                        for c in range(NCH):
                            sp.wait_ge(out_ready, C0 + i * NCH + c + 1)
                            at = (quarter * NCH + c) * CHUNK
                            for src, dst in ((o_hi, sc["qk_hi"]), (o_lo, sc["qk_lo"])):
                                sp.dma_start(dst[bass.ts(i, P), at:at + CHUNK],
                                             src[:, c, :].bitcast(F32)).then_inc(qk_stored[c], 16)

                    def store_v(i, b, last):
                        next_w(i, b)
                        for c in range(NCH):
                            sp.wait_ge(out_ready, C0 + i * NCH + c + 1)
                            at = (quarter * NCH + c) * CHUNK
                            dst = sc["v"][at:at + CHUNK, bass.ts(i - NQ, P)].rearrange("(t p) n -> p t n", p=P)
                            sp.dma_start(dst, o_v[:, c, :].rearrange("p (t n) -> p t n", n=P)).then_inc(v_stored[c], 16)

                    def store_g(i, b, last):
                        next_w(i, b)
                        for c in range(NCH):
                            sp.wait_ge(out_ready, C0 + i * NCH + c + 1)
                            at = (quarter * NCH + c) * CHUNK
                            sp.dma_start(sc["gate"][bass.ts(i - GATES, P), at:at + CHUNK],
                                         o_g[:, c, :]).then_inc(g_stored[c], 16)
                        if quarter < 3 and not (isinstance(i, int) and i + 2 >= NT):
                            load_x(quarter + 1, i - GATES + 2, b)

                    pairs(sp, quarter, 0, NR, store_qk)
                    if quarter < 3:
                        load_tables(quarter + 1)
                    pairs(sp, quarter, NR, NQ, store_qk)
                    if quarter < 3:
                        load_x(quarter + 1, 0, 0)
                        load_x(quarter + 1, 1, 1)
                    pairs(sp, quarter, NQ, GATES, store_v)
                    pairs(sp, quarter, GATES, NT, store_g, peel=True)
                sp.wait_ge(m_stored, 48)
                for b in range(2):
                    sp.wait_ge(qk_stored[b], 32 * NQ * 4)
                    sp.wait_ge(v_stored[b], 16 * NV * 4)
                    sp.wait_ge(g_stored[b], 16 * NG * 4)

            @block.scalar
            def _(act):
                def square(quarter, t, b):
                    n = quarter * XT + t
                    act.wait_ge(x_loaded[b], quarter * 8 * XT + (t - b) * 8 + 16)
                    if not isinstance(n, int) or n >= 2:
                        act.wait_ge(u_turned, n - 1)
                    nc.scalar.activation(ub[:, b, :], xb[:, b, :], ACT.Square,
                                         accum_out=ss[:, b, 0:1]).then_inc(squared, 1)
                    act.wait_ge(meaned, n + 1)
                    nc.scalar.activation(ss[:, b, 2:3], ss[:, b, 1:2], ACT.Sqrt).then_inc(rooted, 1)

                def part(quarter, t, b):
                    act.wait_ge(u_turned, quarter * XT + t + 1)
                    nc.scalar.activation(uT_hi[quarter % 2][:, :, bass.ts(t, P)],
                                         ps_t[:, b, :, :].rearrange("p a (k n) -> p (a k) n", n=P),
                                         ACT.Copy).then_inc(uT_hi_ready, 1)

                def w_part(quarter, i, b):
                    act.wait_ge(w_loaded[b], 16 * quarter * (NT // 2) + (i - b) * 8 + 16)
                    if quarter or not isinstance(i, int) or i >= 2:
                        act.wait_ge(multiplied, quarter * NT * NCH + (i - 1) * NCH)
                    nc.scalar.activation(w_hi[:, b, :, :].rearrange("p k n -> p (k n)"), w_raw[:, b, :],
                                         ACT.Copy).then_inc(w_hi_ready, 1)

                square(0, 0, 0)
                w_part(0, 0, 0)
                square(0, 1, 1)
                for t in range(2, XT):
                    part(0, t - 2, t % 2)
                    square(0, t, t % 2)
                    if t == 4:
                        act.wait_ge(m_loaded, 32)
                        for m in range(MT):
                            nc.scalar.activation(um[:, m, :], mem[:, m, :], ACT.Square,
                                                 accum_out=m_ss[:, m:m + 1]).then_inc(m_squared, 1)
                        act.wait_ge(m_meaned, 1)
                        nc.scalar.activation(m_ss[:, 4:6], m_ss[:, 2:4], ACT.Sqrt).then_inc(m_rooted, 1)
                part(0, XT - 2, 0)
                part(0, XT - 1, 1)
                act.wait_ge(m_multiplied, 1)
                nc.scalar.activation(mk_hi[:], ps[:, 0:2, 0:NMEM], ACT.Copy).then_inc(m_hi_ready, 1)
                act.wait_ge(m_multiplied, 2)
                nc.scalar.activation(mem_v[:], ps[:, 2:4, 0:256], ACT.Copy).then_inc(m_v_ready, 1)

                for quarter in range(4):
                    C0 = quarter * NT * NCH

                    def next_w(i, b):
                        if isinstance(i, int) and i + 1 == NT:
                            if quarter < 3:
                                w_part(quarter + 1, 0, 0)
                        else:
                            w_part(quarter, i + 1, 1 - b)

                    def rope(i, b, last):
                        next_w(i, b)
                        for c in range(NCH):
                            act.wait_ge(rotated, quarter * NR * NCH + i * NCH + c + 1)
                            wait_stored(act, qk_stored, quarter * NQ + i, c)
                            nc.scalar.activation(o_hi[:, c, :], rot[:, c, :], ACT.Copy).then_inc(hi_ready, 1)

                    def plain(i, b, last):
                        next_w(i, b)
                        for c in range(NCH):
                            act.wait_ge(multiplied, C0 + i * NCH + c + 1)
                            wait_stored(act, qk_stored, quarter * NQ + i, c)
                            nc.scalar.activation(o_hi[:, c, :], ps[:, 2 * b + c, :], ACT.Copy).then_inc(hi_ready, 1)

                    def values(i, b, last):
                        next_w(i, b)
                        for c in range(NCH + 1):
                            if c < NCH:
                                act.wait_ge(multiplied, C0 + i * NCH + c + 1)
                                n = quarter * NV * NCH + (i - NQ) * NCH + c
                                if not isinstance(n, int) or n >= 2:
                                    act.wait_ge(v_turned, n - 1)
                                nc.scalar.activation(vT[:, c, :], ps[:, 2 * b + c, :], ACT.Copy).then_inc(vT_ready, 1)
                            if c > 0:
                                act.wait_ge(v_turned, quarter * NV * NCH + (i - NQ) * NCH + c)
                                wait_stored(act, v_stored, quarter * NV + i - NQ, c - 1)
                                nc.scalar.activation(o_v[:, c - 1, :], ps_t[:, c - 1, 0, :],
                                                     ACT.Copy).then_inc(out_ready, 1)

                    def gates(i, b, last):
                        next_w(i, b)
                        if quarter < 3:
                            square(quarter + 1, i - GATES, b)
                        for c in range(NCH):
                            act.wait_ge(multiplied, C0 + i * NCH + c + 1)
                            wait_stored(act, g_stored, quarter * NG + i - GATES, c)
                            nc.scalar.activation(o_g[:, c, :], ps[:, 2 * b + c, :], ACT.Silu).then_inc(out_ready, 1)
                            if c == 0 and quarter < 3:
                                if quarter == 0:
                                    act.wait_ge(m_stored, 48)
                                part(quarter + 1, i - GATES, b)

                    pairs(act, quarter, 0, NR, rope)
                    pairs(act, quarter, NR, NQ, plain)
                    act.wait_ge(out_ready, C0 + NQ * NCH)
                    pairs(act, quarter, NQ, GATES, values)
                    pairs(act, quarter, GATES, NT, gates, peel=True)

            @block.vector
            def _(dve):
                def normalise(quarter, t, b):
                    n = quarter * XT + t
                    dve.wait_ge(squared, n + 1)
                    nc.vector.tensor_scalar(ss[:, b, 1:2], ss[:, b, 0:1], 1.0 / D, EPS,
                                            ALU.mult, ALU.add).then_inc(meaned, 1)
                    dve.wait_ge(rooted, n + 1)
                    nc.vector.reciprocal(ss[:, b, 3:4], ss[:, b, 2:3]).then_inc(inverted, 1)
                    dve.wait_ge(inverted, n + 1)
                    nc.vector.scalar_tensor_tensor(out=ub[:, b, :], in0=xb[:, b, :], scalar=ss[:, b, 3:4],
                                                   in1=gain[:], op0=ALU.mult, op1=ALU.mult).then_inc(u_ready, 1)

                def part(quarter, t, b):
                    dve.wait_ge(uT_hi_ready, quarter * XT + t + 1)
                    place = (slice(None), slice(None), bass.ts(t, P))
                    nc.vector.tensor_tensor(uT_lo[quarter % 2][place],
                                            ps_t[:, b, :, :].rearrange("p a (k n) -> p (a k) n", n=P),
                                            uT_hi[quarter % 2][place].bitcast(F32), ALU.subtract).then_inc(uT_lo_ready, 1)

                def w_part(quarter, i, b):
                    dve.wait_ge(w_hi_ready, quarter * NT + i + 1)
                    nc.vector.tensor_tensor(w_lo[:, b, :, :].rearrange("p k n -> p (k n)"), w_raw[:, b, :],
                                            w_hi[:, b, :, :].rearrange("p k n -> p (k n)").bitcast(F32),
                                            ALU.subtract).then_inc(w_lo_ready, 1)

                dve.wait_ge(consts, 32)
                normalise(0, 0, 0)
                w_part(0, 0, 0)
                normalise(0, 1, 1)
                for t in range(2, XT):
                    part(0, t - 2, t % 2)
                    normalise(0, t, t % 2)
                    if t == 4:
                        dve.wait_ge(m_squared, MT)
                        nc.vector.tensor_scalar(m_ss[:, 2:4], m_ss[:, 0:2], 1.0 / D, EPS, ALU.mult, ALU.add).then_inc(m_meaned, 1)
                        dve.wait_ge(m_rooted, 1)
                        nc.vector.reciprocal(m_ss[:, 0:2], m_ss[:, 4:6]).then_inc(m_inverted, 1)
                        dve.wait_ge(m_inverted, 1)
                        for m in range(MT):
                            nc.vector.scalar_tensor_tensor(out=um[:, m, :], in0=mem[:, m, :], scalar=m_ss[:, m:m + 1],
                                                           in1=mem_gain[:], op0=ALU.mult, op1=ALU.mult).then_inc(m_scaled, 1)
                dve.wait_ge(m_turned, 1)
                nc.vector.tensor_copy(umT[:].rearrange("p (b k) n -> p b (k n)", b=4), ps[:]).then_inc(m_copied, 1)
                part(0, XT - 2, 0)
                part(0, XT - 1, 1)
                dve.wait_ge(m_hi_ready, 1)
                nc.vector.tensor_tensor(mk_lo[:], ps[:, 0:2, 0:NMEM], mk_hi[:].bitcast(F32), ALU.subtract).then_inc(m_lo_ready, 1)

                for quarter in range(4):
                    C0 = quarter * NT * NCH

                    def next_w(i, b):
                        if isinstance(i, int) and i + 1 == NT:
                            if quarter < 3:
                                w_part(quarter + 1, 0, 0)
                        else:
                            w_part(quarter, i + 1, 1 - b)

                    def low(i, c, src):
                        dve.wait_ge(hi_ready, quarter * NQ * NCH + i * NCH + c + 1)
                        nc.vector.tensor_tensor(o_lo[:, c, :], src, o_hi[:, c, :].bitcast(F32),
                                                ALU.subtract).then_inc(out_ready, 1)

                    def rope(i, b, last):
                        next_w(i, b)
                        for c in range(NCH):
                            cols = slice(c * CHUNK, (c + 1) * CHUNK)
                            bank = ps[:, 2 * b + c, :]
                            n = quarter * NR * NCH + i * NCH + c
                            dve.wait_ge(multiplied, C0 + i * NCH + c + 1)
                            if not isinstance(n, int) or n >= 1:
                                dve.wait_ge(rotated, n)
                            if not isinstance(n, int) or n >= 2:
                                dve.wait_ge(out_ready, C0 + i * NCH + c - 1)
                            dve.nop(nofuse=True)
                            nc.vector.stream_shuffle(turned[:], bank, SWAP).then_inc(chain, 1)
                            nc.vector.tensor_tensor(rot[:, c, :], bank, cos[:, cols], ALU.mult).then_inc(straight, 1)
                            dve.wait_ge(chain, 2 * n + 1)
                            nc.vector.tensor_tensor(turned[:], turned[:], sin[:, cols], ALU.mult).then_inc(chain, 1)
                            dve.wait_ge(chain, 2 * n + 2)
                            dve.wait_ge(straight, n + 1)
                            nc.vector.tensor_tensor(rot[:, c, :], rot[:, c, :], turned[:], ALU.add).then_inc(rotated, 1)
                            low(i, c, rot[:, c, :])

                    def plain(i, b, last):
                        next_w(i, b)
                        for c in range(NCH):
                            dve.wait_ge(multiplied, C0 + i * NCH + c + 1)
                            low(i, c, ps[:, 2 * b + c, :])

                    def values(i, b, last):
                        next_w(i, b)

                    def gates(i, b, last):
                        next_w(i, b)
                        if quarter < 3:
                            normalise(quarter + 1, i - GATES, b)
                            if quarter == 0:
                                dve.wait_ge(m_stored, 48)
                            part(quarter + 1, i - GATES, b)

                    dve.wait_ge(table, 32 * (quarter + 1))
                    if quarter:
                        for c in range(NCH):
                            dve.wait_ge(g_stored[c], 16 * NG * quarter)
                    pairs(dve, quarter, 0, NR, rope)
                    pairs(dve, quarter, NR, NQ, plain)
                    pairs(dve, quarter, NQ, GATES, values)
                    pairs(dve, quarter, GATES, NT, gates, peel=True)

            @block.tensor
            def _(pe):
                pe.wait_ge(consts, 32)

                def turn(quarter, t, b):
                    n = quarter * XT + t
                    pe.wait_ge(u_ready, n + 1)
                    if not isinstance(n, int) or n >= 2:
                        pe.wait_ge(uT_lo_ready, n - 1)
                    for k in range(KD):
                        last = nc.tensor.transpose(ps_t[:, b, k // 4, (k % 4) * P:(k % 4 + 1) * P],
                                                   ub[:, b, k * P:(k + 1) * P], ident[:])
                    last.then_inc(u_turned, 1)

                for t in range(XT):
                    turn(0, t, t % 2)
                    if t == XT - 3:
                        pe.wait_ge(m_scaled, MT)
                        for k in range(KD):
                            for m in range(MT):
                                at = (k % 2) * NMEM + m * P
                                last = nc.tensor.transpose(ps[:, k // 2, at:at + P], um[:, m, k * P:(k + 1) * P], ident[:])
                        last.then_inc(m_turned, 1)
                pe.wait_ge(m_weights, 16)
                pe.wait_ge(m_copied, 1)
                for c in range(2):
                    for k in range(KD):
                        last = nc.tensor.matmul(ps[:, c, 0:NMEM], w_mem[:, k, c * P:(c + 1) * P], umT[:, k, :],
                                                start=k == 0, stop=k == KD - 1)
                last.then_inc(m_multiplied, 1)
                for m in range(MT):
                    for k in range(KD):
                        last = nc.tensor.matmul(ps[:, 2 + m, 0:256], umT[:, k, m * P:(m + 1) * P], w_mem[:, k, 256:512],
                                                start=k == 0, stop=k == KD - 1)
                last.then_inc(m_multiplied, 1)

                for quarter in range(4):
                    C0 = quarter * NT * NCH
                    half = quarter % 2
                    pe.wait_ge(uT_lo_ready, (quarter + 1) * XT)

                    def product(i, b, c):
                        n = C0 + i * NCH + c
                        if not isinstance(n, int) or n >= 4:
                            pe.wait_ge(out_ready, n - 3)
                        elif n == 0:
                            pe.wait_ge(m_lo_ready, 1)
                        elif n == 2:
                            pe.wait_ge(m_v_ready, 1)
                        cols = slice(c * CHUNK, (c + 1) * CHUNK)
                        for k in range(KD):
                            last = split_product(nc, ps[:, 2 * b + c, :], w_hi[:, b, k, :], w_lo[:, b, k, :],
                                                 uT_hi[half][:, k, cols], uT_lo[half][:, k, cols],
                                                 k == 0, k == KD - 1)
                        last.then_inc(multiplied, 1)

                    def tile(i, b, last):
                        pe.wait_ge(w_lo_ready, quarter * NT + i + 1)
                        for c in range(NCH):
                            product(i, b, c)

                    def turn_v(i, c):
                        n = quarter * NV * NCH + (i - NQ) * NCH + c
                        pe.wait_ge(vT_ready, n + 1)
                        if not isinstance(n, int) or n >= 2:
                            pe.wait_ge(out_ready, C0 + i * NCH + c - 1)
                        for t in range(CHUNK // P):
                            last = nc.tensor.transpose(ps_t[:, c, 0, t * P:(t + 1) * P],
                                                       vT[:, c, t * P:(t + 1) * P], ident[:])
                        last.then_inc(v_turned, 1)

                    def tile_v(i, b, last):
                        pe.wait_ge(w_lo_ready, quarter * NT + i + 1)
                        for c in range(NCH):
                            product(i, b, c)
                            if c:
                                turn_v(i, c - 1)
                        turn_v(i, NCH - 1)

                    def tile_g(i, b, last):
                        pe.wait_ge(w_lo_ready, quarter * NT + i + 1)
                        product(i, b, 0)
                        if quarter < 3:
                            pe.wait_ge(out_ready, C0 + i * NCH)
                            turn(quarter + 1, i - GATES, b)
                        product(i, b, 1)

                    pairs(pe, quarter, 0, NQ, tile)
                    pairs(pe, quarter, NQ, GATES, tile_v)
                    pairs(pe, quarter, GATES, NT, tile_g, peel=True)


class Unit:

    def __init__(self, q, k, keys, tiles, out, column):
        self.q, self.k, self.keys = q, k, keys
        self.tiles, self.out, self.column = tiles, out, column


def units_of(kind, s):
    groups = []
    if kind == "B":
        for g in range(4):
            groups.append([Unit((r, 16), (r, 16), 256 if s else 128, [("v16", 0, r), ("v16", 1, r)][0 if s else 0:2 if s else 1],
                                ((r % 4) * P, 1), r) for r in range(4 * g, 4 * g + 4)])
    for c in range(NCH):
        group = []
        if kind == "B":
            for r in range(4):
                n = NCH * s + c
                tiles = [("v4", m // NCH, (m % NCH) * 4 + r) for m in (n - 1, n) if m >= 0]
                group.append(Unit((CHUNK * c + r, 4), (CHUNK * max(n - 1, 0) + r, 4), P * len(tiles), tiles,
                                  (r, 4), 16 + 4 * c + r))
        for b in range(4 * c, 4 * c + 4):
            n = 16 * s + b
            if kind == "C":
                tiles, k = [("v1", s, 0), ("v1", s, 1)], NMEM * s
            else:
                tiles, k = [("v1", m // 16, m % 16) for m in (n - 1, n) if m >= 0], P * max(n - 1, 0)
            group.append(Unit((P * b, 1), (k, 1), P * len(tiles), tiles, ((b % 4) * P, 1),
                              (32 if kind == "B" else 0) + b))
        groups.append(group)
    return groups


def strided(start, n, step):
    return slice(start, start + (n - 1) * step + 1, step)


def attend_stage(nc, io, sc, kind):
    heads = {"A": 6, "B": 6, "C": 4}[kind]
    q_row = {"A": QA, "B": QB, "C": QC}[kind]
    y_row = {"A": 0, "B": 384, "C": 768}[kind]
    PLANS = [units_of(kind, s) for s in range(2)]
    FLAT = [[u for g in plan for u in g] for plan in PLANS]
    NU = len(FLAT[0])
    NP = NU // 2
    NG = len(PLANS[0])
    EARLY = 12 if kind == "B" else 1
    GB = 1 if kind == "B" else 2
    NS = 3 if kind == "B" else 4
    SCORED = NP - (4 if kind == "B" else 2)
    NKEY = 2 * NMEM if kind == "C" else SEQ
    kinds_v = {"A": ["v1"], "B": ["v16", "v4", "v1"], "C": ["v1"]}[kind]
    last_of = {}
    first_of = {}
    bank_of = []
    at = 0
    for g, group in enumerate(PLANS[0]):
        first_of[at] = g
        bank_of += [g] * len(group)
        at += len(group)
        last_of[at // 2 - 1] = g
    MERGED = NG - NCH

    def ge(eng, sem, value):
        if not isinstance(value, int) or value > 0:
            eng.wait_ge(sem, value)

    with ExitStack() as ctx:
        sb = lambda n, shape, d=F32: ctx.enter_context(nc.sbuf_tensor(kind + "_" + n, shape, d))
        sem = lambda n: ctx.enter_context(nc.semaphore(kind + "_" + n))
        q = sb("q", [P, 2, HALF], F32R)
        k_hi = sb("k_hi", [P, NKEY], F32R)
        k_lo = sb("k_lo", [P, NKEY], F32R)
        v = {n: sb(n, [P, 2, 16, HD]) for n in kinds_v}
        gate = sb("gate", [HD, GB, HALF])
        probs = sb("probs", [P, 2, NU, 2 * P])
        pT = sb("pT", [P, 2, 2, 2 * P])
        stat = sb("stat", [P, 2, 2, NU])
        coef = sb("coef", [P, 2, NU])
        mask = sb("mask", [P, 2 * P])
        ident = sb("ident", [P, P])
        y = sb("y", [HD, 2, CHUNK])
        work = sb("work", [P, 8, NU])
        if kind == "A":
            sink = sb("sink", [P, 2, heads])
            sink_now = sb("sink_now", [P, 2, 2])
            sink_ready = sem("sink_ready")
        if kind == "B":
            o16 = sb("o16", [HD, 16, P])
            sel = sb("sel", [P, 2 * P + 8 + 32 + 40])
            sel16, sel4 = sel[:, 0:P], sel[:, P:2 * P]
            back16, back4 = sel[:, 256:264], sel[:, 264:296]
            col16, col4 = sel[:, 296:312], sel[:, 312:316]
            bcol16, bcol4 = sel[:, 316:332], sel[:, 332:336]
            moved = sb("moved", [P, 2, 5, P])
            moved_back = moved[:, :, :, :].rearrange("p a b n -> p (a b) n")
        ps_s = ctx.enter_context(nc.psum_tensor(kind + "_ps_s", [P, NS, 2, 2 * P], F32))
        ps_t = ctx.enter_context(nc.psum_tensor(kind + "_ps_t", [P, 2, 2, 2 * P], F32))
        ps_o = ctx.enter_context(nc.psum_tensor(kind + "_ps_o", [P, 2, CHUNK], F32))
        if kind == "B":
            ps_x = ctx.enter_context(nc.psum_tensor(kind + "_ps_x", [P, CHUNK], F32))

        consts = sem("consts")
        q_loaded = [sem(f"q_loaded{s}") for s in range(2)]
        k_loaded = [sem(f"k_loaded{s}") for s in range(2)]
        v_loaded = [sem(f"v_loaded{s}") for s in range(2)]
        gate_loaded = [sem(f"gate_loaded{b}") for b in range(GB)]
        y_stored = [sem(f"y_stored{b}") for b in range(2)]
        scores_ready, max_ready, sums_ready = sem("scores_ready"), sem("max_ready"), sem("sums_ready")
        weighted, turned, turned_copied = sem("weighted"), sem("turned"), sem("turned_copied")
        values_done = sem("values_done")
        kept = sem("kept")
        bank_read, y_ready = sem("bank_read"), sem("y_ready")
        coef_ready = sem("coef_ready")
        spread, gathered, shifted, exps_ready = sem("spread"), sem("gathered"), sem("shifted"), sem("exps_ready")
        step, spread_back, gathered_back = sem("step"), sem("spread_back"), sem("gathered_back")
        CONSTS = 32 if kind == "C" else 48
        done_sem = y_ready if kind == "B" else bank_read
        DVE_STEPS = 5 if kind == "B" else 1

        def rounds(eng, scores, second, rest, late=False):
            def scores_in(a, slot):
                for v in range(NP):
                    if v * SCORED // NP == slot:
                        scores(a, v)
                if slot >= SCORED:
                    scores(a, NP + slot - SCORED)

            def round_(a, c, before):
                for slot in range(NP):
                    if a and not late:
                        scores_in(a, slot)
                    if before:
                        rest(before, slot)
                    if c:
                        second(c, slot)
                    if a and late:
                        scores_in(a, slot)
            round_((0, 0), None, None)
            round_((0, 1), (0, 0), None)
            with eng.Fori(1, heads) as h:
                round_((h, 0), (h - 1, 1), (h - 1, 0))
                round_((h, 1), (h, 0), (h - 1, 1))
            round_(None, (heads - 1, 1), (heads - 1, 0))
            for slot in range(4):
                rest((heads - 1, 1), slot)

        def nothing(phase, slot):
            pass

        def number(phase):
            return phase[0] * 2 + phase[1]

        with nc.Block() as block:
            @block.sync
            def _(sp):
                def load_consts():
                    sp.dma_start(mask[:], io["mask" + kind]).then_inc(consts, 16)
                    sp.dma_start(ident[:], io["ident"]).then_inc(consts, 16)
                    if kind == "A":
                        sp.dma_start(sink[:, 0, :], io["sink"].broadcast_to([P, heads])).then_inc(consts, 16)
                    if kind == "B":
                        sp.dma_start(sel[:], io["sel"]).then_inc(consts, 16)

                def load_q(h, s):
                    rows = bass.ds(q_row + h * HD, HD)
                    cols = slice(s * HALF, (s + 1) * HALF)
                    sp.dma_start(q[0:HD, s, :].bitcast(F32), sc["qk_hi"][rows, cols]).then_inc(q_loaded[s], 16)
                    sp.dma_start(q[HD:P, s, :].bitcast(F32), sc["qk_lo"][rows, cols]).then_inc(q_loaded[s], 16)

                def load_k(h, s):
                    n = NKEY // 2
                    to = slice(s * n, (s + 1) * n)
                    cols = slice(0, n) if kind == "C" else to
                    hi, lo, row = {"A": (sc["qk_hi"], sc["qk_lo"], KA + (h // 3) * HD),
                                   "B": (sc["qk_hi"], sc["qk_lo"], KB + h * HD),
                                   "C": (sc["mk_hi"], sc["mk_lo"], h * HD)}[kind]
                    for part, place in ((hi, k_hi), (lo, k_lo)):
                        for half in range(2):
                            sp.dma_start(place[half * HD:(half + 1) * HD, to].bitcast(F32),
                                         part[bass.ds(row, HD), cols]).then_inc(k_loaded[s], 16)

                def load_v(h, s):
                    sp.nop(nofuse=True)
                    if kind == "C":
                        sp.dma_start(v["v1"][:, s, 0:2, :], sc["mv"][:, bass.ts(h, HD)].rearrange(
                            "(t p) n -> p t n", p=P)).then_inc(v_loaded[s], 16)
                        return
                    col = (h // 3) * HD if kind == "A" else P + h * HD
                    rows = sc["v"][s * HALF:(s + 1) * HALF, bass.ds(col, HD)]
                    views = {"v16": ("(p r) n -> p r n", dict(r=16)), "v1": ("(b p) n -> p b n", dict(p=P))}
                    for n in kinds_v:
                        if n == "v4":
                            for c in range(NCH):
                                sp.dma_start(v[n][:, s, 4 * c:4 * c + 4, :], rows[c * CHUNK:(c + 1) * CHUNK, :].rearrange(
                                    "(p r) n -> p r n", r=4)).then_inc(v_loaded[s], 16)
                        else:
                            sp.dma_start(v[n][:, s, :, :], rows.rearrange(views[n][0], **views[n][1])).then_inc(
                                v_loaded[s], 16)

                def load_gate(h, s):
                    p = h * 2 + s
                    ge(sp, done_sem, (p - GB + 1) * NCH)
                    sp.dma_start(gate[:, s % GB, :], sc["gate"][bass.ds(y_row + h * HD, HD),
                                                               s * HALF:(s + 1) * HALF]).then_inc(gate_loaded[s % GB], 16)

                def head(h, first, new_keys=True):
                    p0, p1 = (h - 1) * 2, (h - 1) * 2 + 1

                    def used(sem, phase, n_pairs):
                        if not first:
                            sp.wait_ge(sem, phase * NP + n_pairs)
                    used(scores_ready, p0, NP)
                    load_q(h, 0)
                    if new_keys:
                        used(scores_ready, *((p0, NP) if kind == "C" else (p1, EARLY)))
                        load_k(h, 0)
                    used(scores_ready, p1, NP)
                    load_q(h, 1)
                    if new_keys:
                        load_k(h, 1)
                    if not first:
                        load_gate(h - 1, 1)
                    if new_keys:
                        used(values_done, *((p0, NP) if kind == "C" else (p1, EARLY)))
                        load_v(h, 0)
                        used(values_done, p1, NP)
                        load_v(h, 1)
                    load_gate(h, 0)
                load_consts()
                head(0, True)
                if kind == "A":
                    for h in range(1, heads, 3):
                        with sp.Fori(h, h + 2) as i:
                            head(i, False, new_keys=False)
                        if h + 2 < heads:
                            head(h + 2, False)
                else:
                    with sp.Fori(1, heads) as h:
                        head(h, False)
                load_gate(heads - 1, 1)

            @block.tensor
            def _(pe):
                pe.wait_ge(consts, CONSTS)

                between = {}

                def scores(phase, slot):
                    h, s = phase
                    n = number(phase) * NP + slot
                    if slot >= NP:
                        if kind == "B" and isinstance(h, int) and h + s == 0:
                            exchange(phase, slot - NP)
                        elif kind == "B":
                            between[slot - NP] = phase
                        return
                    if slot == 0:
                        pe.wait_ge(q_loaded[s], 32 * h + 32)
                        pe.wait_ge(k_loaded[s], 64 * (h // 3 if kind == "A" else h) + 64)
                    ge(pe, max_ready, n - NS + 1)
                    for j in range(2):
                        u = FLAT[s][2 * slot + j]
                        out = ps_s[:, slot % NS, j, 2 * P - u.keys:]
                        w = q[:, s, strided(u.q[0], P, u.q[1])]
                        keys = strided(u.k[0], u.keys, u.k[1])
                        nc.tensor.matmul(out, w, k_hi[:, keys], start=True, stop=False)
                        last = nc.tensor.matmul(out, w, k_lo[:, keys], start=False, stop=True)
                    last.then_inc(scores_ready, 1)

                def exchange(phase, k):
                    p, s = number(phase), phase[1]
                    if k == 1:
                        pe.wait_ge(spread, p + 1)
                        for x in range(2):
                            nc.tensor.matmul(ps_x[:, 16 * x:16 * x + 16], moved[:, x, 0, :], col16,
                                             start=True, stop=True)
                            for c in range(NCH):
                                at = 32 + 16 * x + 4 * c
                                last = nc.tensor.matmul(ps_x[:, at:at + 4], moved[:, x, 1 + c, :], col4,
                                                        start=True, stop=True)
                        last.then_inc(gathered, 1)
                    if k == 3:
                        pe.wait_ge(spread_back, p + 1)
                        nc.tensor.matmul(ps_x[:, 64:80], moved_back[:, 0, :], bcol16, start=True, stop=True)
                        for c in range(NCH):
                            last = nc.tensor.matmul(ps_x[:, 80 + 4 * c:84 + 4 * c], moved_back[:, 1 + c, :], bcol4,
                                                    start=True, stop=True)
                        last.then_inc(gathered_back, 1)

                def times_values(phase, e):
                    h, s = phase
                    p = number(phase)
                    pe.wait_ge(turned_copied, p * NP + e + 1)
                    for j in range(2):
                        n = 2 * e + j
                        u = FLAT[s][n]
                        bank = bank_of[n]
                        if n in first_of:
                            if 2 <= bank < MERGED + 2 and MERGED:
                                pe.wait_ge(kept, p * MERGED + bank - 1)
                            else:
                                before = p * NCH + (bank - MERGED - 2 if bank >= 2 else bank - 2)
                                ge(pe, bank_read, before + 1)
                        for i, (name, half, tile) in enumerate(u.tiles):
                            at = 2 - len(u.tiles) + i
                            last = nc.tensor.matmul(ps_o[0:HD, bank % 2, strided(u.out[0], P, u.out[1])],
                                                    v[name][:, half, tile, :], pT[:, e % 2, j, at * P:(at + 1) * P],
                                                    start=n in first_of and i == 0,
                                                    stop=e in last_of and j == 1 and i == len(u.tiles) - 1,
                                                    skip_group_check=True)
                    last.then_inc(values_done, 1)

                def second(phase, slot):
                    h, s = phase
                    e = slot
                    p = number(phase)
                    if e == 0:
                        pe.wait_ge(v_loaded[s], 16 * (6 if kind == "B" else 1) * ((h // 3 if kind == "A" else h) + 1))
                    pe.wait_ge(weighted, p * NP + e + 1)
                    ge(pe, turned_copied, p * NP + e - 1)
                    for j in range(2):
                        u = FLAT[s][2 * e + j]
                        for at in range(2 - len(u.tiles), 2):
                            last = nc.tensor.transpose(ps_t[:, e % 2, j, at * P:(at + 1) * P],
                                                       probs[:, s, 2 * e + j, at * P:(at + 1) * P], ident[:])
                    last.then_inc(turned, 1)
                    for k in list(between):
                        exchange(between.pop(k), k)
                    if e > 0:
                        times_values(phase, e - 1)
                    if e == NP - 1:
                        times_values(phase, e)
                rounds(pe, scores, second, nothing)

            @block.vector
            def _(dve):
                dve.wait_ge(consts, CONSTS)
                if kind == "A":
                    nc.vector.tensor_scalar(sink[:, 1, :], sink[:, 0, :], -1.0, None, ALU.mult).then_inc(coef_ready, 1)
                    dve.wait_ge(coef_ready, 1)
                C1 = 1 if kind == "A" else 0

                def scores(phase, slot):
                    h, s = phase
                    p = number(phase)
                    if slot >= NP:
                        (exchange if kind == "B" else inverse)(phase, slot - NP)
                        return
                    n = p * NP + slot
                    dve.wait_ge(scores_ready, n + 1)
                    ge(dve, turned, n + 1 - 2 * NP)
                    if kind == "A" and slot == 0:
                        dve.nop(nofuse=True)
                        nc.vector.tensor_copy(sink_now[:, s, :], sink[:, :, bass.ds(h, 1)].rearrange(
                            "p a o -> p (a o)")).then_inc(sink_ready, 1)
                        dve.wait_ge(sink_ready, p + 1)
                    dve.nop(nofuse=True)
                    for j in range(2):
                        u = FLAT[s][2 * slot + j]
                        a = 2 * P - u.keys
                        start = sink_now[:, s, 1:2] if kind == "A" else 3e38
                        last = nc.vector.tensor_tensor_reduce(
                            out=probs[:, s, 2 * slot + j, a:], in0=ps_s[:, slot % NS, j, a:], in1=mask[:, a:],
                            scale=-SCALE, scalar=start, op0=ALU.add, op1=ALU.min,
                            accum_out=stat[:, s, 0, u.column:u.column + 1])
                    last.then_inc(max_ready, 1)

                def inverse(phase, k):
                    p, s = number(phase), phase[1]
                    if k == 1:
                        dve.wait_ge(sums_ready, p * NP + NP)
                        if kind == "A":
                            dve.wait_ge(exps_ready, p + 1)
                            nc.vector.tensor_tensor(work[:, 1, :], work[:, 0, :], stat[:, s, 1, :],
                                                    ALU.add).then_inc(step, 1)
                            dve.wait_ge(step, p + 1)
                            nc.vector.reciprocal(coef[:, s, :], work[:, 1, :]).then_inc(coef_ready, 1)
                        else:
                            nc.vector.reciprocal(coef[:, s, :], stat[:, s, 1, :]).then_inc(coef_ready, 1)

                def exchange(phase, k):
                    p, s = number(phase), phase[1]
                    n = [p * DVE_STEPS + (2 if k == 2 else 0)]

                    def own(ins):
                        n[0] = n[0] + 1
                        ins.then_inc(step, 1)
                        dve.wait_ge(step, n[0])
                    m1 = stat[:, s, 0, 32:48]
                    x = ps_x[:, 0:64].rearrange("p (a x n) -> p a x n", a=2, x=2)
                    if k == 0:
                        dve.wait_ge(sums_ready, p * NP + NP)
                        for a in range(2):
                            nc.vector.tensor_tensor(moved[:, a, 0, :].rearrange("p (a r) -> p a r", r=16),
                                                    stat[:, s, a, 0:16].unsqueeze(1).broadcast_to([P, 8, 16]),
                                                    sel16.rearrange("p (a r) -> p a r", r=16), ALU.mult)
                            last = nc.vector.tensor_tensor(
                                moved[:, a, 1:5, :].rearrange("p c (a r) -> p c a r", r=4),
                                stat[:, s, a, 16:32].rearrange("p (c r) -> p c r", r=4).unsqueeze(2).broadcast_to([P, 4, 32, 4]),
                                sel4.rearrange("p (a r) -> p a r", r=4).unsqueeze(1).broadcast_to([P, 4, 32, 4]), ALU.mult)
                        last.then_inc(spread, 1)
                    if k == 1:
                        dve.wait_ge(gathered, p + 1)
                        own(nc.vector.tensor_tensor(work[:, 0, 0:16], x[:, 0, 0, :], m1, ALU.min))
                        own(nc.vector.tensor_tensor(work[:, 1, 0:16], x[:, 1, 0, :], work[:, 0, 0:16], ALU.min))
                        low = work[:, 1, 0:16]
                        nc.vector.tensor_tensor(work[:, 2, 0:32].rearrange("p (a n) -> p a n", a=2),
                                                low.unsqueeze(1).broadcast_to([P, 2, 16]), x[:, :, 0, :], ALU.subtract)
                        nc.vector.tensor_tensor(work[:, 2, 32:48], low, m1, ALU.subtract).then_inc(shifted, 1)
                    if k == 2:
                        dve.wait_ge(exps_ready, p + 1)
                        ex = work[:, 3, :]
                        nc.vector.tensor_tensor(work[:, 4, 0:32].rearrange("p (a n) -> p a n", a=2),
                                                ex[:, 0:32].rearrange("p (a n) -> p a n", a=2), x[:, :, 1, :], ALU.mult)
                        own(nc.vector.tensor_tensor(work[:, 4, 32:48], ex[:, 32:48], stat[:, s, 1, 32:48], ALU.mult))
                        own(nc.vector.reduce_sum(work[:, 5, 0:16], work[:, 4, :].rearrange("p (a n) -> p n a", a=3),
                                                 mybir.AxisListType.X))
                        own(nc.vector.reciprocal(work[:, 6, 0:16], work[:, 5, 0:16]))
                        inv = work[:, 6, 0:16]
                        nc.vector.tensor_tensor(coef[:, s, 32:48], ex[:, 32:48], inv, ALU.mult)
                        nc.vector.tensor_tensor(work[:, 7, 0:32].rearrange("p (a n) -> p a n", a=2),
                                                ex[:, 0:32].rearrange("p (a n) -> p a n", a=2),
                                                inv.unsqueeze(1).broadcast_to([P, 2, 16]), ALU.mult).then_inc(shifted, 1)
                        dve.wait_ge(shifted, 2 * p + 2)
                        nc.vector.tensor_tensor(moved_back[:, 0, :].rearrange("p (n a) -> p n a", a=8),
                                                work[:, 7, 0:16].unsqueeze(2).broadcast_to([P, 16, 8]),
                                                back16.unsqueeze(1).broadcast_to([P, 16, 8]), ALU.mult)
                        nc.vector.tensor_tensor(moved_back[:, 1:5, :].rearrange("p c (b a) -> p (c b) a", a=32),
                                                work[:, 7, 16:32].unsqueeze(2).broadcast_to([P, 16, 32]),
                                                back4.unsqueeze(1).broadcast_to([P, 16, 32]), ALU.mult).then_inc(spread_back, 1)
                    if k == 3:
                        dve.wait_ge(gathered_back, p + 1)
                        nc.vector.tensor_copy(coef[:, s, 0:32], ps_x[:, 64:96]).then_inc(coef_ready, 1)

                def second(phase, slot):
                    h, s = phase
                    p = number(phase)
                    for e in ([0, 1] if slot == 0 else [slot + 1]):
                        if e == NP:
                            continue
                        if e == 0:
                            dve.wait_ge(coef_ready, p + 1 + C1)
                        for j in range(2):
                            u = FLAT[s][2 * e + j]
                            place = probs[:, s, 2 * e + j, 2 * P - u.keys:]
                            last = nc.vector.tensor_scalar(place, place, coef[:, s, u.column:u.column + 1], None, ALU.mult)
                        last.then_inc(weighted, 1)
                    d = slot - 2
                    if last_of.get(d, -1) >= MERGED:
                        finish_bank(phase, d, last_of[d] - MERGED)

                def rest(phase, slot):
                    if slot == 1:
                        finish_bank(phase, NP - 1, NCH - 1)

                def finish_bank(phase, d, c):
                    h, s = phase
                    p = number(phase)
                    n = p * NCH + c
                    dve.wait_ge(values_done, p * NP + d + 1)
                    if not isinstance(n, int) or n >= 2:
                        dve.wait_ge(y_stored[c % 2], 16 * (p * 2 + c // 2))
                    dve.wait_ge(gate_loaded[s % GB], 16 * p + 16 if GB == 1 else 16 * h + 16)
                    out = ps_o[0:HD, (MERGED + c) % 2, :]
                    if kind == "B":
                        dve.wait_ge(kept, p * MERGED + MERGED)
                        nc.vector.tensor_tensor(y[:, c % 2, :].rearrange("p (j r) -> p j r", r=16),
                                                out.rearrange("p (j r) -> p j r", r=16),
                                                o16[:, :, 32 * c:32 * c + 32].rearrange("p r j -> p j r"),
                                                ALU.add).then_inc(bank_read, 1)
                        dve.wait_ge(bank_read, n + 1)
                        nc.vector.tensor_tensor(y[:, c % 2, :], y[:, c % 2, :], gate[:, s % GB, c * CHUNK:(c + 1) * CHUNK],
                                                ALU.mult).then_inc(y_ready, 1)
                    else:
                        nc.vector.tensor_tensor(y[:, c % 2, :], out, gate[:, s % GB, c * CHUNK:(c + 1) * CHUNK], ALU.mult).then_inc(bank_read, 1)
                rounds(dve, scores, second, rest, late=True)

            @block.scalar
            def _(act):
                act.wait_ge(consts, CONSTS)

                def scores(phase, slot):
                    h, s = phase
                    p = number(phase)
                    if slot >= NP:
                        if kind == "A" and slot == NP:
                            act.wait_ge(max_ready, p * NP + NP)
                            nc.scalar.activation(work[:, 0, :], stat[:, s, 0, :], ACT.Exp,
                                                 bias=sink_now[:, s, 0:1]).then_inc(exps_ready, 1)
                        if kind == "B" and slot == NP + 1:
                            act.wait_ge(shifted, 2 * p + 1)
                            nc.scalar.activation(work[:, 3, :], work[:, 2, :], ACT.Exp).then_inc(exps_ready, 1)
                        return
                    act.wait_ge(max_ready, p * NP + slot + 1)
                    for j in range(2):
                        u = FLAT[s][2 * slot + j]
                        place = probs[:, s, 2 * slot + j, 2 * P - u.keys:]
                        last = nc.scalar.activation(place, place, ACT.Exp, scale=-1.0,
                                                    bias=stat[:, s, 0, u.column:u.column + 1],
                                                    accum_out=stat[:, s, 1, u.column:u.column + 1])
                    last.then_inc(sums_ready, 1)

                def second(phase, slot):
                    h, s = phase
                    p = number(phase)
                    e = slot
                    act.wait_ge(turned, p * NP + e + 1)
                    ge(act, values_done, p * NP + e - 1)
                    a = [2 * P - FLAT[s][2 * e + j].keys for j in range(2)]
                    if a[0] == a[1]:
                        nc.scalar.activation(pT[:, e % 2, :, a[0]:], ps_t[:, e % 2, :, a[0]:],
                                             ACT.Copy).then_inc(turned_copied, 1)
                    else:
                        nc.scalar.activation(pT[:, e % 2, 0, a[0]:], ps_t[:, e % 2, 0, a[0]:], ACT.Copy)
                        nc.scalar.activation(pT[:, e % 2, 1, a[1]:], ps_t[:, e % 2, 1, a[1]:],
                                             ACT.Copy).then_inc(turned_copied, 1)
                    if 0 <= last_of.get(e - 2, -1) < MERGED:
                        keep(phase, e - 2, last_of[e - 2])

                def keep(phase, d, g):
                    p = number(phase)
                    act.wait_ge(values_done, p * NP + d + 1)
                    ge(act, y_ready, p * NCH)
                    nc.scalar.activation(o16[:, 4 * g:4 * g + 4, :].rearrange("p r j -> p (r j)"),
                                         ps_o[0:HD, g % 2, :], ACT.Copy).then_inc(kept, 1)
                rounds(act, scores, second, nothing, late=True)

            @block.gpsimd
            def _(pool):
                def store(h, s):
                    for c in range(NCH):
                        pool.wait_ge(done_sem, (h * 2 + s) * NCH + c + 1)
                        pool.nop(nofuse=True)
                        pool.dma_start(sc["y"][bass.ds(y_row + h * HD, HD),
                                               s * HALF + c * CHUNK:s * HALF + (c + 1) * CHUNK],
                                       y[:, c % 2, :]).then_inc(y_stored[c % 2], 16)
                with pool.Fori(0, heads) as h:
                    for s in range(2):
                        store(h, s)
                for b in range(2):
                    pool.wait_ge(y_stored[b], 16 * 2 * 2 * heads)


def finish_stage(nc, io, sc, out):
    with ExitStack() as ctx:
        sb = lambda n, s, d=F32: ctx.enter_context(nc.sbuf_tensor("f_" + n, s, d))
        sem = lambda n: ctx.enter_context(nc.semaphore("f_" + n))
        TW = 256
        NB = SEQ // TW
        w_raw = sb("w_raw", [P, 2, D])
        w_hi = sb("w_hi", [P, KD, D], F32R)
        w_lo = sb("w_lo", [P, KD, D], F32R)
        gain = sb("gain", [P, D])
        yT = sb("yT", [P, 2, KD, TW])
        y_hi = sb("y_hi", [P, 2, KD, TW], F32R)
        y_lo = sb("y_lo", [P, 2, KD, TW], F32R)
        xb = sb("xb", [P, 2, D])
        o = sb("o", [P, 2, D])
        junk = sb("junk", [P, D])
        ss = sb("ss", [P, 2, 4])
        ps = ctx.enter_context(nc.psum_tensor("f_ps", [P, 4, 2, CHUNK], F32))
        gain_loaded = sem("gain_loaded")
        w_loaded = [sem(f"w_loaded{b}") for b in range(2)]
        y_loaded = [sem(f"y_loaded{b}") for b in range(2)]
        x_loaded = [sem(f"x_loaded{b}") for b in range(2)]
        stored = [sem(f"stored{b}") for b in range(2)]
        w_hi_ready, w_lo_ready, y_hi_ready, y_lo_ready = sem("w_hi_ready"), sem("w_lo_ready"), sem("y_hi_ready"), sem("y_lo_ready")
        multiplied, squared, meaned, rooted = sem("multiplied"), sem("squared"), sem("meaned"), sem("rooted")
        inverted, normed, added = sem("inverted"), sem("normed"), sem("added")
        with nc.Block() as block:
            @block.sync
            def _(sp):
                def load_y(i, b):
                    for k in range(0, KD, 4):
                        sp.dma_start(yT[:, b, k:k + 4, :], sc["y"][k * P:(k + 4) * P, bass.ts(i, TW)].rearrange(
                            "(k p) n -> p k n", p=P)).then_inc(y_loaded[b], 16)

                def load_x(i, b):
                    sp.dma_start(xb[:, b, :], io["x"][bass.ts(i, P), :]).then_inc(x_loaded[b], 16)

                def store(i, b):
                    sp.wait_ge(added, i + 1)
                    sp.dma_start(out[bass.ts(i, P), :], o[:, b, :]).then_inc(stored[b], 16)
                sp.dma_start(gain[:], io["post_gain"].broadcast_to([P, D])).then_inc(gain_loaded, 16)
                load_y(0, 0)
                for k in range(KD):
                    if k >= 2:
                        sp.wait_ge(w_lo_ready, k - 1)
                    sp.dma_start(w_raw[:, k % 2, :], io["w_out"][k * P:(k + 1) * P, :]).then_inc(w_loaded[k % 2], 16)
                load_y(1, 1)
                load_x(0, 0)
                load_x(1, 1)
                with sp.Fori(0, NB // 2 - 1) as two:
                    i = 2 * two
                    for b in range(2):
                        for t in range(2):
                            store(2 * (i + b) + t, t)
                            load_x(2 * (i + b) + t + 2, t)
                        sp.wait_ge(y_lo_ready, i + b + 1)
                        load_y(i + b + 2, b)
                for t in range(4):
                    store(2 * NB - 4 + t, t % 2)
                    if t < 2:
                        load_x(2 * NB - 2 + t, t)
                for b in range(2):
                    sp.wait_ge(stored[b], 16 * NB)

            @block.scalar
            def _(act):
                def part(i, b):
                    act.wait_ge(y_loaded[b], 32 * ((i - b) // 2) + 32 if isinstance(i, int) else 16 * (i - b) + 32)
                    if not isinstance(i, int) or i >= 2:
                        act.wait_ge(multiplied, 2 * i - 2)
                    nc.scalar.activation(y_hi[:, b, :, :], yT[:, b, :, :], ACT.Copy).then_inc(y_hi_ready, 1)

                def square(i, b):
                    act.wait_ge(multiplied, i + 1)
                    nc.scalar.activation(junk[:], ps[:, b, :, :].rearrange("p a n -> p (a n)"), ACT.Square,
                                         accum_out=ss[:, b % 2, 0:1]).then_inc(squared, 1)
                    act.wait_ge(meaned, i + 1)
                    nc.scalar.activation(ss[:, b % 2, 2:3], ss[:, b % 2, 1:2], ACT.Sqrt).then_inc(rooted, 1)
                part(0, 0)
                for k in range(KD):
                    act.wait_ge(w_loaded[k % 2], 16 * (k // 2) + 16)
                    nc.scalar.activation(w_hi[:, k, :], w_raw[:, k % 2, :], ACT.Copy).then_inc(w_hi_ready, 1)
                part(1, 1)
                with act.Fori(0, NB // 2 - 1) as two:
                    i = 2 * two
                    for b in range(2):
                        for t in range(2):
                            square(2 * (i + b) + t, 2 * b + t)
                        part(i + b + 2, b)
                for t in range(4):
                    square(2 * NB - 4 + t, t)

            @block.vector
            def _(dve):
                dve.wait_ge(gain_loaded, 16)

                def part(i, b):
                    dve.wait_ge(y_hi_ready, i + 1)
                    nc.vector.tensor_tensor(y_lo[:, b, :, :], yT[:, b, :, :], y_hi[:, b, :, :].bitcast(F32),
                                            ALU.subtract).then_inc(y_lo_ready, 1)

                def norm(i, b):
                    dve.wait_ge(squared, i + 1)
                    nc.vector.tensor_scalar(ss[:, b % 2, 1:2], ss[:, b % 2, 0:1], 1.0 / D, EPS,
                                            ALU.mult, ALU.add).then_inc(meaned, 1)
                    dve.wait_ge(rooted, i + 1)
                    nc.vector.reciprocal(ss[:, b % 2, 3:4], ss[:, b % 2, 2:3]).then_inc(inverted, 1)
                    dve.wait_ge(inverted, i + 1)
                    if not isinstance(i, int) or i >= 2:
                        dve.wait_ge(stored[b % 2], 16 * ((i - b % 2) // 2) if isinstance(i, int) else 8 * (i - b % 2))
                    nc.vector.scalar_tensor_tensor(out=o[:, b % 2, :], in0=ps[:, b, :, :].rearrange("p a n -> p (a n)"),
                                                   scalar=ss[:, b % 2, 3:4], in1=gain[:],
                                                   op0=ALU.mult, op1=ALU.mult).then_inc(normed, 1)
                    dve.wait_ge(normed, i + 1)
                    dve.wait_ge(x_loaded[b % 2], 16 * ((i - b % 2) // 2) + 16 if isinstance(i, int)
                                else 8 * (i - b % 2) + 16)
                    nc.vector.tensor_tensor(o[:, b % 2, :], o[:, b % 2, :], xb[:, b % 2, :], ALU.add).then_inc(added, 1)
                part(0, 0)
                for k in range(KD):
                    dve.wait_ge(w_hi_ready, k + 1)
                    nc.vector.tensor_tensor(w_lo[:, k, :], w_raw[:, k % 2, :], w_hi[:, k, :].bitcast(F32),
                                            ALU.subtract).then_inc(w_lo_ready, 1)
                part(1, 1)
                for t in range(2):
                    norm(t, t)
                part(2, 0)
                for t in range(2):
                    norm(2 + t, 2 + t)
                part(3, 1)
                with dve.Fori(1, NB // 2 - 1) as two:
                    i = 2 * two
                    for b in range(2):
                        for t in range(2):
                            norm(2 * (i + b) + t, 2 * b + t)
                        part(i + b + 2, b)
                for t in range(4):
                    norm(2 * NB - 4 + t, t)

            @block.tensor
            def _(pe):
                def product(i, b):
                    pe.wait_ge(y_lo_ready, i + 1)
                    for t in range(2):
                        if not isinstance(i, int) or i >= 2:
                            pe.wait_ge(normed, 2 * i + t - 3)
                        for c in range(2):
                            for k in range(KD):
                                if isinstance(i, int) and i == 0 and t == 0 and c == 0:
                                    pe.wait_ge(w_lo_ready, k + 1)
                                y, cols = slice(t * P, (t + 1) * P), slice(c * CHUNK, (c + 1) * CHUNK)
                                last = split_product(nc, ps[:, 2 * b + t, c, :], y_hi[:, b, k, y], y_lo[:, b, k, y],
                                                     w_hi[:, k, cols], w_lo[:, k, cols], k == 0, k == KD - 1)
                        last.then_inc(multiplied, 1)
                product(0, 0)
                product(1, 1)
                with pe.Fori(1, NB // 2) as two:
                    i = 2 * two
                    for b in range(2):
                        product(i + b, b)


def build(nc, io, out):
    scratch = lambda n, s, d=F32: nc.dram_tensor("scratch_" + n, s, d, kind="Internal").ap()
    sc = {
        "qk_hi": scratch("qk_hi", [NQK * P, SEQ]), "qk_lo": scratch("qk_lo", [NQK * P, SEQ]),
        "v": scratch("v", [SEQ, len(V_TILES) * P]), "gate": scratch("gate", [D, SEQ]), "y": scratch("y", [D, SEQ]),
        "mk_hi": scratch("mk_hi", [256, NMEM]), "mk_lo": scratch("mk_lo", [256, NMEM]),
        "mv": scratch("mv", [NMEM, 256]),
    }
    project_stage(nc, io, sc)
    for kind in "BAC":
        attend_stage(nc, io, sc, kind)
    finish_stage(nc, io, sc, out)


def constants():
    import numpy as np
    rot = HD // 4
    inv = (np.float32(500000.0) ** (-np.arange(0, rot, 2, dtype=np.float32) / np.float32(rot))).astype(np.float32)
    ang = (np.arange(SEQ, dtype=np.float32)[None, :] * inv[:, None]).astype(np.float32)
    c, s = np.cos(ang).astype(np.float32), np.sin(ang).astype(np.float32)
    cos, sin = np.ones((P, SEQ), np.float32), np.zeros((P, SEQ), np.float32)
    for h in (0, HD):
        cos[h:h + 8], cos[h + 8:h + 16] = c, c
        sin[h:h + 8], sin[h + 8:h + 16] = -s, s
    q, k = np.arange(P)[:, None], np.arange(P)[None, :]
    diag = np.where(k <= q, 0.0, NEG)
    mask_a = np.concatenate([np.where(k > q, 0.0, NEG), diag], 1).astype(np.float32)
    mask_b = np.concatenate([np.where(k >= q, 0.0, NEG), diag], 1).astype(np.float32)
    j = np.arange(P)[:, None]
    n = lambda m: np.arange(m)[None, :]
    sel = np.concatenate([
        j % 8 == n(P) // 16,
        j % 32 == n(P) // 4,
        j // 16 == n(8), j // 4 == n(32),
        j // 8 == n(16), j // 32 == n(4), j % 16 == n(16), j % 4 == n(4),
    ], 1).astype(np.float32)
    return {"cos": cos, "sin": sin, "maskA": mask_a, "maskB": mask_b, "maskC": np.zeros((P, 2 * P), np.float32),
            "sel": sel, "ident": np.eye(P, dtype=np.float32)}


def kernel(x, mem, pre_norm, w_in, sink_a, mem_norm, w_mem_kv, w_out, post_norm):
    import numpy as np
    import concourse.bacc as bacc
    from concourse.bass_utils import run_bass_kernel_spmd

    nc = bacc.Bacc("TRN2", target_bir_lowering=False, num_devices=1)
    w = np.asarray(w_in)[0].reshape(KD, P, NT, P).transpose(2, 1, 0, 3)[np.array(ORDER)]
    given = {
        "x": np.asarray(x)[0], "mem": np.asarray(mem)[0], "pre_gain": np.asarray(pre_norm), "w_in": w.reshape(NT, P, D),
        "sink": np.asarray(sink_a), "mem_gain": np.asarray(mem_norm), "w_mem": np.asarray(w_mem_kv)[0],
        "w_out": np.asarray(w_out)[0], "post_gain": np.asarray(post_norm), **constants(),
    }
    arrays = {f"in_{n}": np.ascontiguousarray(a) for n, a in given.items()}
    io = {n: nc.dram_tensor(f"in_{n}", a.shape, F32, kind="ExternalInput").ap() for n, a in given.items()}
    out = nc.dram_tensor("out_0", [SEQ, D], F32, kind="ExternalOutput").ap()
    build(nc, io, out)
    r = run_bass_kernel_spmd(nc, [arrays], core_ids=[0])
    return r.results[0]["out_0"].reshape(1, SEQ, D)
```

```python
from collections import namedtuple
from contextlib import ExitStack

import concourse.bass as bass
from concourse import mybir

F32 = mybir.dt.float32
F32R = mybir.dt.float32r
ALU = mybir.AluOpType
ACT = mybir.ActivationFunctionType

P = 128
D = 1024
KD = D // P
SEQ = 4096
NMEM = 256
HD = 64
CHUNK = 512
HALF = SEQ // 2
NCH = HALF // CHUNK
SCALE = HD ** -0.5
NEG = -1e30
EPS = 1e-6
ROPE_TILES = [0, 1, 2, 3, 8, 9, 10, 11, 12, 13]
PLAIN_TILES = [20, 21]
V_TILES = [4, 14, 15, 16]
GATE_TILES = [5, 6, 7, 17, 18, 19, 22, 23]
ORDER = ROPE_TILES + PLAIN_TILES + V_TILES + GATE_TILES
NT = len(ORDER)
NQK = len(ROPE_TILES) + len(PLAIN_TILES)
QA, KA, QB, KB, QC = 0, 384, 512, 896, 1280
B_UNITS = 48
SWAP = [8, 9, 10, 11, 12, 13, 14, 15, 0, 1, 2, 3, 4, 5, 6, 7] + list(range(16, 32))


def split_product(nc, out, w_hi, w_lo, m_hi, m_lo, first, last):
    nc.tensor.matmul(out, w_hi, m_hi, start=first, stop=False)
    nc.tensor.matmul(out, w_hi, m_lo, start=False, stop=False)
    return nc.tensor.matmul(out, w_lo, m_hi, start=False, stop=last)


def project_stage(nc, io, sc, early):
    with ExitStack() as ctx:
        sb = lambda n, s, d=F32: ctx.enter_context(nc.sbuf_tensor("p_" + n, s, d))
        sem = lambda n: ctx.enter_context(nc.semaphore("p_" + n))
        QT = SEQ // 4
        NCH = QT // CHUNK
        XT = QT // P
        MT = NMEM // P
        with ExitStack() as given_back:
            tmp = lambda n, s, d=F32: given_back.enter_context(nc.sbuf_tensor("m_" + n, s, d))
            mem = tmp("mem", [P, MT, D])
            um = tmp("um", [P, MT, D])
            umT = tmp("umT", [P, KD, NMEM])
            mem_gain = tmp("gain", [P, D])
            w_mem = tmp("w", [P, KD, 512])
            mk_hi = tmp("k_hi", [P, 2, NMEM], F32R)
            mk_lo = tmp("k_lo", [P, 2, NMEM], F32R)
            mem_v = tmp("v", [P, MT, 256])
        uT_hi, uT_lo = {}, {}
        for half in (1, 0):
            uT_hi[half] = sb(f"uT_hi{half}", [P, KD, QT], F32R)
            uT_lo[half] = sb(f"uT_lo{half}", [P, KD, QT], F32R)
            if half:
                w_hi = sb("w_hi", [P, 2, KD, P], F32R)
                w_lo = sb("w_lo", [P, 2, KD, P], F32R)
                w_raw = sb("w_raw", [P, 2, D])
                xb = sb("x", [P, 2, D])
        ub = sb("u", [P, 2, D])
        gain = sb("gain", [P, D])
        ident = sb("ident", [P, P])
        ss = sb("ss", [P, 2, 4])
        cos = sb("cos", [P, QT])
        sin = sb("sin", [P, QT])
        turned = sb("turned", [P, CHUNK])
        rot = sb("rot", [P, 2, CHUNK])
        o_hi = sb("o_hi", [P, 2, CHUNK], F32R)
        o_lo = sb("o_lo", [P, 2, CHUNK], F32R)
        vT = sb("vT", [P, 2, CHUNK])
        o_v = sb("o_v", [P, 2, CHUNK])
        o_g = rot
        ps = ctx.enter_context(nc.psum_tensor("p_ps", [P, 4, CHUNK], F32))
        ps_t = ctx.enter_context(nc.psum_tensor("p_ps_t", [P, 2, 2, CHUNK], F32))
        m_ss = sb("m_ss", [P, 3 * MT])
        m_loaded, m_weights, m_squared, m_meaned = sem("m_loaded"), sem("m_weights"), sem("m_squared"), sem("m_meaned")
        m_rooted, m_inverted, m_scaled, m_turned = sem("m_rooted"), sem("m_inverted"), sem("m_scaled"), sem("m_turned")
        m_copied, m_multiplied, m_hi_ready, m_lo_ready = (sem("m_copied"), sem("m_multiplied"), sem("m_hi_ready"),
                                                          sem("m_lo_ready"))
        m_v_ready, m_stored = sem("m_v_ready"), sem("m_stored")
        consts, table = sem("consts"), sem("table")
        x_loaded = [sem(f"x_loaded{b}") for b in range(2)]
        squared, meaned, rooted, inverted = sem("squared"), sem("meaned"), sem("rooted"), sem("inverted")
        u_ready, u_turned, uT_hi_ready, uT_lo_ready = sem("u_ready"), sem("u_turned"), sem("uT_hi_ready"), sem("uT_lo_ready")
        w_loaded = [sem(f"w_loaded{b}") for b in range(2)]
        w_hi_ready, w_lo_ready = sem("w_hi_ready"), sem("w_lo_ready")
        multiplied = sem("multiplied")
        chain, straight = sem("chain"), sem("straight")
        rotated, hi_ready = sem("rotated"), sem("hi_ready")
        out_ready = sem("out_ready")
        vT_ready, v_turned = sem("vT_ready"), sem("v_turned")
        qk_stored, v_stored, g_stored = ([sem(f"{n}_stored{b}") for b in range(2)] for n in ("qk", "v", "g"))

        NR, NQ, NV, NG = len(ROPE_TILES), NQK, len(V_TILES), len(GATE_TILES)
        GATES = NQ + NV
        assert NG == XT and QT % (2 * P) == 0

        def pairs(eng, quarter, lo, hi, body, peel=False):
            end = hi - 2 if peel else hi
            if quarter == 0 and lo in (0, NQ) and end - lo > 2:
                for b in range(2):
                    body(lo + b, b, False)
                lo += 2
            if end - lo > 2:
                with eng.Fori(lo // 2, end // 2) as two:
                    i = 2 * two
                    for b in range(2):
                        body(i + b, b, False)
            elif end > lo:
                for b in range(2):
                    body(lo + b, b, False)
            if peel:
                for b in range(2):
                    body(end + b, b, end + b == hi - 1)

        def wait_stored(eng, sems, n, c):
            if not isinstance(n, int) or n >= 1:
                eng.wait_ge(sems[c], (32 if sems is qk_stored else 16) * n)

        with nc.Block() as block:
            @block.sync
            def _(sp):
                def load_x(quarter, t, b):
                    n = quarter * XT + t
                    if not isinstance(n, int) or n >= 2:
                        sp.wait_ge(u_ready, n - 1)
                    sp.dma_start(xb[:, b, :], io["x"][bass.ts(n, P), :]).then_inc(x_loaded[b], 16)

                def load_w(i, b):
                    sp.dma_start(w_raw[:, b, :], io["w_in"][i, :, :]).then_inc(w_loaded[b], 16)

                def load_tables(quarter):
                    for t, d in ((cos, "cos"), (sin, "sin")):
                        sp.dma_start(t[:], io[d][:, quarter * QT:(quarter + 1) * QT]).then_inc(table, 16)

                load_x(0, 0, 0)
                sp.dma_start(gain[:], io["pre_gain"].broadcast_to([P, D])).then_inc(consts, 16)
                sp.dma_start(ident[:], io["ident"]).then_inc(consts, 16)
                load_x(0, 1, 1)
                load_w(0, 0)
                sp.dma_start(mem[:], io["mem"].rearrange("(t p) d -> p t d", p=P)).then_inc(m_loaded, 16)
                sp.dma_start(mem_gain[:], io["mem_gain"].broadcast_to([P, D])).then_inc(m_loaded, 16)
                for t in range(2, XT):
                    load_x(0, t, t % 2)
                    if t == 3:
                        sp.dma_start(w_mem[:], io["w_mem"].rearrange("(k p) n -> p k n", p=P)).then_inc(m_weights, 16)
                load_w(1, 1)
                load_tables(0)
                sp.wait_ge(m_hi_ready, 1)
                sp.wait_ge(m_lo_ready, 1)
                sp.dma_start(sc["mk_hi"].rearrange("(t p) n -> p t n", p=P), mk_hi[:].bitcast(F32)).then_inc(m_stored, 16)
                sp.dma_start(sc["mk_lo"].rearrange("(t p) n -> p t n", p=P), mk_lo[:].bitcast(F32)).then_inc(m_stored, 16)
                sp.wait_ge(m_v_ready, 1)
                sp.dma_start(sc["mv"].rearrange("(t p) n -> p t n", p=P), mem_v[:]).then_inc(m_stored, 16)

                for quarter in range(4):
                    C0 = quarter * NT * NCH

                    def next_w(i, b):
                        if isinstance(i, int) and i + 2 >= NT and quarter == 3:
                            return
                        sp.wait_ge(w_lo_ready, quarter * NT + i + 1)
                        load_w(i + 2 - NT if isinstance(i, int) and i + 2 >= NT else i + 2, b)

                    def store_qk(i, b, last):
                        next_w(i, b)
                        for c in range(NCH):
                            sp.wait_ge(out_ready, C0 + i * NCH + c + 1)
                            at = (quarter * NCH + c) * CHUNK
                            for src, dst in ((o_hi, sc["qk_hi"]), (o_lo, sc["qk_lo"])):
                                sp.dma_start(dst[bass.ts(i, P), at:at + CHUNK],
                                             src[:, c, :].bitcast(F32)).then_inc(qk_stored[c], 16)

                    def store_v(i, b, last):
                        next_w(i, b)
                        for c in range(NCH):
                            sp.wait_ge(out_ready, C0 + i * NCH + c + 1)
                            at = (quarter * NCH + c) * CHUNK
                            dst = sc["v"][at:at + CHUNK, bass.ts(i - NQ, P)].rearrange("(t p) n -> p t n", p=P)
                            sp.dma_start(dst, o_v[:, c, :].rearrange("p (t n) -> p t n", n=P)).then_inc(v_stored[c], 16)

                    def store_g(i, b, last):
                        next_w(i, b)
                        for c in range(NCH):
                            sp.wait_ge(out_ready, C0 + i * NCH + c + 1)
                            at = (quarter * NCH + c) * CHUNK
                            sp.dma_start(sc["gate"][bass.ts(i - GATES, P), at:at + CHUNK],
                                         o_g[:, c, :]).then_inc(g_stored[c], 16)
                        if quarter < 3 and not (isinstance(i, int) and i + 2 >= NT):
                            load_x(quarter + 1, i - GATES + 2, b)

                    pairs(sp, quarter, 0, NR, store_qk)
                    if quarter < 3:
                        load_tables(quarter + 1)
                    pairs(sp, quarter, NR, NQ, store_qk)
                    if quarter < 3:
                        load_x(quarter + 1, 0, 0)
                        load_x(quarter + 1, 1, 1)
                    pairs(sp, quarter, NQ, GATES, store_v)
                    pairs(sp, quarter, GATES, NT, store_g, peel=True)
                sp.wait_ge(m_stored, 48)
                for b in range(2):
                    sp.wait_ge(qk_stored[b], 32 * NQ * 4)
                    sp.wait_ge(v_stored[b], 16 * NV * 4)
                    sp.wait_ge(g_stored[b], 16 * NG * 4)

            @block.scalar
            def _(act):
                def square(quarter, t, b):
                    n = quarter * XT + t
                    act.wait_ge(x_loaded[b], quarter * 8 * XT + (t - b) * 8 + 16)
                    if not isinstance(n, int) or n >= 2:
                        act.wait_ge(u_turned, n - 1)
                    nc.scalar.activation(ub[:, b, :], xb[:, b, :], ACT.Square,
                                         accum_out=ss[:, b, 0:1]).then_inc(squared, 1)
                    act.wait_ge(meaned, n + 1)
                    nc.scalar.activation(ss[:, b, 2:3], ss[:, b, 1:2], ACT.Sqrt).then_inc(rooted, 1)

                def part(quarter, t, b):
                    act.wait_ge(u_turned, quarter * XT + t + 1)
                    nc.scalar.activation(uT_hi[quarter % 2][:, :, bass.ts(t, P)],
                                         ps_t[:, b, :, :].rearrange("p a (k n) -> p (a k) n", n=P),
                                         ACT.Copy).then_inc(uT_hi_ready, 1)

                def w_part(quarter, i, b):
                    act.wait_ge(w_loaded[b], 16 * quarter * (NT // 2) + (i - b) * 8 + 16)
                    if quarter or not isinstance(i, int) or i >= 2:
                        act.wait_ge(multiplied, quarter * NT * NCH + (i - 1) * NCH)
                    nc.scalar.activation(w_hi[:, b, :, :].rearrange("p k n -> p (k n)"), w_raw[:, b, :],
                                         ACT.Copy).then_inc(w_hi_ready, 1)

                square(0, 0, 0)
                w_part(0, 0, 0)
                square(0, 1, 1)
                for t in range(2, XT):
                    part(0, t - 2, t % 2)
                    square(0, t, t % 2)
                    if t == 4:
                        act.wait_ge(m_loaded, 32)
                        for m in range(MT):
                            nc.scalar.activation(um[:, m, :], mem[:, m, :], ACT.Square,
                                                 accum_out=m_ss[:, m:m + 1]).then_inc(m_squared, 1)
                        act.wait_ge(m_meaned, 1)
                        nc.scalar.activation(m_ss[:, 4:6], m_ss[:, 2:4], ACT.Sqrt).then_inc(m_rooted, 1)
                part(0, XT - 2, 0)
                part(0, XT - 1, 1)
                act.wait_ge(m_multiplied, 1)
                nc.scalar.activation(mk_hi[:], ps[:, 0:2, 0:NMEM], ACT.Copy).then_inc(m_hi_ready, 1)
                act.wait_ge(m_multiplied, 2)
                nc.scalar.activation(mem_v[:], ps[:, 2:4, 0:256], ACT.Copy).then_inc(m_v_ready, 1)

                for quarter in range(4):
                    C0 = quarter * NT * NCH

                    def next_w(i, b):
                        if isinstance(i, int) and i + 1 == NT:
                            if quarter < 3:
                                w_part(quarter + 1, 0, 0)
                        else:
                            w_part(quarter, i + 1, 1 - b)

                    def rope(i, b, last):
                        next_w(i, b)
                        for c in range(NCH):
                            act.wait_ge(rotated, quarter * NR * NCH + i * NCH + c + 1)
                            wait_stored(act, qk_stored, quarter * NQ + i, c)
                            nc.scalar.activation(o_hi[:, c, :], rot[:, c, :], ACT.Copy).then_inc(hi_ready, 1)

                    def plain(i, b, last):
                        next_w(i, b)
                        for c in range(NCH):
                            act.wait_ge(multiplied, C0 + i * NCH + c + 1)
                            wait_stored(act, qk_stored, quarter * NQ + i, c)
                            nc.scalar.activation(o_hi[:, c, :], ps[:, 2 * b + c, :], ACT.Copy).then_inc(hi_ready, 1)

                    def values(i, b, last):
                        next_w(i, b)
                        for c in range(NCH + 1):
                            if c < NCH:
                                act.wait_ge(multiplied, C0 + i * NCH + c + 1)
                                n = quarter * NV * NCH + (i - NQ) * NCH + c
                                if not isinstance(n, int) or n >= 2:
                                    act.wait_ge(v_turned, n - 1)
                                nc.scalar.activation(vT[:, c, :], ps[:, 2 * b + c, :], ACT.Copy).then_inc(vT_ready, 1)
                            if c > 0:
                                act.wait_ge(v_turned, quarter * NV * NCH + (i - NQ) * NCH + c)
                                wait_stored(act, v_stored, quarter * NV + i - NQ, c - 1)
                                nc.scalar.activation(o_v[:, c - 1, :], ps_t[:, c - 1, 0, :],
                                                     ACT.Copy).then_inc(out_ready, 1)

                    def gates(i, b, last):
                        next_w(i, b)
                        if quarter < 3:
                            square(quarter + 1, i - GATES, b)
                        for c in range(NCH):
                            act.wait_ge(multiplied, C0 + i * NCH + c + 1)
                            wait_stored(act, g_stored, quarter * NG + i - GATES, c)
                            nc.scalar.activation(o_g[:, c, :], ps[:, 2 * b + c, :], ACT.Silu).then_inc(out_ready, 1)
                            if c == 0 and quarter < 3:
                                if quarter == 0:
                                    act.wait_ge(m_stored, 48)
                                part(quarter + 1, i - GATES, b)

                    pairs(act, quarter, 0, NR, rope)
                    pairs(act, quarter, NR, NQ, plain)
                    act.wait_ge(out_ready, C0 + NQ * NCH)
                    pairs(act, quarter, NQ, GATES, values)
                    pairs(act, quarter, GATES, NT, gates, peel=True)

            @block.vector
            def _(dve):
                def normalise(quarter, t, b):
                    n = quarter * XT + t
                    dve.wait_ge(squared, n + 1)
                    nc.vector.tensor_scalar(ss[:, b, 1:2], ss[:, b, 0:1], 1.0 / D, EPS,
                                            ALU.mult, ALU.add).then_inc(meaned, 1)
                    dve.wait_ge(rooted, n + 1)
                    nc.vector.reciprocal(ss[:, b, 3:4], ss[:, b, 2:3]).then_inc(inverted, 1)
                    dve.wait_ge(inverted, n + 1)
                    nc.vector.scalar_tensor_tensor(out=ub[:, b, :], in0=xb[:, b, :], scalar=ss[:, b, 3:4],
                                                   in1=gain[:], op0=ALU.mult, op1=ALU.mult).then_inc(u_ready, 1)

                def part(quarter, t, b):
                    dve.wait_ge(uT_hi_ready, quarter * XT + t + 1)
                    place = (slice(None), slice(None), bass.ts(t, P))
                    nc.vector.tensor_tensor(uT_lo[quarter % 2][place],
                                            ps_t[:, b, :, :].rearrange("p a (k n) -> p (a k) n", n=P),
                                            uT_hi[quarter % 2][place].bitcast(F32), ALU.subtract).then_inc(uT_lo_ready, 1)

                def w_part(quarter, i, b):
                    dve.wait_ge(w_hi_ready, quarter * NT + i + 1)
                    nc.vector.tensor_tensor(w_lo[:, b, :, :].rearrange("p k n -> p (k n)"), w_raw[:, b, :],
                                            w_hi[:, b, :, :].rearrange("p k n -> p (k n)").bitcast(F32),
                                            ALU.subtract).then_inc(w_lo_ready, 1)

                dve.wait_ge(consts, 32)
                normalise(0, 0, 0)
                w_part(0, 0, 0)
                normalise(0, 1, 1)
                for t in range(2, XT):
                    part(0, t - 2, t % 2)
                    normalise(0, t, t % 2)
                    if t == 4:
                        dve.wait_ge(m_squared, MT)
                        nc.vector.tensor_scalar(m_ss[:, 2:4], m_ss[:, 0:2], 1.0 / D, EPS, ALU.mult, ALU.add).then_inc(m_meaned, 1)
                        dve.wait_ge(m_rooted, 1)
                        nc.vector.reciprocal(m_ss[:, 0:2], m_ss[:, 4:6]).then_inc(m_inverted, 1)
                        dve.wait_ge(m_inverted, 1)
                        for m in range(MT):
                            nc.vector.scalar_tensor_tensor(out=um[:, m, :], in0=mem[:, m, :], scalar=m_ss[:, m:m + 1],
                                                           in1=mem_gain[:], op0=ALU.mult, op1=ALU.mult).then_inc(m_scaled, 1)
                dve.wait_ge(m_turned, 1)
                nc.vector.tensor_copy(umT[:].rearrange("p (b k) n -> p b (k n)", b=4), ps[:]).then_inc(m_copied, 1)
                part(0, XT - 2, 0)
                part(0, XT - 1, 1)
                dve.wait_ge(m_hi_ready, 1)
                nc.vector.tensor_tensor(mk_lo[:], ps[:, 0:2, 0:NMEM], mk_hi[:].bitcast(F32), ALU.subtract).then_inc(m_lo_ready, 1)

                for quarter in range(4):
                    C0 = quarter * NT * NCH

                    def next_w(i, b):
                        if isinstance(i, int) and i + 1 == NT:
                            if quarter < 3:
                                w_part(quarter + 1, 0, 0)
                        else:
                            w_part(quarter, i + 1, 1 - b)

                    def low(i, c, src):
                        dve.wait_ge(hi_ready, quarter * NQ * NCH + i * NCH + c + 1)
                        nc.vector.tensor_tensor(o_lo[:, c, :], src, o_hi[:, c, :].bitcast(F32),
                                                ALU.subtract).then_inc(out_ready, 1)

                    def rope(i, b, last):
                        next_w(i, b)
                        for c in range(NCH):
                            cols = slice(c * CHUNK, (c + 1) * CHUNK)
                            bank = ps[:, 2 * b + c, :]
                            n = quarter * NR * NCH + i * NCH + c
                            dve.wait_ge(multiplied, C0 + i * NCH + c + 1)
                            if not isinstance(n, int) or n >= 1:
                                dve.wait_ge(rotated, n)
                            if not isinstance(n, int) or n >= 2:
                                dve.wait_ge(out_ready, C0 + i * NCH + c - 1)
                            dve.nop(nofuse=True)
                            nc.vector.stream_shuffle(turned[:], bank, SWAP).then_inc(chain, 1)
                            nc.vector.tensor_tensor(rot[:, c, :], bank, cos[:, cols], ALU.mult).then_inc(straight, 1)
                            dve.wait_ge(chain, 2 * n + 1)
                            nc.vector.tensor_tensor(turned[:], turned[:], sin[:, cols], ALU.mult).then_inc(chain, 1)
                            dve.wait_ge(chain, 2 * n + 2)
                            dve.wait_ge(straight, n + 1)
                            nc.vector.tensor_tensor(rot[:, c, :], rot[:, c, :], turned[:], ALU.add).then_inc(rotated, 1)
                            low(i, c, rot[:, c, :])

                    def plain(i, b, last):
                        next_w(i, b)
                        for c in range(NCH):
                            dve.wait_ge(multiplied, C0 + i * NCH + c + 1)
                            low(i, c, ps[:, 2 * b + c, :])

                    def values(i, b, last):
                        next_w(i, b)

                    def gates(i, b, last):
                        next_w(i, b)
                        if quarter < 3:
                            normalise(quarter + 1, i - GATES, b)
                            if quarter == 0:
                                dve.wait_ge(m_stored, 48)
                            part(quarter + 1, i - GATES, b)

                    dve.wait_ge(table, 32 * (quarter + 1))
                    if quarter:
                        for c in range(NCH):
                            dve.wait_ge(g_stored[c], 16 * NG * quarter)
                    pairs(dve, quarter, 0, NR, rope)
                    pairs(dve, quarter, NR, NQ, plain)
                    pairs(dve, quarter, NQ, GATES, values)
                    pairs(dve, quarter, GATES, NT, gates, peel=True)

            @block.tensor
            def _(pe):
                pe.wait_ge(consts, 32)

                def turn(quarter, t, b):
                    n = quarter * XT + t
                    pe.wait_ge(u_ready, n + 1)
                    if not isinstance(n, int) or n >= 2:
                        pe.wait_ge(uT_lo_ready, n - 1)
                    for k in range(KD):
                        last = nc.tensor.transpose(ps_t[:, b, k // 4, (k % 4) * P:(k % 4 + 1) * P],
                                                   ub[:, b, k * P:(k + 1) * P], ident[:])
                    last.then_inc(u_turned, 1)

                for t in range(XT):
                    turn(0, t, t % 2)
                    if t == XT - 3:
                        pe.wait_ge(m_scaled, MT)
                        for k in range(KD):
                            for m in range(MT):
                                at = (k % 2) * NMEM + m * P
                                last = nc.tensor.transpose(ps[:, k // 2, at:at + P], um[:, m, k * P:(k + 1) * P], ident[:])
                        last.then_inc(m_turned, 1)
                pe.wait_ge(m_weights, 16)
                pe.wait_ge(m_copied, 1)
                for c in range(2):
                    for k in range(KD):
                        last = nc.tensor.matmul(ps[:, c, 0:NMEM], w_mem[:, k, c * P:(c + 1) * P], umT[:, k, :],
                                                start=k == 0, stop=k == KD - 1)
                last.then_inc(m_multiplied, 1)
                for m in range(MT):
                    for k in range(KD):
                        last = nc.tensor.matmul(ps[:, 2 + m, 0:256], umT[:, k, m * P:(m + 1) * P], w_mem[:, k, 256:512],
                                                start=k == 0, stop=k == KD - 1)
                last.then_inc(m_multiplied, 1)

                for quarter in range(4):
                    C0 = quarter * NT * NCH
                    half = quarter % 2
                    pe.wait_ge(uT_lo_ready, (quarter + 1) * XT)

                    def product(i, b, c):
                        n = C0 + i * NCH + c
                        if not isinstance(n, int) or n >= 4:
                            pe.wait_ge(out_ready, n - 3)
                        elif n == 0:
                            pe.wait_ge(m_lo_ready, 1)
                        elif n == 2:
                            pe.wait_ge(m_v_ready, 1)
                        cols = slice(c * CHUNK, (c + 1) * CHUNK)
                        for k in range(KD):
                            last = split_product(nc, ps[:, 2 * b + c, :], w_hi[:, b, k, :], w_lo[:, b, k, :],
                                                 uT_hi[half][:, k, cols], uT_lo[half][:, k, cols],
                                                 k == 0, k == KD - 1)
                        last.then_inc(multiplied, 1)

                    def tile(i, b, last):
                        pe.wait_ge(w_lo_ready, quarter * NT + i + 1)
                        for c in range(NCH):
                            product(i, b, c)

                    def turn_v(i, c):
                        n = quarter * NV * NCH + (i - NQ) * NCH + c
                        pe.wait_ge(vT_ready, n + 1)
                        if not isinstance(n, int) or n >= 2:
                            pe.wait_ge(out_ready, C0 + i * NCH + c - 1)
                        for t in range(CHUNK // P):
                            last = nc.tensor.transpose(ps_t[:, c, 0, t * P:(t + 1) * P],
                                                       vT[:, c, t * P:(t + 1) * P], ident[:])
                        last.then_inc(v_turned, 1)

                    def tile_v(i, b, last):
                        pe.wait_ge(w_lo_ready, quarter * NT + i + 1)
                        for c in range(NCH):
                            product(i, b, c)
                            if c:
                                turn_v(i, c - 1)
                        turn_v(i, NCH - 1)

                    def tile_g(i, b, last):
                        pe.wait_ge(w_lo_ready, quarter * NT + i + 1)
                        product(i, b, 0)
                        if quarter < 3:
                            pe.wait_ge(out_ready, C0 + i * NCH)
                            turn(quarter + 1, i - GATES, b)
                        product(i, b, 1)

                    pairs(pe, quarter, 0, NQ, tile)
                    pairs(pe, quarter, NQ, GATES, tile_v)
                    pairs(pe, quarter, GATES, NT, tile_g, peel=True)

            @block.gpsimd
            def _(pool):
                for b in range(2):
                    pool.wait_ge(qk_stored[b], 32 * NQ * 4)
                rows, n = {"q": bass.ds(QB, HD), "k": bass.ds(KB, HD)}, 0
                for s in range(2):
                    cols = slice(s * HALF, (s + 1) * HALF)
                    for part, of, place, sem_ in (
                            ("qk_hi", "q", early.q[0:HD, s, :], early.q_loaded), ("qk_lo", "q", early.q[HD:P, s, :], early.q_loaded),
                            ("qk_hi", "k", early.k_hi[0:HD, cols], early.k_loaded), ("qk_hi", "k", early.k_hi[HD:P, cols], early.k_loaded),
                            ("qk_lo", "k", early.k_lo[0:HD, cols], early.k_loaded), ("qk_lo", "k", early.k_lo[HD:P, cols], early.k_loaded)):
                        pool.wait_ge(multiplied, (3 * NT + GATES) * NCH + n)
                        n += 1
                        pool.dma_start(place.bitcast(F32), sc[part][rows[of], cols]).then_inc(sem_[s], 16)


def named(**things):
    return namedtuple("Named", list(things))(**things)


class Unit:

    def __init__(self, q, k, keys, tiles, out, column):
        self.q, self.k, self.keys = q, k, keys
        self.tiles, self.out, self.column = tiles, out, column


def units_of(kind, s):
    groups = []
    if kind == "B":
        for g in range(4):
            groups.append([Unit((r, 16), (r, 16), 256 if s else 128, [("v16", 0, r), ("v16", 1, r)][0 if s else 0:2 if s else 1],
                                ((r % 4) * P, 1), r) for r in range(4 * g, 4 * g + 4)])
    for c in range(NCH):
        group = []
        if kind == "B":
            for r in range(4):
                n = NCH * s + c
                tiles = [("v4", m // NCH, (m % NCH) * 4 + r) for m in (n - 1, n) if m >= 0]
                group.append(Unit((CHUNK * c + r, 4), (CHUNK * max(n - 1, 0) + r, 4), P * len(tiles), tiles,
                                  (r, 4), 16 + 4 * c + r))
        for b in range(4 * c, 4 * c + 4):
            n = 16 * s + b
            if kind == "C":
                tiles, k = [("v1", s, 0), ("v1", s, 1)], NMEM * s
            else:
                tiles, k = [("v1", m // 16, m % 16) for m in (n - 1, n) if m >= 0], P * max(n - 1, 0)
            group.append(Unit((P * b, 1), (k, 1), P * len(tiles), tiles, ((b % 4) * P, 1),
                              (32 if kind == "B" else 0) + b))
        groups.append(group)
    return groups


def strided(start, n, step):
    return slice(start, start + (n - 1) * step + 1, step)


def head_group(nc, io, sc, kind, buf, ctx, prev):
    heads = {"A": 6, "B": 6, "C": 4}[kind]
    q_row = {"A": QA, "B": QB, "C": QC}[kind]
    y_row = {"A": 0, "B": 384, "C": 768}[kind]
    PLANS = [units_of(kind, s) for s in range(2)]
    FLAT = [[u for g in plan for u in g] for plan in PLANS]
    NU = len(FLAT[0])
    NP = NU // 2
    NG = len(PLANS[0])
    EARLY = 12 if kind == "B" else 1
    GB = 1 if kind == "B" else 2
    NS = 3 if kind == "B" else 4
    STEPS = 4 if kind == "B" else 2
    if kind == "B":
        SLOTS = list(range(8)) + [8 + v * 11 // 16 for v in range(16)]
    else:
        SLOTS = [v * (NP - STEPS) // NP for v in range(NP)]
    NKEY = 2 * NMEM if kind == "C" else SEQ
    kinds_v = {"A": ["v1"], "B": ["v16", "v4", "v1"], "C": ["v1"]}[kind]
    last_of = {}
    first_of = {}
    bank_of = []
    at = 0
    for g, group in enumerate(PLANS[0]):
        first_of[at] = g
        bank_of += [g] * len(group)
        at += len(group)
        last_of[at // 2 - 1] = g
    MERGED = NG - NCH

    def ge(eng, sem, value):
        if not isinstance(value, int) or value > 0:
            eng.wait_ge(sem, value)

    sem = lambda n: ctx.enter_context(nc.semaphore(kind + "_" + n))
    q, k_hi, k_lo, v, pT, ident, y = buf.q, buf.k_hi, buf.k_lo, buf.v, buf.pT, buf.ident, buf.y
    probs, stat, coef, work = (buf.probs[:, :, 0:NU, :], buf.stat[:, :, :, 0:NU], buf.coef[:, :, 0:NU],
                               buf.work[:, :, 0:NU])
    mask, sink, sink_now, sel, moved, o16 = buf.masks[kind], buf.sink, buf.sink_now, buf.sel, buf.moved, buf.o16
    gate = [buf.gate[:], buf.v["v4"][0:HD].rearrange("p a t n -> p (a t n)")]
    sel16, sel4 = sel[:, 0:P], sel[:, P:2 * P]
    back16, back4 = sel[:, 256:264], sel[:, 264:296]
    col16, col4 = sel[:, 296:312], sel[:, 312:316]
    bcol16, bcol4 = sel[:, 316:332], sel[:, 332:336]
    moved_back = moved[:, :, :, :].rearrange("p a b n -> p (a b) n")
    ps_s, ps_t, ps_o, ps_x = buf.ps_s, buf.ps_t, buf.ps_o, buf.ps_s[:, 3, :, :].rearrange("p a n -> p (a n)")
    sink_ready = sem("sink_ready") if kind == "A" else None
    q_loaded = [sem(f"q_loaded{s}") for s in range(2)]
    k_loaded = [sem(f"k_loaded{s}") for s in range(2)]
    early_heads = 0 if prev else 1
    v_loaded = [sem(f"v_loaded{s}") for s in range(2)]
    gate_loaded = [sem(f"gate_loaded{b}") for b in range(GB)]
    y_stored = [sem(f"y_stored{b}") for b in range(2)]
    scores_ready, max_ready, sums_ready = sem("scores_ready"), sem("max_ready"), sem("sums_ready")
    weighted, turned, turned_copied = sem("weighted"), sem("turned"), sem("turned_copied")
    values_done = sem("values_done")
    kept = sem("kept")
    bank_read, y_ready = sem("bank_read"), sem("y_ready")
    coef_ready = sem("coef_ready")
    spread, gathered, shifted, exps_ready = sem("spread"), sem("gathered"), sem("shifted"), sem("exps_ready")
    step, spread_back, gathered_back = sem("step"), sem("spread_back"), sem("gathered_back")
    done_sem = y_ready if kind == "B" else bank_read
    DVE_STEPS = 5 if kind == "B" else 1

    def nothing(phase, slot):
        pass

    def number(phase):
        return phase[0] * 2 + phase[1]

    TOTAL = 2 * heads * NP

    def loads(sp, load_last_gate):
        def first_head(h):
            return isinstance(h, int) and h == 0

        def load_q(h, s):
            rows = bass.ds(q_row + h * HD, HD)
            cols = slice(s * HALF, (s + 1) * HALF)
            if prev or not first_head(h):
                sp.dma_start(q[0:HD, s, :].bitcast(F32), sc["qk_hi"][rows, cols]).then_inc(q_loaded[s], 16)
                sp.dma_start(q[HD:P, s, :].bitcast(F32), sc["qk_lo"][rows, cols]).then_inc(q_loaded[s], 16)

        def load_k(h, s):
            if not prev and first_head(h):
                return
            n = NKEY // 2
            to = slice(s * n, (s + 1) * n)
            cols = slice(0, n) if kind == "C" else to
            hi, lo, row = {"A": (sc["qk_hi"], sc["qk_lo"], KA + (h // 3) * HD),
                           "B": (sc["qk_hi"], sc["qk_lo"], KB + h * HD),
                           "C": (sc["mk_hi"], sc["mk_lo"], h * HD)}[kind]
            for part, place in ((hi, k_hi), (lo, k_lo)):
                for half in range(2):
                    sp.dma_start(place[half * HD:(half + 1) * HD, to].bitcast(F32),
                                 part[bass.ds(row, HD), cols]).then_inc(k_loaded[s], 16)

        def load_v(h, s):
            sp.nop(nofuse=True)
            if kind == "C":
                sp.dma_start(v["v1"][:, s, 0:2, :], sc["mv"][:, bass.ts(h, HD)].rearrange(
                    "(t p) n -> p t n", p=P)).then_inc(v_loaded[s], 16)
                return
            col = (h // 3) * HD if kind == "A" else P + h * HD
            rows = sc["v"][s * HALF:(s + 1) * HALF, bass.ds(col, HD)]
            views = {"v16": ("(p r) n -> p r n", dict(r=16)), "v1": ("(b p) n -> p b n", dict(p=P))}
            for n in kinds_v:
                if n == "v4":
                    for c in range(NCH):
                        sp.dma_start(v[n][:, s, 4 * c:4 * c + 4, :], rows[c * CHUNK:(c + 1) * CHUNK, :].rearrange(
                            "(p r) n -> p r n", r=4)).then_inc(v_loaded[s], 16)
                else:
                    sp.dma_start(v[n][:, s, :, :], rows.rearrange(views[n][0], **views[n][1])).then_inc(
                        v_loaded[s], 16)

        def load_gate(h, s):
            p = h * 2 + s
            if prev and isinstance(p, int) and p < GB:
                sp.wait_ge(prev.done_sem, prev.phases * NCH)
            else:
                ge(sp, done_sem, (p - GB + 1) * NCH)
            sp.dma_start(gate[s % GB], sc["gate"][bass.ds(y_row + h * HD, HD),
                                                       s * HALF:(s + 1) * HALF]).then_inc(gate_loaded[s % GB], 16)

        def head(h, first, new_keys=True):
            p0, p1 = (h - 1) * 2, (h - 1) * 2 + 1

            def scored(phase, n_pairs, n_before):
                if not first:
                    sp.wait_ge(scores_ready, phase * NP + n_pairs)
                elif prev:
                    sp.wait_ge(prev.scores_ready, n_before)

            def valued(phase, n_pairs, n_before):
                if not first:
                    sp.wait_ge(values_done, phase * NP + n_pairs)
                elif prev:
                    sp.wait_ge(prev.values_done, n_before)
            total = prev.TOTAL if prev else 0
            before_last = total - prev.NP if prev else 0
            early = before_last + prev.EARLY if prev else 0
            early_of = (p0, NP) if kind == "C" else (p1, EARLY)
            scored(p0, NP, before_last)
            load_q(h, 0)
            if new_keys:
                scored(*early_of, early)
                load_k(h, 0)
            scored(p1, NP, total)
            load_q(h, 1)
            if new_keys:
                load_k(h, 1)
            if not first:
                load_gate(h - 1, 1)
            elif prev:
                load_last_gate()
            if new_keys:
                valued(*early_of, early)
                load_v(h, 0)
                valued(p1, NP, total)
                load_v(h, 1)
            load_gate(h, 0)
        head(0, True)
        if kind == "A":
            for h in range(1, heads, 3):
                with sp.Fori(h, h + 2) as i:
                    head(i, False, new_keys=False)
                if h + 2 < heads:
                    head(h + 2, False)
        else:
            with sp.Fori(1, heads) as h:
                head(h, False)
        return lambda: load_gate(heads - 1, 1)

    def tensor_parts(pe):

        between = {}

        def scores(phase, slot):
            h, s = phase
            n = number(phase) * NP + slot
            if slot >= NP:
                if kind == "B" and isinstance(h, int) and h + s == 0:
                    exchange(phase, slot - NP)
                elif kind == "B":
                    between[slot - NP] = phase
                return
            if slot == 0:
                if early_heads and isinstance(h, int) and h == 0:
                    pe.wait_ge(buf.early.q_loaded[s], 32)
                    pe.wait_ge(buf.early.k_loaded[s], 64)
                else:
                    pe.wait_ge(q_loaded[s], 32 * (h - early_heads) + 32)
                    pe.wait_ge(k_loaded[s], 64 * (h // 3 if kind == "A" else h - early_heads) + 64)
            if prev and isinstance(h, int) and h + s == 0 and slot < NS:
                if slot == 0:
                    pe.wait_ge(prev.max_ready, prev.TOTAL)
                if slot == 3 and prev.kind == "B":
                    pe.wait_ge(prev.coef_ready, prev.phases)
            ge(pe, max_ready, n - NS + 1)
            for j in range(2):
                u = FLAT[s][2 * slot + j]
                out = ps_s[:, slot % NS, j, 2 * P - u.keys:]
                w = q[:, s, strided(u.q[0], P, u.q[1])]
                keys = strided(u.k[0], u.keys, u.k[1])
                nc.tensor.matmul(out, w, k_hi[:, keys], start=True, stop=False)
                last = nc.tensor.matmul(out, w, k_lo[:, keys], start=False, stop=True)
            last.then_inc(scores_ready, 1)

        def exchange(phase, k):
            p, s = number(phase), phase[1]
            if k == 1:
                pe.wait_ge(spread, p + 1)
                for x in range(2):
                    nc.tensor.matmul(ps_x[:, 16 * x:16 * x + 16], moved[:, x, 0, :], col16,
                                     start=True, stop=True)
                    for c in range(NCH):
                        at = 32 + 16 * x + 4 * c
                        last = nc.tensor.matmul(ps_x[:, at:at + 4], moved[:, x, 1 + c, :], col4,
                                                start=True, stop=True)
                last.then_inc(gathered, 1)
            if k == 3:
                pe.wait_ge(spread_back, p + 1)
                nc.tensor.matmul(ps_x[:, 64:80], moved_back[:, 0, :], bcol16, start=True, stop=True)
                for c in range(NCH):
                    last = nc.tensor.matmul(ps_x[:, 80 + 4 * c:84 + 4 * c], moved_back[:, 1 + c, :], bcol4,
                                            start=True, stop=True)
                last.then_inc(gathered_back, 1)

        def times_values(phase, e):
            h, s = phase
            p = number(phase)
            pe.wait_ge(turned_copied, p * NP + e + 1)
            for j in range(2):
                n = 2 * e + j
                u = FLAT[s][n]
                bank = bank_of[n]
                if n in first_of:
                    if 2 <= bank < MERGED + 2 and MERGED:
                        pe.wait_ge(kept, p * MERGED + bank - 1)
                    else:
                        before = p * NCH + (bank - MERGED - 2 if bank >= 2 else bank - 2)
                        if prev and isinstance(before, int) and before < 0:
                            pe.wait_ge(prev.bank_read, prev.phases * NCH + before + 1)
                        ge(pe, bank_read, before + 1)
                for i, (name, half, tile) in enumerate(u.tiles):
                    at = 2 - len(u.tiles) + i
                    last = nc.tensor.matmul(ps_o[0:HD, bank % 2, strided(u.out[0], P, u.out[1])],
                                            v[name][:, half, tile, :], pT[:, e % 2, j, at * P:(at + 1) * P],
                                            start=n in first_of and i == 0,
                                            stop=e in last_of and j == 1 and i == len(u.tiles) - 1,
                                            skip_group_check=True)
            last.then_inc(values_done, 1)

        def second(phase, slot):
            h, s = phase
            e = slot
            p = number(phase)
            if e == 0:
                pe.wait_ge(v_loaded[s], 16 * (6 if kind == "B" else 1) * ((h // 3 if kind == "A" else h) + 1))
            pe.wait_ge(weighted, p * NP + e + 1)
            if prev and isinstance(p, int) and p == 0 and e < 2:
                pe.wait_ge(prev.turned_copied, prev.TOTAL + e - 1)
            ge(pe, turned_copied, p * NP + e - 1)
            for j in range(2):
                u = FLAT[s][2 * e + j]
                for at in range(2 - len(u.tiles), 2):
                    last = nc.tensor.transpose(ps_t[:, e % 2, j, at * P:(at + 1) * P],
                                               probs[:, s, 2 * e + j, at * P:(at + 1) * P], ident[:])
            last.then_inc(turned, 1)
            for k in list(between):
                exchange(between.pop(k), k)
            if e > 0:
                times_values(phase, e - 1)
            if e == NP - 1:
                times_values(phase, e)
        return scores, second, nothing

    def vector_parts(dve):
        if kind == "A":
            nc.vector.tensor_scalar(sink[:, 1, :], sink[:, 0, :], -1.0, None, ALU.mult).then_inc(coef_ready, 1)
            dve.wait_ge(coef_ready, 1)
        C1 = 1 if kind == "A" else 0

        def scores(phase, slot):
            h, s = phase
            p = number(phase)
            if slot >= NP:
                (exchange if kind == "B" else inverse)(phase, slot - NP)
                return
            n = p * NP + slot
            dve.wait_ge(scores_ready, n + 1)
            if prev and isinstance(h, int) and h == 0 and slot == 0:
                dve.wait_ge(prev.turned, prev.TOTAL - (1 - s) * prev.NP)
            ge(dve, turned, n + 1 - 2 * NP)
            if kind == "A" and slot == 0:
                dve.nop(nofuse=True)
                nc.vector.tensor_copy(sink_now[:, s, :], sink[:, :, bass.ds(h, 1)].rearrange(
                    "p a o -> p (a o)")).then_inc(sink_ready, 1)
                dve.wait_ge(sink_ready, p + 1)
            dve.nop(nofuse=True)
            for j in range(2):
                u = FLAT[s][2 * slot + j]
                a = 2 * P - u.keys
                start = sink_now[:, s, 1:2] if kind == "A" else 3e38
                last = nc.vector.tensor_tensor_reduce(
                    out=probs[:, s, 2 * slot + j, a:], in0=ps_s[:, slot % NS, j, a:], in1=mask[:, a:],
                    scale=-SCALE, scalar=start, op0=ALU.add, op1=ALU.min,
                    accum_out=stat[:, s, 0, u.column:u.column + 1])
            last.then_inc(max_ready, 1)

        def inverse(phase, k):
            p, s = number(phase), phase[1]
            if k == 1:
                dve.wait_ge(sums_ready, p * NP + NP)
                if kind == "A":
                    dve.wait_ge(exps_ready, p + 1)
                    nc.vector.tensor_tensor(work[:, 1, :], work[:, 0, :], stat[:, s, 1, :],
                                            ALU.add).then_inc(step, 1)
                    dve.wait_ge(step, p + 1)
                    nc.vector.reciprocal(coef[:, s, :], work[:, 1, :]).then_inc(coef_ready, 1)
                else:
                    nc.vector.reciprocal(coef[:, s, :], stat[:, s, 1, :]).then_inc(coef_ready, 1)

        def exchange(phase, k):
            p, s = number(phase), phase[1]
            n = [p * DVE_STEPS + (2 if k == 2 else 0)]

            def own(ins):
                n[0] = n[0] + 1
                ins.then_inc(step, 1)
                dve.wait_ge(step, n[0])
            m1 = stat[:, s, 0, 32:48]
            x = ps_x[:, 0:64].rearrange("p (a x n) -> p a x n", a=2, x=2)
            if k == 0:
                dve.wait_ge(sums_ready, p * NP + NP)
                for a in range(2):
                    nc.vector.tensor_tensor(moved[:, a, 0, :].rearrange("p (a r) -> p a r", r=16),
                                            stat[:, s, a, 0:16].unsqueeze(1).broadcast_to([P, 8, 16]),
                                            sel16.rearrange("p (a r) -> p a r", r=16), ALU.mult)
                    last = nc.vector.tensor_tensor(
                        moved[:, a, 1:5, :].rearrange("p c (a r) -> p c a r", r=4),
                        stat[:, s, a, 16:32].rearrange("p (c r) -> p c r", r=4).unsqueeze(2).broadcast_to([P, 4, 32, 4]),
                        sel4.rearrange("p (a r) -> p a r", r=4).unsqueeze(1).broadcast_to([P, 4, 32, 4]), ALU.mult)
                last.then_inc(spread, 1)
            if k == 1:
                dve.wait_ge(gathered, p + 1)
                own(nc.vector.tensor_tensor(work[:, 0, 0:16], x[:, 0, 0, :], m1, ALU.min))
                own(nc.vector.tensor_tensor(work[:, 1, 0:16], x[:, 1, 0, :], work[:, 0, 0:16], ALU.min))
                low = work[:, 1, 0:16]
                nc.vector.tensor_tensor(work[:, 2, 0:32].rearrange("p (a n) -> p a n", a=2),
                                        low.unsqueeze(1).broadcast_to([P, 2, 16]), x[:, :, 0, :], ALU.subtract)
                nc.vector.tensor_tensor(work[:, 2, 32:48], low, m1, ALU.subtract).then_inc(shifted, 1)
            if k == 2:
                dve.wait_ge(exps_ready, p + 1)
                ex = work[:, 3, :]
                nc.vector.tensor_tensor(work[:, 4, 0:32].rearrange("p (a n) -> p a n", a=2),
                                        ex[:, 0:32].rearrange("p (a n) -> p a n", a=2), x[:, :, 1, :], ALU.mult)
                own(nc.vector.tensor_tensor(work[:, 4, 32:48], ex[:, 32:48], stat[:, s, 1, 32:48], ALU.mult))
                own(nc.vector.reduce_sum(work[:, 5, 0:16], work[:, 4, :].rearrange("p (a n) -> p n a", a=3),
                                         mybir.AxisListType.X))
                own(nc.vector.reciprocal(work[:, 6, 0:16], work[:, 5, 0:16]))
                inv = work[:, 6, 0:16]
                nc.vector.tensor_tensor(coef[:, s, 32:48], ex[:, 32:48], inv, ALU.mult)
                nc.vector.tensor_tensor(work[:, 7, 0:32].rearrange("p (a n) -> p a n", a=2),
                                        ex[:, 0:32].rearrange("p (a n) -> p a n", a=2),
                                        inv.unsqueeze(1).broadcast_to([P, 2, 16]), ALU.mult).then_inc(shifted, 1)
                dve.wait_ge(shifted, 2 * p + 2)
                nc.vector.tensor_tensor(moved_back[:, 0, :].rearrange("p (n a) -> p n a", a=8),
                                        work[:, 7, 0:16].unsqueeze(2).broadcast_to([P, 16, 8]),
                                        back16.unsqueeze(1).broadcast_to([P, 16, 8]), ALU.mult)
                nc.vector.tensor_tensor(moved_back[:, 1:5, :].rearrange("p c (b a) -> p (c b) a", a=32),
                                        work[:, 7, 16:32].unsqueeze(2).broadcast_to([P, 16, 32]),
                                        back4.unsqueeze(1).broadcast_to([P, 16, 32]), ALU.mult).then_inc(spread_back, 1)
            if k == 3:
                dve.wait_ge(gathered_back, p + 1)
                nc.vector.tensor_copy(coef[:, s, 0:32], ps_x[:, 64:96]).then_inc(coef_ready, 1)

        def second(phase, slot):
            h, s = phase
            p = number(phase)
            for e in ([0, 1] if slot == 0 else [slot + 1]):
                if e == NP:
                    continue
                if e == 0:
                    dve.wait_ge(coef_ready, p + 1 + C1)
                for j in range(2):
                    u = FLAT[s][2 * e + j]
                    place = probs[:, s, 2 * e + j, 2 * P - u.keys:]
                    last = nc.vector.tensor_scalar(place, place, coef[:, s, u.column:u.column + 1], None, ALU.mult)
                last.then_inc(weighted, 1)
            d = slot - 2
            if last_of.get(d, -1) >= MERGED:
                finish_bank(phase, d, last_of[d] - MERGED)

        def rest(phase, slot):
            if slot == 1:
                finish_bank(phase, NP - 1, NCH - 1)

        def finish_bank(phase, d, c):
            h, s = phase
            p = number(phase)
            n = p * NCH + c
            dve.wait_ge(values_done, p * NP + d + 1)
            if not isinstance(n, int) or n >= 2:
                dve.wait_ge(y_stored[c % 2], 16 * (p * 2 + c // 2))
            elif prev:
                dve.wait_ge(prev.y_stored[c % 2], 16 * 2 * prev.phases)
            dve.wait_ge(gate_loaded[s % GB], 16 * p + 16 if GB == 1 else 16 * h + 16)
            out = ps_o[0:HD, (MERGED + c) % 2, :]
            if kind == "B":
                dve.wait_ge(kept, p * MERGED + MERGED)
                nc.vector.tensor_tensor(y[:, c % 2, :].rearrange("p (j r) -> p j r", r=16),
                                        out.rearrange("p (j r) -> p j r", r=16),
                                        o16[:, :, 32 * c:32 * c + 32].rearrange("p r j -> p j r"),
                                        ALU.add).then_inc(bank_read, 1)
                dve.wait_ge(bank_read, n + 1)
                nc.vector.tensor_tensor(y[:, c % 2, :], y[:, c % 2, :], gate[s % GB][:, c * CHUNK:(c + 1) * CHUNK],
                                        ALU.mult).then_inc(y_ready, 1)
            else:
                nc.vector.tensor_tensor(y[:, c % 2, :], out, gate[s % GB][:, c * CHUNK:(c + 1) * CHUNK], ALU.mult).then_inc(bank_read, 1)
        return scores, second, rest

    def scalar_parts(act):

        def scores(phase, slot):
            h, s = phase
            p = number(phase)
            if slot >= NP:
                if kind == "A" and slot == NP:
                    act.wait_ge(max_ready, p * NP + NP)
                    nc.scalar.activation(work[:, 0, :], stat[:, s, 0, :], ACT.Exp,
                                         bias=sink_now[:, s, 0:1]).then_inc(exps_ready, 1)
                if kind == "B" and slot == NP + 1:
                    act.wait_ge(shifted, 2 * p + 1)
                    nc.scalar.activation(work[:, 3, :], work[:, 2, :], ACT.Exp).then_inc(exps_ready, 1)
                return
            act.wait_ge(max_ready, p * NP + slot + 1)
            for j in range(2):
                u = FLAT[s][2 * slot + j]
                place = probs[:, s, 2 * slot + j, 2 * P - u.keys:]
                last = nc.scalar.activation(place, place, ACT.Exp, scale=-1.0,
                                            bias=stat[:, s, 0, u.column:u.column + 1],
                                            accum_out=stat[:, s, 1, u.column:u.column + 1])
            last.then_inc(sums_ready, 1)

        def second(phase, slot):
            h, s = phase
            p = number(phase)
            e = slot
            act.wait_ge(turned, p * NP + e + 1)
            if prev and isinstance(p, int) and p == 0 and e < 2:
                act.wait_ge(prev.values_done, prev.TOTAL + e - 1)
            ge(act, values_done, p * NP + e - 1)
            a = [2 * P - FLAT[s][2 * e + j].keys for j in range(2)]
            if a[0] == a[1]:
                nc.scalar.activation(pT[:, e % 2, :, a[0]:], ps_t[:, e % 2, :, a[0]:],
                                     ACT.Copy).then_inc(turned_copied, 1)
            else:
                nc.scalar.activation(pT[:, e % 2, 0, a[0]:], ps_t[:, e % 2, 0, a[0]:], ACT.Copy)
                nc.scalar.activation(pT[:, e % 2, 1, a[1]:], ps_t[:, e % 2, 1, a[1]:],
                                     ACT.Copy).then_inc(turned_copied, 1)
            if 0 <= last_of.get(e - 2, -1) < MERGED:
                keep(phase, e - 2, last_of[e - 2])

        def keep(phase, d, g):
            p = number(phase)
            act.wait_ge(values_done, p * NP + d + 1)
            ge(act, y_ready, p * NCH)
            nc.scalar.activation(o16[:, 4 * g:4 * g + 4, :].rearrange("p r j -> p (r j)"),
                                 ps_o[0:HD, g % 2, :], ACT.Copy).then_inc(kept, 1)
        return scores, second, nothing

    def stores(pool):
        def store(h, s):
            for c in range(NCH):
                pool.wait_ge(done_sem, (h * 2 + s) * NCH + c + 1)
                pool.nop(nofuse=True)
                pool.dma_start(sc["y"][bass.ds(y_row + h * HD, HD),
                                       s * HALF + c * CHUNK:s * HALF + (c + 1) * CHUNK],
                               y[:, c % 2, :]).then_inc(y_stored[c % 2], 16)
        with pool.Fori(0, heads) as h:
            for s in range(2):
                store(h, s)

    return named(
        kind=kind, heads=heads, phases=2 * heads, NP=NP, SLOTS=SLOTS, STEPS=STEPS, EARLY=EARLY, TOTAL=TOTAL,
        scores_ready=scores_ready, values_done=values_done, max_ready=max_ready, turned=turned,
        turned_copied=turned_copied, bank_read=bank_read, coef_ready=coef_ready, done_sem=done_sem, y_stored=y_stored,
        loads=loads, tensor_parts=tensor_parts, vector_parts=vector_parts, scalar_parts=scalar_parts, stores=stores)


def load_y(sp, sc, ahead, i, b):
    n = ahead.yT.shape[3]
    for k in range(0, KD, 4):
        sp.dma_start(ahead.yT[:, b, k:k + 4, :], sc["y"][k * P:(k + 4) * P, bass.ts(i, n)].rearrange(
            "(k p) n -> p k n", p=P)).then_inc(ahead.y_loaded[b], 16)


def attend_stage(nc, io, sc, early, probs, ahead):
    with ExitStack() as ctx:
        sb = lambda n, shape, d=F32: ctx.enter_context(nc.sbuf_tensor("a_" + n, shape, d))
        NU = B_UNITS
        for n in ("q_place", "k_hi_place", "k_lo_place"):
            sb(n, [P, SEQ], F32R)
        buf = named(
            early=early,
            q=early.q,
            k_hi=early.k_hi, k_lo=early.k_lo,
            v={n: sb(n, [P, 2, 16, HD]) for n in ("v16", "v4", "v1")},
            gate=sb("gate", [HD, HALF]),
            probs=probs,
            pT=sb("pT", [P, 2, 2, 2 * P]),
            stat=sb("stat", [P, 2, 2, NU]),
            coef=sb("coef", [P, 2, NU]),
            masks={kind: sb("mask" + kind, [P, 2 * P]) for kind in "BAC"},
            ident=sb("ident", [P, P]),
            y=sb("y", [HD, 2, CHUNK]),
            work=sb("work", [P, 8, NU]),
            sink=sb("sink", [P, 2, 6]),
            sink_now=sb("sink_now", [P, 2, 2]),
            o16=sb("o16", [HD, 16, P]),
            sel=sb("sel", [P, 2 * P + 8 + 32 + 40]),
            moved=sb("moved", [P, 2, 5, P]),
            ps_s=ctx.enter_context(nc.psum_tensor("a_ps_s", [P, 4, 2, 2 * P], F32)),
            ps_t=ctx.enter_context(nc.psum_tensor("a_ps_t", [P, 2, 2, 2 * P], F32)),
            ps_o=ctx.enter_context(nc.psum_tensor("a_ps_o", [P, 2, CHUNK], F32)))
        consts = ctx.enter_context(nc.semaphore("a_consts"))
        CONSTS = 16 * 6
        groups = []
        for kind in "BAC":
            groups.append(head_group(nc, io, sc, kind, buf, ctx, groups[-1] if groups else None))

        def rounds(eng, parts_of, late=False):
            def round_(a, c, before):
                slots = max(x[0].NP for x in (a, c) if x)
                every = slots // a[0].NP if a else 1

                def scores_in(slot):
                    g, (scores, _, _), phase = a
                    if slot % every == 0:
                        slot = slot // every
                        for v in range(g.NP):
                            if g.SLOTS[v] == slot:
                                scores(phase, v)
                        if g.NP - g.STEPS <= slot < g.NP:
                            scores(phase, slot + g.STEPS)
                for slot in range(slots):
                    if a and not late:
                        scores_in(slot)
                    if before:
                        before[1][2](before[2], slot)
                    if c and slot < c[0].NP:
                        c[1][1](c[2], slot)
                    if a and late:
                        scores_in(slot)

            c = before = None
            for g in groups:
                parts = parts_of(g)
                for s in range(2):
                    a = (g, parts, (0, s))
                    round_(a, c, before)
                    c, before = a, c
                with eng.Fori(1, g.heads) as h:
                    round_((g, parts, (h, 0)), (g, parts, (h - 1, 1)), (g, parts, (h - 1, 0)))
                    round_((g, parts, (h, 1)), (g, parts, (h, 0)), (g, parts, (h - 1, 1)))
                c, before = (g, parts, (g.heads - 1, 1)), (g, parts, (g.heads - 1, 0))
            round_(None, c, before)
            for slot in range(4):
                c[1][2](c[2], slot)

        with nc.Block() as block:
            @block.sync
            def _(sp):
                sp.dma_start(buf.ident[:], io["ident"]).then_inc(consts, 16)
                sp.dma_start(buf.sel[:], io["sel"]).then_inc(consts, 16)
                sp.dma_start(buf.sink[:, 0, :], io["sink"].broadcast_to([P, 6])).then_inc(consts, 16)
                for kind in "BAC":
                    sp.dma_start(buf.masks[kind][:], io["mask" + kind]).then_inc(consts, 16)
                load_last_gate = None
                for g in groups:
                    load_last_gate = g.loads(sp, load_last_gate)
                load_last_gate()
                sp.dma_start(ahead.gain, io["post_gain"].broadcast_to([P, D])).then_inc(ahead.gain_loaded, 16)
                for b in range(2):
                    sp.dma_start(ahead.xb[:, b, :], io["x"][b * P:(b + 1) * P, :]).then_inc(ahead.x_loaded[b], 16)
                for g in groups[:-1]:
                    for b in range(2):
                        sp.wait_ge(g.y_stored[b], 16 * 2 * g.phases)
                sp.wait_ge(groups[-1].y_stored[0], 16 * (2 * (groups[-1].phases - 2) + 1))
                for b in range(2):
                    load_y(sp, sc, ahead, b, b)

            @block.tensor
            def _(pe):
                pe.wait_ge(consts, CONSTS)
                rounds(pe, lambda g: g.tensor_parts(pe))

            @block.vector
            def _(dve):
                dve.wait_ge(consts, CONSTS)
                rounds(dve, lambda g: g.vector_parts(dve), late=True)

            @block.scalar
            def _(act):
                act.wait_ge(consts, CONSTS)
                rounds(act, lambda g: g.scalar_parts(act), late=True)

            @block.gpsimd
            def _(pool):
                for n, g in enumerate(groups):
                    g.stores(pool)
                    if n < 2:
                        pool.wait_ge(groups[0].turned, groups[0].TOTAL)
                        for k in range(4 * n, 4 * n + 4):
                            pool.dma_start(ahead.w_raw[:, k, :], io["w_out"][k * P:(k + 1) * P, :]).then_inc(ahead.w_loaded, 16)
                for g in groups:
                    for b in range(2):
                        pool.wait_ge(g.y_stored[b], 16 * 2 * g.phases)


def finish_stage(nc, io, sc, out, ahead):
    with ExitStack() as ctx:
        sb = lambda n, s, d=F32: ctx.enter_context(nc.sbuf_tensor("f_" + n, s, d))
        sem = lambda n: ctx.enter_context(nc.semaphore("f_" + n))
        TW = 256
        NB = SEQ // TW
        w_raw, gain, yT, xb = ahead.w_raw, ahead.gain, ahead.yT, ahead.xb
        w_hi = sb("w_hi", [P, KD, D], F32R)
        w_lo = sb("w_lo", [P, KD, D], F32R)
        y_hi = sb("y_hi", [P, 2, KD, TW], F32R)
        y_lo = sb("y_lo", [P, 2, KD, TW], F32R)
        o = sb("o", [P, 2, D])
        junk = sb("junk", [P, D])
        ss = sb("ss", [P, 2, 4])
        ps = ctx.enter_context(nc.psum_tensor("f_ps", [P, 4, 2, CHUNK], F32))
        gain_loaded, w_loaded, y_loaded, x_loaded = ahead.gain_loaded, ahead.w_loaded, ahead.y_loaded, ahead.x_loaded
        stored = [sem(f"stored{b}") for b in range(2)]
        w_hi_ready, w_lo_ready, y_hi_ready, y_lo_ready = sem("w_hi_ready"), sem("w_lo_ready"), sem("y_hi_ready"), sem("y_lo_ready")
        multiplied, squared, meaned, rooted = sem("multiplied"), sem("squared"), sem("meaned"), sem("rooted")
        inverted, normed, added = sem("inverted"), sem("normed"), sem("added")
        with nc.Block() as block:
            @block.sync
            def _(sp):
                def load_x(i, b):
                    sp.dma_start(xb[:, b, :], io["x"][bass.ts(i, P), :]).then_inc(x_loaded[b], 16)

                def store(i, b):
                    sp.wait_ge(added, i + 1)
                    sp.dma_start(out[bass.ts(i, P), :], o[:, b, :]).then_inc(stored[b], 16)
                with sp.Fori(0, NB // 2 - 1) as two:
                    i = 2 * two
                    for b in range(2):
                        for t in range(2):
                            store(2 * (i + b) + t, t)
                            load_x(2 * (i + b) + t + 2, t)
                        sp.wait_ge(y_lo_ready, i + b + 1)
                        load_y(sp, sc, ahead, i + b + 2, b)
                for t in range(4):
                    store(2 * NB - 4 + t, t % 2)
                    if t < 2:
                        load_x(2 * NB - 2 + t, t)
                for b in range(2):
                    sp.wait_ge(stored[b], 16 * NB)

            @block.scalar
            def _(act):
                def part(i, b):
                    act.wait_ge(y_loaded[b], 32 * ((i - b) // 2) + 32 if isinstance(i, int) else 16 * (i - b) + 32)
                    if not isinstance(i, int) or i >= 2:
                        act.wait_ge(multiplied, 2 * i - 2)
                    nc.scalar.activation(y_hi[:, b, :, :], yT[:, b, :, :], ACT.Copy).then_inc(y_hi_ready, 1)

                def square(i, b):
                    act.wait_ge(multiplied, i + 1)
                    nc.scalar.activation(junk[:], ps[:, b, :, :].rearrange("p a n -> p (a n)"), ACT.Square,
                                         accum_out=ss[:, b % 2, 0:1]).then_inc(squared, 1)
                    act.wait_ge(meaned, i + 1)
                    nc.scalar.activation(ss[:, b % 2, 2:3], ss[:, b % 2, 1:2], ACT.Sqrt).then_inc(rooted, 1)
                part(0, 0)
                act.wait_ge(w_loaded, 16 * KD)
                for k in range(KD):
                    nc.scalar.activation(w_hi[:, k, :], w_raw[:, k, :], ACT.Copy).then_inc(w_hi_ready, 1)
                part(1, 1)
                with act.Fori(0, NB // 2 - 1) as two:
                    i = 2 * two
                    for b in range(2):
                        for t in range(2):
                            square(2 * (i + b) + t, 2 * b + t)
                        part(i + b + 2, b)
                for t in range(4):
                    square(2 * NB - 4 + t, t)

            @block.vector
            def _(dve):
                dve.wait_ge(gain_loaded, 16)

                def part(i, b):
                    dve.wait_ge(y_hi_ready, i + 1)
                    nc.vector.tensor_tensor(y_lo[:, b, :, :], yT[:, b, :, :], y_hi[:, b, :, :].bitcast(F32),
                                            ALU.subtract).then_inc(y_lo_ready, 1)

                def norm(i, b):
                    dve.wait_ge(squared, i + 1)
                    nc.vector.tensor_scalar(ss[:, b % 2, 1:2], ss[:, b % 2, 0:1], 1.0 / D, EPS,
                                            ALU.mult, ALU.add).then_inc(meaned, 1)
                    dve.wait_ge(rooted, i + 1)
                    nc.vector.reciprocal(ss[:, b % 2, 3:4], ss[:, b % 2, 2:3]).then_inc(inverted, 1)
                    dve.wait_ge(inverted, i + 1)
                    if not isinstance(i, int) or i >= 2:
                        dve.wait_ge(stored[b % 2], 16 * ((i - b % 2) // 2) if isinstance(i, int) else 8 * (i - b % 2))
                    nc.vector.scalar_tensor_tensor(out=o[:, b % 2, :], in0=ps[:, b, :, :].rearrange("p a n -> p (a n)"),
                                                   scalar=ss[:, b % 2, 3:4], in1=gain,
                                                   op0=ALU.mult, op1=ALU.mult).then_inc(normed, 1)
                    dve.wait_ge(normed, i + 1)
                    dve.wait_ge(x_loaded[b % 2], 16 * ((i - b % 2) // 2) + 16 if isinstance(i, int)
                                else 8 * (i - b % 2) + 16)
                    nc.vector.tensor_tensor(o[:, b % 2, :], o[:, b % 2, :], xb[:, b % 2, :], ALU.add).then_inc(added, 1)
                part(0, 0)
                for k in range(KD):
                    dve.wait_ge(w_hi_ready, k + 1)
                    nc.vector.tensor_tensor(w_lo[:, k, :], w_raw[:, k, :], w_hi[:, k, :].bitcast(F32),
                                            ALU.subtract).then_inc(w_lo_ready, 1)
                part(1, 1)
                for t in range(2):
                    norm(t, t)
                part(2, 0)
                for t in range(2):
                    norm(2 + t, 2 + t)
                part(3, 1)
                with dve.Fori(1, NB // 2 - 1) as two:
                    i = 2 * two
                    for b in range(2):
                        for t in range(2):
                            norm(2 * (i + b) + t, 2 * b + t)
                        part(i + b + 2, b)
                for t in range(4):
                    norm(2 * NB - 4 + t, t)

            @block.tensor
            def _(pe):
                def product(i, b):
                    pe.wait_ge(y_lo_ready, i + 1)
                    for t in range(2):
                        if not isinstance(i, int) or i >= 2:
                            pe.wait_ge(normed, 2 * i + t - 3)
                        first = isinstance(i, int) and i == 0 and t == 0
                        for c, k in ([(c, k) for k in range(KD) for c in range(2)] if first else
                                     [(c, k) for c in range(2) for k in range(KD)]):
                            if first and c == 0:
                                pe.wait_ge(w_lo_ready, k + 1)
                            y, cols = slice(t * P, (t + 1) * P), slice(c * CHUNK, (c + 1) * CHUNK)
                            last = split_product(nc, ps[:, 2 * b + t, c, :], y_hi[:, b, k, y], y_lo[:, b, k, y],
                                                 w_hi[:, k, cols], w_lo[:, k, cols], k == 0, k == KD - 1)
                        last.then_inc(multiplied, 1)
                product(0, 0)
                product(1, 1)
                with pe.Fori(1, NB // 2) as two:
                    i = 2 * two
                    for b in range(2):
                        product(i + b, b)


def build(nc, io, out):
    scratch = lambda n, s, d=F32: nc.dram_tensor("scratch_" + n, s, d, kind="Internal").ap()
    sc = {
        "qk_hi": scratch("qk_hi", [NQK * P, SEQ]), "qk_lo": scratch("qk_lo", [NQK * P, SEQ]),
        "v": scratch("v", [SEQ, len(V_TILES) * P]), "gate": scratch("gate", [D, SEQ]), "y": scratch("y", [D, SEQ]),
        "mk_hi": scratch("mk_hi", [256, NMEM]), "mk_lo": scratch("mk_lo", [256, NMEM]),
        "mv": scratch("mv", [NMEM, 256]),
    }
    with ExitStack() as ctx:
        sem = lambda n: ctx.enter_context(nc.semaphore("e_" + n))
        with ExitStack() as places:
            places.enter_context(nc.sbuf_tensor("e_probs", [P, 2, B_UNITS, 2 * P], F32))
            q, k_hi, k_lo = (places.enter_context(nc.sbuf_tensor(n, [P, SEQ], F32R)) for n in ("q", "k_hi", "k_lo"))
        early = named(q=q[:].rearrange("p (s n) -> p s n", s=2), k_hi=k_hi, k_lo=k_lo,
                      q_loaded=[sem(f"q_loaded{s}") for s in range(2)], k_loaded=[sem(f"k_loaded{s}") for s in range(2)])
        project_stage(nc, io, sc, early)
        sem = lambda n: ctx.enter_context(nc.semaphore("f_" + n))
        probs = ctx.enter_context(nc.sbuf_tensor("probs", [P, 2, B_UNITS, 2 * P], F32))
        room = probs[:, :, B_UNITS // 3:, :].rearrange("p s u n -> p s (u n)")
        ahead = named(
            w_raw=room[:, 0, :].rearrange("p (k n) -> p k n", k=KD),
            yT=room[:, 1, 0:4 * D].rearrange("p (b k n) -> p b k n", b=2, k=KD),
            xb=room[:, 1, 4 * D:6 * D].rearrange("p (b n) -> p b n", b=2),
            gain=room[:, 1, 6 * D:7 * D],
            gain_loaded=sem("gain_loaded"), w_loaded=sem("w_loaded"),
            y_loaded=[sem(f"y_loaded{b}") for b in range(2)], x_loaded=[sem(f"x_loaded{b}") for b in range(2)])
        attend_stage(nc, io, sc, early, probs, ahead)
        finish_stage(nc, io, sc, out, ahead)


def constants():
    import numpy as np
    rot = HD // 4
    inv = (np.float32(500000.0) ** (-np.arange(0, rot, 2, dtype=np.float32) / np.float32(rot))).astype(np.float32)
    ang = (np.arange(SEQ, dtype=np.float32)[None, :] * inv[:, None]).astype(np.float32)
    c, s = np.cos(ang).astype(np.float32), np.sin(ang).astype(np.float32)
    cos, sin = np.ones((P, SEQ), np.float32), np.zeros((P, SEQ), np.float32)
    for h in (0, HD):
        cos[h:h + 8], cos[h + 8:h + 16] = c, c
        sin[h:h + 8], sin[h + 8:h + 16] = -s, s
    q, k = np.arange(P)[:, None], np.arange(P)[None, :]
    diag = np.where(k <= q, 0.0, NEG)
    mask_a = np.concatenate([np.where(k > q, 0.0, NEG), diag], 1).astype(np.float32)
    mask_b = np.concatenate([np.where(k >= q, 0.0, NEG), diag], 1).astype(np.float32)
    j = np.arange(P)[:, None]
    n = lambda m: np.arange(m)[None, :]
    sel = np.concatenate([
        j % 8 == n(P) // 16,
        j % 32 == n(P) // 4,
        j // 16 == n(8), j // 4 == n(32),
        j // 8 == n(16), j // 32 == n(4), j % 16 == n(16), j % 4 == n(4),
    ], 1).astype(np.float32)
    return {"cos": cos, "sin": sin, "maskA": mask_a, "maskB": mask_b, "maskC": np.zeros((P, 2 * P), np.float32),
            "sel": sel, "ident": np.eye(P, dtype=np.float32)}


def kernel(x, mem, pre_norm, w_in, sink_a, mem_norm, w_mem_kv, w_out, post_norm):
    import numpy as np
    import concourse.bacc as bacc
    from concourse.bass_utils import run_bass_kernel_spmd

    nc = bacc.Bacc("TRN2", target_bir_lowering=False, num_devices=1)
    w = np.asarray(w_in)[0].reshape(KD, P, NT, P).transpose(2, 1, 0, 3)[np.array(ORDER)]
    given = {
        "x": np.asarray(x)[0], "mem": np.asarray(mem)[0], "pre_gain": np.asarray(pre_norm), "w_in": w.reshape(NT, P, D),
        "sink": np.asarray(sink_a), "mem_gain": np.asarray(mem_norm), "w_mem": np.asarray(w_mem_kv)[0],
        "w_out": np.asarray(w_out)[0], "post_gain": np.asarray(post_norm), **constants(),
    }
    arrays = {f"in_{n}": np.ascontiguousarray(a) for n, a in given.items()}
    io = {n: nc.dram_tensor(f"in_{n}", a.shape, F32, kind="ExternalInput").ap() for n, a in given.items()}
    out = nc.dram_tensor("out_0", [SEQ, D], F32, kind="ExternalOutput").ap()
    build(nc, io, out)
    r = run_bass_kernel_spmd(nc, [arrays], core_ids=[0])
    return r.results[0]["out_0"].reshape(1, SEQ, D)
```
